# Optimizing a Trainium2 kernel written in Bass

```python
import math
import jax
import jax.numpy as jnp
from jax import lax
import numpy as np

D_MODEL = 1024
BATCH = 1
SEQ = 256
DEPTH = 1

D_MIX = D_MODEL
D_S5 = D_MIX // 2
S5_GROUP = 16
N_S5_GROUPS = D_S5 // S5_GROUP
S5_STATE = 64
D_GDN = D_MIX - D_S5
GDN_HEAD_DIM = 128
N_GDN_HEADS = D_GDN // GDN_HEAD_DIM
CONV_WIDTH = 4
CHUNK = 64
D_IN = D_S5 + 4 * D_GDN + 2 * N_GDN_HEADS
N_EXPERT_GROUPS = 4
EXPERTS_PER_GROUP = 8
N_EXPERTS = N_EXPERT_GROUPS * EXPERTS_PER_GROUP
TOP_K_IN_GROUP = 2
D_EXPERT = D_MODEL // 4
N_MOD = 6
EPS = 1e-6


def rmsnorm(x, g):
    x32 = x.astype(jnp.float32)
    y = x32 * lax.rsqrt(jnp.mean(x32 * x32, axis=-1, keepdims=True) + EPS)
    return (y * g.astype(jnp.float32)).astype(x.dtype)

def l2norm(x):
    return x * lax.rsqrt(jnp.sum(x * x, axis=-1, keepdims=True) + EPS)

def modulate(h, shift, scale):
    return h * (1.0 + scale[:, None, :]) + shift[:, None, :]

def _linear_recurrence_combine(e1, e2):
    a1, b1 = e1
    a2, b2 = e2
    return a1 * a2, a2 * b1 + b2

def s5_mixer(u, lam_re, lam_im, log_step, b_re, b_im, c_re, c_im, d_skip, w_glu, b_glu):
    f32 = jnp.float32
    bsz, seq, _ = u.shape
    u32 = u.astype(f32)
    ug = u32.reshape(bsz, seq, N_S5_GROUPS, S5_GROUP)
    lam = lax.complex(lam_re.astype(f32), lam_im.astype(f32))
    step = jnp.exp(log_step.astype(f32))[:, None]
    lam_bar = jnp.exp(lam * step)
    b_c = lax.complex(b_re.astype(f32), b_im.astype(f32))
    b_bar = ((lam_bar - 1.0) / lam)[..., None] * b_c
    bu = lax.complex(jnp.einsum('gph,blgh->blgp', b_bar.real, ug),
                     jnp.einsum('gph,blgh->blgp', b_bar.imag, ug))
    a = jnp.broadcast_to(lam_bar, bu.shape)
    _, states = lax.associative_scan(_linear_recurrence_combine, (a, bu), axis=1)
    c_c = lax.complex(c_re.astype(f32), c_im.astype(f32))
    y = jnp.einsum('ghp,blgp->blgh', c_c, states).real.reshape(bsz, seq, D_S5)
    y = y + d_skip.astype(f32) * u32
    y = jax.nn.gelu(y)
    y = y * jax.nn.sigmoid(y @ w_glu.astype(f32) + b_glu.astype(f32))
    return y.astype(u.dtype)

def causal_depthwise_conv(x, w):
    k, ch = w.shape
    return lax.conv_general_dilated(x, w[:, None, :], window_strides=(1,),
                                    padding=[(k - 1, 0)],
                                    dimension_numbers=('NWC', 'WIO', 'NWC'),
                                    feature_group_count=ch)

def gated_delta_rule(q, k, v, g, beta):
    bsz, nh, seq, dk = q.shape
    dv = v.shape[-1]
    n_chunks = seq // CHUNK
    q = q.reshape(bsz, nh, n_chunks, CHUNK, dk)
    k = k.reshape(bsz, nh, n_chunks, CHUNK, dk)
    v = v.reshape(bsz, nh, n_chunks, CHUNK, dv)
    beta = beta.reshape(bsz, nh, n_chunks, CHUNK)
    g = jnp.cumsum(g.reshape(bsz, nh, n_chunks, CHUNK), axis=-1)
    idx = jnp.arange(CHUNK)
    causal = idx[:, None] >= idx[None, :]
    strict = idx[:, None] > idx[None, :]
    decay = jnp.exp(jnp.where(causal, g[..., :, None] - g[..., None, :], -jnp.inf))
    k_beta = k * beta[..., None]
    v_beta = v * beta[..., None]
    kkt = jnp.einsum('bhncd,bhnsd->bhncs', k_beta, k) * decay
    a_mat = jnp.where(strict, kkt, 0.0) + jnp.eye(CHUNK, dtype=q.dtype)
    rhs = jnp.concatenate([v_beta, k_beta * jnp.exp(g)[..., None]], axis=-1)
    sol = lax.linalg.triangular_solve(a_mat, rhs, left_side=True, lower=True,
                                      unit_diagonal=True)
    value, k_cumdecay = sol[..., :dv], sol[..., dv:]
    qk = jnp.einsum('bhncd,bhnsd->bhncs', q, k) * decay
    q_decay = q * jnp.exp(g)[..., None]
    k_tail = k * jnp.exp(g[..., -1:] - g)[..., None]
    g_last = jnp.exp(g[..., -1])

    def chunk_step(state, inp):
        qk_i, qd_i, kc_i, val_i, kt_i, gl_i = inp
        v_new = val_i - jnp.einsum('bhcd,bhde->bhce', kc_i, state)
        o_i = (jnp.einsum('bhcd,bhde->bhce', qd_i, state)
               + jnp.einsum('bhcs,bhse->bhce', qk_i, v_new))
        state = state * gl_i[..., None, None] + jnp.einsum('bhcd,bhce->bhde', kt_i, v_new)
        return state, o_i

    xs = tuple(jnp.moveaxis(t, 2, 0) for t in (qk, q_decay, k_cumdecay, value, k_tail, g_last))
    state0 = jnp.zeros((bsz, nh, dk, dv), q.dtype)
    _, o = lax.scan(chunk_step, state0, xs)
    return jnp.moveaxis(o, 0, 2).reshape(bsz, nh, seq, dv)

def gdn_mixer(qkv, z, a_gate, b_gate, conv_w, a_log, dt_bias, gdn_norm_g):
    f32 = jnp.float32
    bsz, seq, _ = qkv.shape
    qkv = jax.nn.silu(causal_depthwise_conv(qkv, conv_w)).astype(f32)
    q, k, v = jnp.split(qkv, 3, axis=-1)

    def heads(t):
        return t.reshape(bsz, seq, N_GDN_HEADS, GDN_HEAD_DIM).transpose(0, 2, 1, 3)

    q = l2norm(heads(q)) * (GDN_HEAD_DIM ** -0.5)
    k = l2norm(heads(k))
    v = heads(v)
    beta = jax.nn.sigmoid(b_gate.astype(f32)).transpose(0, 2, 1)
    g = (-jnp.exp(a_log.astype(f32))
         * jax.nn.softplus(a_gate.astype(f32) + dt_bias.astype(f32))).transpose(0, 2, 1)
    o = gated_delta_rule(q, k, v, g, beta).transpose(0, 2, 1, 3)
    zh = z.astype(f32).reshape(bsz, seq, N_GDN_HEADS, GDN_HEAD_DIM)
    o = rmsnorm(o, gdn_norm_g) * jax.nn.silu(zh)
    return o.reshape(bsz, seq, D_GDN).astype(z.dtype)

def hybrid_mixer(h, w_in, lam_re, lam_im, log_step, s5_b_re, s5_b_im, s5_c_re, s5_c_im,
                 s5_d, w_glu, b_glu, conv_w, a_log, dt_bias, gdn_norm_g, w_out):
    proj = h @ w_in
    splits = [D_S5, D_S5 + 3 * D_GDN, D_S5 + 4 * D_GDN, D_S5 + 4 * D_GDN + N_GDN_HEADS]
    u_s5, qkv, z, a_gate, b_gate = jnp.split(proj, splits, axis=-1)
    y_s5 = s5_mixer(u_s5, lam_re, lam_im, log_step, s5_b_re, s5_b_im, s5_c_re, s5_c_im,
                    s5_d, w_glu, b_glu)
    y_gdn = gdn_mixer(qkv, z, a_gate, b_gate, conv_w, a_log, dt_bias, gdn_norm_g)
    return jnp.concatenate([y_s5, y_gdn], axis=-1) @ w_out

def hier_moe(h, w_router_grp, w_router_exp, w_gate, w_up, w_down):
    f32 = jnp.float32
    bsz, seq, d = h.shape
    hf = h.reshape(bsz * seq, d)
    grp_logits = (hf @ w_router_grp).astype(f32)
    grp_prob = jax.nn.softmax(grp_logits, axis=-1)
    grp_idx = jnp.argmax(grp_logits, axis=-1)
    grp_onehot = jax.nn.one_hot(grp_idx, N_EXPERT_GROUPS, dtype=f32)
    p_grp = jnp.sum(grp_prob * grp_onehot, axis=-1)
    exp_logits = (hf @ w_router_exp).astype(f32).reshape(-1, N_EXPERT_GROUPS, EXPERTS_PER_GROUP)
    sel_logits = jnp.einsum('tg,tge->te', grp_onehot, exp_logits)
    top_val, top_idx = lax.top_k(sel_logits, TOP_K_IN_GROUP)
    w_k = jax.nn.softmax(top_val, axis=-1) * p_grp[:, None]
    expert_id = grp_idx[:, None] * EXPERTS_PER_GROUP + top_idx
    combine = jnp.einsum('tk,tke->te', w_k,
                         jax.nn.one_hot(expert_id, N_EXPERTS, dtype=f32)).astype(h.dtype)

    def expert_step(acc, ws):
        wg, wu, wd, gate_col = ws
        y = (jax.nn.silu(hf @ wg) * (hf @ wu)) @ wd
        return acc + gate_col[:, None] * y, None

    acc0 = jnp.zeros_like(hf)
    out, _ = lax.scan(expert_step, acc0, (w_gate, w_up, w_down, combine.T))
    return out.reshape(bsz, seq, d)

def first_inputs(seed: int = 0) -> dict:
    key = jax.random.key(seed)
    ks = jax.random.split(key, 32)
    f32 = jnp.float32

    def nrm(k, shape, scale):
        return jax.random.normal(k, shape, f32) * scale

    nl = DEPTH
    gp = (nl, N_S5_GROUPS, S5_STATE)
    n_idx = jnp.arange(S5_STATE, dtype=f32)
    dt_init = jnp.exp(jax.random.uniform(ks[21], (nl, N_GDN_HEADS), f32,
                                         math.log(1e-3), math.log(1e-1)))
    return {
        'x': nrm(ks[0], (BATCH, SEQ, D_MODEL), 1.0),
        'c': nrm(ks[1], (BATCH, D_MODEL), 1.0),
        'norm1_g': 1.0 + nrm(ks[2], (nl, D_MODEL), 0.02),
        'norm2_g': 1.0 + nrm(ks[3], (nl, D_MODEL), 0.02),
        'w_ada': nrm(ks[4], (nl, D_MODEL, N_MOD * D_MODEL), 0.5 * D_MODEL ** -0.5),
        'b_ada': nrm(ks[5], (nl, N_MOD * D_MODEL), 0.02),
        'w_in': nrm(ks[6], (nl, D_MODEL, D_IN), D_MODEL ** -0.5),
        'lam_re': -0.5 + nrm(ks[7], gp, 0.01),
        'lam_im': math.pi * n_idx + nrm(ks[8], gp, 0.01),
        'log_step': jax.random.uniform(ks[9], (nl, N_S5_GROUPS), f32,
                                       math.log(1e-3), math.log(1e-1)),
        's5_b_re': nrm(ks[10], (nl, N_S5_GROUPS, S5_STATE, S5_GROUP), (2 * S5_GROUP) ** -0.5),
        's5_b_im': nrm(ks[11], (nl, N_S5_GROUPS, S5_STATE, S5_GROUP), (2 * S5_GROUP) ** -0.5),
        's5_c_re': nrm(ks[12], (nl, N_S5_GROUPS, S5_GROUP, S5_STATE), S5_STATE ** -0.5),
        's5_c_im': nrm(ks[13], (nl, N_S5_GROUPS, S5_GROUP, S5_STATE), S5_STATE ** -0.5),
        's5_d': nrm(ks[14], (nl, D_S5), 0.5),
        'w_glu': nrm(ks[15], (nl, D_S5, D_S5), D_S5 ** -0.5),
        'b_glu': nrm(ks[16], (nl, D_S5), 0.02),
        'conv_w': nrm(ks[17], (nl, CONV_WIDTH, 3 * D_GDN), CONV_WIDTH ** -0.5),
        'a_log': jnp.log(jax.random.uniform(ks[18], (nl, N_GDN_HEADS), f32, 1.0, 16.0)),
        'dt_bias': dt_init + jnp.log(-jnp.expm1(-dt_init)),
        'gdn_norm_g': 1.0 + nrm(ks[19], (nl, GDN_HEAD_DIM), 0.02),
        'w_out': nrm(ks[20], (nl, D_MIX, D_MODEL), D_MIX ** -0.5),
        'w_router_grp': nrm(ks[22], (nl, D_MODEL, N_EXPERT_GROUPS), D_MODEL ** -0.5),
        'w_router_exp': nrm(ks[23], (nl, D_MODEL, N_EXPERTS), D_MODEL ** -0.5),
        'w_gate': nrm(ks[24], (nl, N_EXPERTS, D_MODEL, D_EXPERT), D_MODEL ** -0.5),
        'w_up': nrm(ks[25], (nl, N_EXPERTS, D_MODEL, D_EXPERT), D_MODEL ** -0.5),
        'w_down': nrm(ks[26], (nl, N_EXPERTS, D_EXPERT, D_MODEL), D_EXPERT ** -0.5),
        'normf_g': 1.0 + nrm(ks[27], (D_MODEL,), 0.02),
    }

def first_block(x, c, norm1_g, norm2_g, w_ada, b_ada, w_in, lam_re, lam_im, log_step,
              s5_b_re, s5_b_im, s5_c_re, s5_c_im, s5_d, w_glu, b_glu, conv_w, a_log,
              dt_bias, gdn_norm_g, w_out, w_router_grp, w_router_exp, w_gate, w_up,
              w_down, normf_g):
    h = x
    c_act = jax.nn.silu(c)
    for l in range(DEPTH):
        mod = c_act @ w_ada[l] + b_ada[l]
        sh1, sc1, gt1, sh2, sc2, gt2 = jnp.split(mod, N_MOD, axis=-1)
        a_in = modulate(rmsnorm(h, norm1_g[l]), sh1, sc1)
        mix = hybrid_mixer(a_in, w_in[l], lam_re[l], lam_im[l], log_step[l], s5_b_re[l],
                           s5_b_im[l], s5_c_re[l], s5_c_im[l], s5_d[l], w_glu[l], b_glu[l],
                           conv_w[l], a_log[l], dt_bias[l], gdn_norm_g[l], w_out[l])
        h = h + gt1[:, None, :] * mix
        m_in = modulate(rmsnorm(h, norm2_g[l]), sh2, sc2)
        moe = hier_moe(m_in, w_router_grp[l], w_router_exp[l], w_gate[l], w_up[l], w_down[l])
        h = h + gt2[:, None, :] * moe
    return rmsnorm(h, normf_g)


DEPTH_2 = 4

N_MIXERS = 3
N_A = (DEPTH_2 + 2) // 3
N_B = (DEPTH_2 + 1) // 3
N_C = DEPTH_2 // 3
D_FF = 2816
NEG_INF = -1e30
HEADS_A = 16
HEAD_DIM_A = D_MODEL // HEADS_A
LEFT_CHUNKS = 8
BAND = (LEFT_CHUNKS + 1) * CHUNK
REL_CLIP = 128
GMLP_CHUNK = 128
D_GATE = D_MODEL
GMLP_GROUPS = 8
GMLP_GROUP_DIM = D_GATE // GMLP_GROUPS
HEADS_C = 8
HEAD_DIM_C = D_MODEL // (2 * HEADS_C)
Q_BLOCK = 128


def rms_norm(x, g):
    xf = x.astype(jnp.float32)
    y = xf * lax.rsqrt(jnp.mean(xf * xf, axis=-1, keepdims=True) + EPS)
    return (y * g.astype(jnp.float32)).astype(x.dtype)

def swiglu(h, w_in, w_out):
    gate, up = jnp.split(h @ w_in, 2, axis=-1)
    return (jax.nn.silu(gate) * up) @ w_out

def mixer_a(h, w_qkv, rel_bias, w_o):
    B, S, D = h.shape
    nc = S // CHUNK
    pad = LEFT_CHUNKS * CHUNK
    q, k, v = jnp.split(h @ w_qkv, 3, axis=-1)
    q = q.reshape(B, nc, CHUNK, HEADS_A, HEAD_DIM_A).transpose(1, 0, 2, 3, 4)
    k = jnp.pad(k.reshape(B, S, HEADS_A, HEAD_DIM_A), ((0, 0), (pad, 0), (0, 0), (0, 0)))
    v = jnp.pad(v.reshape(B, S, HEADS_A, HEAD_DIM_A), ((0, 0), (pad, 0), (0, 0), (0, 0)))
    rel = jnp.clip(pad + jnp.arange(CHUNK)[:, None] - jnp.arange(BAND)[None, :], -REL_CLIP, REL_CLIP) + REL_CLIP
    bias = rel_bias.astype(jnp.float32)[:, rel]
    scale = HEAD_DIM_A ** -0.5

    def one_chunk(args):
        c, qc = args
        start = c * CHUNK
        kb = lax.dynamic_slice_in_dim(k, start, BAND, axis=1)
        vb = lax.dynamic_slice_in_dim(v, start, BAND, axis=1)
        s = jnp.einsum('bqhd,bkhd->bhqk', qc, kb).astype(jnp.float32) * scale + bias
        valid = (start - pad + jnp.arange(BAND)) >= 0
        s = jnp.where(valid, s, NEG_INF)
        p = jax.nn.softmax(s, axis=-1).astype(vb.dtype)
        return jnp.einsum('bhqk,bkhd->bqhd', p, vb)

    o = lax.map(one_chunk, (jnp.arange(nc), q))
    o = o.transpose(1, 0, 2, 3, 4).reshape(B, S, D)
    return o @ w_o

def mixer_b(h, w_in, ln_g, ln_b, w_s, b_s, w_o):
    B, S, _ = h.shape
    n = S // GMLP_CHUNK
    u, v = jnp.split(jax.nn.gelu(h @ w_in, approximate=False), 2, axis=-1)
    vf = v.astype(jnp.float32)
    mu = jnp.mean(vf, axis=-1, keepdims=True)
    var = jnp.mean(jnp.square(vf - mu), axis=-1, keepdims=True)
    v = ((vf - mu) * lax.rsqrt(var + EPS) * ln_g.astype(jnp.float32) + ln_b.astype(jnp.float32)).astype(h.dtype)
    v = v.reshape(B, n, GMLP_CHUNK, GMLP_GROUPS, GMLP_GROUP_DIM)
    causal = jnp.tril(jnp.ones((GMLP_CHUNK, GMLP_CHUNK), dtype=bool))
    w = jnp.where(causal[None], w_s, 0.0)
    sv = jnp.einsum('gts,bnsgc->bntgc', w, v) + b_s.T[None, None, :, :, None]
    y = u * sv.reshape(B, S, D_GATE)
    return y @ w_o

def mixer_c(h, w_qkv, lam, subln_g, w_o, lambda_init):
    B, S, D = h.shape
    nb = S // Q_BLOCK
    q, k, v = jnp.split(h @ w_qkv, 3, axis=-1)
    q = q.reshape(B, nb, Q_BLOCK, HEADS_C, 2, HEAD_DIM_C).transpose(1, 0, 2, 3, 4, 5)
    k = k.reshape(B, S, HEADS_C, 2, HEAD_DIM_C)
    v = v.reshape(B, S, HEADS_C, 2 * HEAD_DIM_C)
    lamf = lam.astype(jnp.float32)
    lam_full = jnp.exp(jnp.sum(lamf[0] * lamf[1])) - jnp.exp(jnp.sum(lamf[2] * lamf[3])) + lambda_init
    slopes = 2.0 ** (-8.0 * (jnp.arange(HEADS_C, dtype=jnp.float32) + 1.0) / HEADS_C)
    kpos = jnp.arange(S)
    scale = HEAD_DIM_C ** -0.5

    def one_block(args):
        blk, qblk = args
        qpos = blk * Q_BLOCK + jnp.arange(Q_BLOCK)
        dist = jnp.abs(qpos[:, None] - kpos[None, :]).astype(jnp.float32)
        alibi = -slopes[:, None, None] * dist
        allowed = kpos[None, :] < (qpos[:, None] // CHUNK + 1) * CHUNK
        s = jnp.einsum('bqhmd,bkhmd->bmhqk', qblk, k).astype(jnp.float32) * scale + alibi
        s = jnp.where(allowed, s, NEG_INF)
        p = jax.nn.softmax(s, axis=-1)
        a = p[:, 0] - lam_full * p[:, 1]
        return jnp.einsum('bhqk,bkhe->bqhe', a.astype(v.dtype), v)

    o = lax.map(one_block, (jnp.arange(nb), q))
    o = o.transpose(1, 0, 2, 3, 4).reshape(B, S, HEADS_C, 2 * HEAD_DIM_C)
    o = rms_norm(o, subln_g) * (1.0 - lambda_init)
    return o.reshape(B, S, D) @ w_o

def second_inputs(seed: int = 0) -> dict:
    key = jax.random.key(seed)
    ks = jax.random.split(key, 20)

    def nrm(k, shape, scale):
        return jax.random.normal(k, shape, jnp.float32) * scale

    D = D_MODEL
    return {
        'x': nrm(ks[0], (BATCH, SEQ, D), 1.0),
        'norm_g': 1.0 + nrm(ks[1], (DEPTH_2, 6, D), 0.05),
        'ff1_w_in': nrm(ks[2], (DEPTH_2, D, 2 * D_FF), D ** -0.5),
        'ff1_w_out': nrm(ks[3], (DEPTH_2, D_FF, D), D_FF ** -0.5),
        'ff2_w_in': nrm(ks[4], (DEPTH_2, D, 2 * D_FF), D ** -0.5),
        'ff2_w_out': nrm(ks[5], (DEPTH_2, D_FF, D), D_FF ** -0.5),
        'a_w_qkv': nrm(ks[6], (N_A, D, 3 * D), D ** -0.5),
        'a_rel_bias': nrm(ks[7], (N_A, HEADS_A, 2 * REL_CLIP + 1), 0.5),
        'a_w_o': nrm(ks[8], (N_A, D, D), D ** -0.5),
        'b_w_in': nrm(ks[9], (N_B, D, 2 * D_GATE), D ** -0.5),
        'b_ln_g': 1.0 + nrm(ks[10], (N_B, D_GATE), 0.05),
        'b_ln_b': nrm(ks[11], (N_B, D_GATE), 0.05),
        'b_w_s': nrm(ks[12], (N_B, GMLP_GROUPS, GMLP_CHUNK, GMLP_CHUNK), GMLP_CHUNK ** -0.5),
        'b_b_s': 1.0 + nrm(ks[13], (N_B, GMLP_GROUPS, GMLP_CHUNK), 0.1),
        'b_w_o': nrm(ks[14], (N_B, D_GATE, D), D_GATE ** -0.5),
        'c_w_qkv': nrm(ks[15], (N_C, D, 3 * D), D ** -0.5),
        'c_lambda': nrm(ks[16], (N_C, 4, HEAD_DIM_C), 0.1),
        'c_subln_g': 1.0 + nrm(ks[17], (N_C, 2 * HEAD_DIM_C), 0.05),
        'c_w_o': nrm(ks[18], (N_C, D, D), D ** -0.5),
    }

def second_block(x, norm_g, ff1_w_in, ff1_w_out, ff2_w_in, ff2_w_out, a_w_qkv, a_rel_bias, a_w_o, b_w_in, b_ln_g, b_ln_b, b_w_s, b_b_s, b_w_o, c_w_qkv, c_lambda, c_subln_g, c_w_o):
    for i in range(DEPTH_2):
        g = norm_g[i]
        x = x + 0.5 * rms_norm(swiglu(rms_norm(x, g[0]), ff1_w_in[i], ff1_w_out[i]), g[1])
        h = rms_norm(x, g[2])
        kind, j = i % N_MIXERS, i // N_MIXERS
        if kind == 0:
            m = mixer_a(h, a_w_qkv[j], a_rel_bias[j], a_w_o[j])
        elif kind == 1:
            m = mixer_b(h, b_w_in[j], b_ln_g[j], b_ln_b[j], b_w_s[j], b_b_s[j], b_w_o[j])
        else:
            lambda_init = 0.8 - 0.6 * math.exp(-0.3 * i)
            m = mixer_c(h, c_w_qkv[j], c_lambda[j], c_subln_g[j], c_w_o[j], lambda_init)
        x = x + rms_norm(m, g[3])
        x = x + 0.5 * rms_norm(swiglu(rms_norm(x, g[4]), ff2_w_in[i], ff2_w_out[i]), g[5])
    return x


def setup_inputs(seed=0):
    out = dict(first_inputs(seed))
    for name, value in second_inputs(seed + 1).items():
        if name != "x":
            out[name + "_2"] = value
    return out


def reference(
    x, c, norm1_g, norm2_g, w_ada, b_ada, w_in, lam_re, lam_im, log_step, s5_b_re, s5_b_im,
    s5_c_re, s5_c_im, s5_d, w_glu, b_glu, conv_w, a_log, dt_bias, gdn_norm_g, w_out,
    w_router_grp, w_router_exp, w_gate, w_up, w_down, normf_g, norm_g_2, ff1_w_in_2,
    ff1_w_out_2, ff2_w_in_2, ff2_w_out_2, a_w_qkv_2, a_rel_bias_2, a_w_o_2, b_w_in_2, b_ln_g_2,
    b_ln_b_2, b_w_s_2, b_b_s_2, b_w_o_2, c_w_qkv_2, c_lambda_2, c_subln_g_2, c_w_o_2,
):
    x = first_block(
        x, c, norm1_g, norm2_g, w_ada, b_ada, w_in, lam_re, lam_im, log_step, s5_b_re, s5_b_im,
        s5_c_re, s5_c_im, s5_d, w_glu, b_glu, conv_w, a_log, dt_bias, gdn_norm_g, w_out,
        w_router_grp, w_router_exp, w_gate, w_up, w_down, normf_g,
    )
    return second_block(
        x, norm_g_2, ff1_w_in_2, ff1_w_out_2, ff2_w_in_2, ff2_w_out_2, a_w_qkv_2, a_rel_bias_2,
        a_w_o_2, b_w_in_2, b_ln_g_2, b_ln_b_2, b_w_s_2, b_b_s_2, b_w_o_2, c_w_qkv_2, c_lambda_2,
        c_subln_g_2, c_w_o_2,
    )


_drawn_inputs = setup_inputs


def setup_inputs(seed=0):
    import zlib

    import numpy as np

    out = dict(_drawn_inputs(seed))
    spreads = {}
    factors = {'norm1_g': 3.311,
     'lam_re': 64.0,
     's5_b_re': 4.045,
     's5_b_im': 2.887,
     's5_c_re': 3.217,
     's5_c_im': 3.653,
     'b_glu': 41.285,
     'gdn_norm_g': 3.7,
     'b_ln_g_2': 3.595,
     'b_ln_b_2': 3.162,
     'c_lambda_2': 2.888,
     'norm2_g': 5.974}
    for name, (base, spread) in spreads.items():
        noise = np.random.default_rng([zlib.crc32(name.encode()), seed]).standard_normal(out[name].shape)
        drawn = base * np.exp(spread * noise) if base else spread * noise
        out[name] = jnp.asarray(drawn.astype(out[name].dtype))
    for name, factor in factors.items():
        out[name] = (out[name] * factor).astype(out[name].dtype)
    return out
```

```python
import math
from contextlib import ExitStack

import numpy as np

import concourse.bass as bass
from concourse import mybir

F32 = mybir.dt.float32
F32R = mybir.dt.float32r
ALU = mybir.AluOpType
ACT = mybir.ActivationFunctionType
AX = mybir.AxisListType.X

P = 128
D = 1024
T = 256
KD = D // P
NT = T // P
EPS = 1e-6
N_EXPERTS = 32
N_GROUPS = 4
PER_GROUP = 8
D_FF = 2816
HID = 256
FF_STEPS = D_FF // HID
LAYERS = 4
KINDS = [i % 3 for i in range(LAYERS)]
D_S5 = 512
CS5 = D_S5 // P
HEADS = 4
DK = 128
TH = HEADS * NT
CONV = 4
S5_TILES = 16
LEVELS = 7
LAMBDA_INIT = 0.8 - 0.6 * math.exp(-0.3 * 2)
GA, GU, GD = 0, 1, 2

COLS = {}


def _cols(spec):
    at = 0
    for name, n in spec:
        COLS[name] = (at, at + n)
        at += n
    return at


NCOLS = _cols([("lam_re", 16), ("lam_im", 16), ("log_step", 16), ("s5_d", CS5), ("b_glu", CS5),
               ("conv_w", 12 * CONV), ("norm1", KD), ("norm2", KD), ("pre", LAYERS * 3 * KD), ("gdn_g", 1),
               ("subln", 1), ("c", KD), ("dt_bias", TH), ("a_log", TH), ("lam_c", 4),
               ("b_re", CS5 * P), ("b_im", CS5 * P), ("c_re", S5_TILES * 32), ("c_im", S5_TILES * 32)])

MATS = {name: i for i, name in enumerate(["ident", "upto", "ones", "flip"] + [f"level{k}" for k in range(LEVELS)])}


def constants():
    i, j = np.arange(P)[:, None], np.arange(P)[None, :]
    mats = [i == j, i <= j, np.ones((P, P), bool), i + j == P - 1]
    for k in range(LEVELS):
        s = 1 << k
        mats.append((i // (2 * s) == j // (2 * s)) & (i // s % 2 == 1) & (j // s % 2 == 0))
    mats = np.stack(mats, 1).astype(np.float32).reshape(P, -1)
    slopes = (2.0 ** (-8.0 * (np.arange(8, dtype=np.float32) + 1.0) / 8)).astype(np.float32)
    q = np.arange(P)
    k1 = np.arange(T)
    dist = np.abs(q[:, None] + P - k1).astype(np.float32)
    barred = k1 >= ((q[:, None] + P) // 64 + 1) * 64
    alibi = np.where(barred, np.float32(-1e30), -slopes[:, None, None] * dist)
    alibi = np.repeat(alibi, 2, 0).transpose(1, 0, 2)
    first = np.tile(np.array([8, 7, 6, 5, 4, 3, 2, 1], np.float32), (P, 1))
    return mats, np.ascontiguousarray(alibi.astype(np.float32)), first


class Plan:

    def __init__(self):
        self.base = {}
        self.at = [0, 0, 0]

    def add(self, name, *counts):
        self.base[name] = tuple(self.at)
        self.at = [a + n for a, n in zip(self.at, counts)]


PLAN = Plan()
PLAN.add("ada", 12, 12, 0)
PLAN.add("w_in", 5, 5, 0)
PLAN.add("w_glu", 0, 0, 1)
PLAN.add("w_out", 2, 2, 0)
PLAN.add("moe", N_EXPERTS, N_EXPERTS, N_EXPERTS)
for _l in range(LAYERS):
    PLAN.add(f"ff{_l}a", FF_STEPS, FF_STEPS, FF_STEPS)
    PLAN.add(f"mix{_l}", *((4, 4, 0) if KINDS[_l] == 1 else (6, 6, 0)))
    PLAN.add(f"wo{_l}", 2, 2, 0)
    PLAN.add(f"ff{_l}b", FF_STEPS, FF_STEPS, FF_STEPS)


def build(nc, a, out):
    ctx = ExitStack()
    sems = {}

    def S(name):
        if name not in sems:
            sems[name] = ctx.enter_context(nc.semaphore(name))
        return sems[name]

    def sb(name, shape, dt=F32):
        return ctx.enter_context(nc.sbuf_tensor(name, shape, dt))

    with ctx:
        raw = [sb(f"raw{s}", [P, 2048]) for s in range(3)]
        whi = [sb(f"whi{s}", [P, 2048], F32R) for s in range(3)]
        wlo = [sb(f"wlo{s}", [P, 2048], F32R) for s in range(3)]
        x = sb("x", [P, NT, D])
        act_f = sb("act_f", [P, KD, T])
        act_hi = sb("act_hi", [P, KD, T], F32R)
        act_lo = sb("act_lo", [P, KD, T], F32R)
        h_hi = sb("h_hi", [P, 2, T], F32R)
        h_lo = sb("h_lo", [P, 2, T], F32R)
        scratch = sb("scratch", [P, 4096])
        junk = scratch[:, 0:1024]
        rows = scratch[:, 1024:3072].rearrange("p (s n) -> p s n", s=2)
        sil = scratch[:, 3072:3584]
        h_raw = scratch[:, 3584:4096]
        mats = sb("mats", [P, len(MATS), P])
        cols = sb("cols", [P, NCOLS])
        modc = sb("modc", [P, 4, KD])
        first = sb("first", [P, PER_GROUP])
        small = sb("small", [P, 512])
        half = sb("half", [P, 8])
        arena = sb("arena", [P, 16384])
        psum = ctx.enter_context(nc.psum_tensor("psum", [P, 8, 512], F32))
        acc = psum[:, 0:4, :]
        gu = psum[:, 4:8, :]

        def mat(name):
            return mats[:, MATS[name], :]

        def col(name, k=0, n=1):
            at = COLS[name][0] + k
            return cols[:, at:at + n]

        def area(block, n, blocks=1):
            return arena[:, 1024 * block:1024 * block + n]

        ident = mat("ident")

        raw_loaded = [S(f"raw_loaded{s}") for s in range(3)]
        hi_ready = [S(f"hi_ready{s}") for s in range(3)]
        lo_ready = [S(f"lo_ready{s}") for s in range(3)]
        slab_used = [S(f"slab_used{s}") for s in range(3)]

        block = ctx.enter_context(nc.Block())

        def col_slab(w, c0):
            return w[:, c0:c0 + 256].rearrange("(k p) n -> p k n", p=P)

        def load(sp, s, n, src):
            if not (isinstance(n, int) and n == 0):
                sp.wait_ge(lo_ready[s], n)
            k = src.shape[1]
            sp.dma_start(raw[s][:, :k * src.shape[2]].rearrange("p (k n) -> p k n", k=k), src).then_inc(raw_loaded[s], 16)

        def split_hi(act, s, n):
            act.wait_ge(raw_loaded[s], n * 16 + 16)
            if not (isinstance(n, int) and n == 0):
                act.wait_ge(slab_used[s], n)
            act.activation(whi[s][:], raw[s][:], ACT.Copy).then_inc(hi_ready[s], 1)

        def split_lo(dve, s, n):
            dve.wait_ge(hi_ready[s], n + 1)
            dve.tensor_tensor(wlo[s][:], raw[s][:], whi[s][:].bitcast(F32), ALU.subtract).then_inc(lo_ready[s], 1)

        def slab_views(s, k):
            return (whi[s][:].rearrange("p (k n) -> p k n", k=k), wlo[s][:].rearrange("p (k n) -> p k n", k=k))

        def three(pe, out_ap, lhs, rhs, first, last):
            pe.matmul(out_ap, lhs[0], rhs[0], start=first, stop=False)
            pe.matmul(out_ap, lhs[0], rhs[1], start=False, stop=False)
            return pe.matmul(out_ap, lhs[1], rhs[0], start=False, stop=last)

        def proj_t(pe, s, bank, act_k=KD, m0=0, ms=2, k_cols=256):
            hi, lo = slab_views(s, 2048 // k_cols)
            for m in range(ms):
                for k in range(act_k):
                    c = (m0 + m) * P
                    last = three(pe, psum[:, bank, m * T:(m + 1) * T], (hi[:, k, c:c + P], lo[:, k, c:c + P]),
                                 (act_hi[:, k, :], act_lo[:, k, :]), k == 0, k == act_k - 1)
            return last

        def proj_n(pe, s, out_of):
            hi, lo = slab_views(s, KD)
            for t in range(NT):
                for k in range(KD):
                    last = three(pe, out_of(t), (act_hi[:, k, t * P:(t + 1) * P], act_lo[:, k, t * P:(t + 1) * P]),
                                 (hi[:, k, :], lo[:, k, :]), k == 0, k == KD - 1)
            return last

        ss_pre, r_pre, ss_post, r_post = (small[:, 8 * i:8 * i + NT] for i in range(4))

        def pre_act(act, n):
            for t in range(NT):
                if n:
                    act.wait_ge(S("x_ready"), NT * (n - 1) + t + 1)
                    act.wait_ge(S("pre_rstd"), NT * (n - 1) + t + 1)
                else:
                    act.wait_ge(S("x_loaded"), 16)
                if n == 2:
                    act.wait_ge(S("final_sums"), NT)
                elif n > 2:
                    act.wait_ge(S("post_sums"), NT * (n - 2))
                if t:
                    act.wait_ge(S("pre_sums"), NT * n + t)
                act.activation(junk, x[:, t, :], ACT.Square, accum_out=ss_pre[:, t:t + 1]).then_inc(S("pre_sums"), 1)

        def rstd(pool, out_ap, in_ap, scale, eps, sem):
            pool.tensor_scalar(out_ap, in_ap, scale, eps, ALU.mult, ALU.add).then_inc(S("pool_step"), 1)
            pool_steps[0] += 1
            pool.wait_ge(S("pool_step"), pool_steps[0])
            pool.tensor_tensor(out_ap, out_ap, half[:, 0:out_ap.shape[1]], ALU.pow).then_inc(sem, 1)

        pool_steps = [0]

        def pre_pool(pool, n):
            for t in range(NT):
                pool.wait_ge(S("pre_sums"), NT * n + t + 1)
                if n:
                    pool.wait_ge(S("normed"), NT * (n - 1) + t + 1)
                rstd(pool, r_pre[:, t:t + 1], ss_pre[:, t:t + 1], 1.0 / D, EPS, S("pre_rstd"))

        def pre_dve(dve, n, scales, shifts=None, normed=None):
            for t in range(NT):
                dve.wait_ge(S("pre_rstd"), NT * n + t + 1)
                dve.tensor_scalar(xn(t), x[:, t, :], r_pre[:, t:t + 1], None, ALU.mult).then_inc(S("normed"), 1)
            for k in range(KD):
                if k % 2 == 0:
                    dve.wait_ge(S("transposed"), 4 * n + k // 2 + 1)
                dve.tensor_scalar(act_f[:, k, :], gu[:, k // 2, (k % 2) * T:(k % 2 + 1) * T], scales(k),
                                  shifts(k) if shifts else None, ALU.mult,
                                  ALU.add if shifts else ALU.bypass).then_inc(S("act_f"), 1)

        acts = [0]

        def pre_split_dve(dve, n_act):
            for q in range(4):
                dve.wait_ge(S("act_hi"), 4 * n_act + q + 1)
                dve.tensor_tensor(act_lo[:, 2 * q:2 * q + 2, :], act_f[:, 2 * q:2 * q + 2, :],
                                  act_hi[:, 2 * q:2 * q + 2, :].bitcast(F32), ALU.subtract).then_inc(S("act_lo"), 1)

        def split_act(act, n_act):
            for q in range(4):
                act.wait_ge(S("act_f"), 8 * n_act + 2 * q + 2)
                act.activation(act_hi[:, 2 * q:2 * q + 2, :], act_f[:, 2 * q:2 * q + 2, :], ACT.Copy)\
                   .then_inc(S("act_hi"), 1)

        def xn(t):
            return arena[:, 14336 + t * D:14336 + (t + 1) * D]

        def pre_pe(pe, n):
            for t in range(NT):
                pe.wait_ge(S("normed"), NT * n + t + 1)
                for k in range(KD):
                    at = (k % 2) * T + t * P
                    last = pe.transpose(gu[:, k // 2, at:at + P], xn(t)[:, k * P:(k + 1) * P], ident)
                    if t == NT - 1 and k % 2:
                        last.then_inc(S("transposed"), 1)

        def steps(eng, name):
            count = [0]

            def done(ins):
                ins.then_inc(S(name), 1)
                count[0] += 1
                eng.wait_ge(S(name), count[0])
            return done

        def bc(ap, n):
            return ap.unsqueeze(2).to_broadcast([P, ap.shape[1], n])

        def rep(ap, m):
            return ap.unsqueeze(1).to_broadcast([P, m, ap.shape[1]])

        def post_act(act, n, s, used):
            for t in range(NT):
                act.wait_ge(slab_used[s], used)
                if n:
                    act.wait_ge(S("post_rstd"), NT * (n - 1) + t + 1)
                if t:
                    act.wait_ge(S("post_sums"), NT * n + t)
                act.activation(junk.rearrange("p (b n) -> p b n", b=2), acc[:, 2 * t:2 * t + 2, :], ACT.Square,
                               accum_out=ss_post[:, t:t + 1]).then_inc(S("post_sums"), 1)

        def post_pool(pool, n, f):
            for t in range(NT):
                pool.wait_ge(S("post_sums"), NT * n + t + 1)
                if n:
                    pool.wait_ge(S("y_scaled"), NT * (n - 1) + t + 1)
                rstd(pool, r_post[:, t:t + 1], ss_post[:, t:t + 1], 1.0 / (D * f * f), EPS / (f * f), S("post_rstd"))

        def post_dve(dve, n, row):
            dve.wait_ge(S(f"row_loaded{row % 2}"), 16 * (row // 2 + 1))
            g = rows[:, row % 2, :].rearrange("p (b n) -> p b n", b=2)
            for t in range(NT):
                dve.wait_ge(S("post_rstd"), NT * n + t + 1)
                y = xn(t).rearrange("p (b n) -> p b n", b=2)
                ins = dve.scalar_tensor_tensor(y, acc[:, 2 * t:2 * t + 2, :], r_post[:, t:t + 1], g, ALU.mult, ALU.mult)
                ins.then_inc(S("y_scaled"), 1)
                dve.wait_ge(S("y_scaled"), NT * n + t + 1)
                dve.tensor_tensor(x[:, t, :], x[:, t, :], xn(t), ALU.add).then_inc(S("x_ready"), 1)

        gbank, ubank = psum[:, 4, :], psum[:, 5, :]

        def ff_load(sp, name, n, g_src, u_src, d_src):
            b = PLAN.base[name]
            load(sp, GA, b[GA], g_src(0))
            load(sp, GU, b[GU], u_src(0))
            with sp.Fori(1, n) as i:
                load(sp, GA, i + b[GA], g_src(i))
                load(sp, GU, i + b[GU], u_src(i))
                load(sp, GD, i + (b[GD] - 1), d_src(i - 1))
            load(sp, GD, b[GD] + n - 1, d_src(n - 1))

        def silu_step(act, b, hb, i):
            act.wait_ge(slab_used[GU], i + (b[GU] + 1))
            act.wait_ge(S("h_raw"), i + hb)
            act.activation(sil, gbank, ACT.Silu).then_inc(S("sil"), 1)

        def h_hi_step(act, b, hb, i):
            act.wait_ge(S("h_raw"), i + (hb + 1))
            act.wait_ge(slab_used[GD], i + b[GD])
            act.activation(h_hi[:].rearrange("p m t -> p (m t)"), h_raw, ACT.Copy).then_inc(S("h_hi"), 1)

        def ff_act(act, name, n, hb, nxt):
            b = PLAN.base[name]
            with act.Fori(1, n) as i:
                split_hi(act, GA, i + b[GA])
                silu_step(act, b, hb, i - 1)
                split_hi(act, GU, i + b[GU])
                h_hi_step(act, b, hb, i - 1)
                split_hi(act, GD, i + (b[GD] - 1))
            silu_step(act, b, hb, n - 1)
            h_hi_step(act, b, hb, n - 1)
            split_hi(act, GD, b[GD] + n - 1)
            head_act(act, nxt)

        def h_step(dve, b, hb, i, gates):
            dve.wait_ge(S("sil"), i + (hb + 1))
            dve.wait_ge(S("h_lo"), i + hb)
            if gates is None:
                dve.tensor_tensor(h_raw, sil, ubank, ALU.mult).then_inc(S("h_raw"), 1)
            else:
                dve.tensor_tensor(h_raw, sil, ubank, ALU.mult).then_inc(S("h_ungated"), 1)
                dve.wait_ge(S("h_ungated"), i + 1)
                v = h_raw.rearrange("p (m t) -> p m t", m=2)
                gate = gates[:, bass.ds(i * T, T)] if not isinstance(i, int) else gates[:, i * T:(i + 1) * T]
                dve.tensor_tensor(v, v, rep(gate, 2), ALU.mult).then_inc(S("h_raw"), 1)

        def h_lo_step(dve, b, hb, i):
            dve.wait_ge(S("h_hi"), i + (hb + 1))
            dve.tensor_tensor(h_lo[:].rearrange("p m t -> p (m t)"), h_raw,
                              h_hi[:].rearrange("p m t -> p (m t)").bitcast(F32), ALU.subtract).then_inc(S("h_lo"), 1)

        def ff_dve(dve, name, n, hb, nxt, gates=None):
            b = PLAN.base[name]
            with dve.Fori(1, n) as i:
                split_lo(dve, GA, i + b[GA])
                h_step(dve, b, hb, i - 1, gates)
                split_lo(dve, GU, i + b[GU])
                h_lo_step(dve, b, hb, i - 1)
                split_lo(dve, GD, i + (b[GD] - 1))
            h_step(dve, b, hb, n - 1, gates)
            h_lo_step(dve, b, hb, n - 1)
            split_lo(dve, GD, b[GD] + n - 1)
            head_dve(dve, nxt)

        def ff_up(pe, b, hb, i, first):
            pe.wait_ge(lo_ready[GA], i + (b[GA] + 1))
            if not first:
                pe.wait_ge(S("h_raw"), i + hb)
            proj_t(pe, GA, 4).then_inc(slab_used[GA], 1)
            pe.wait_ge(lo_ready[GU], i + (b[GU] + 1))
            proj_t(pe, GU, 5).then_inc(slab_used[GU], 1)

        def ff_down(pe, b, hb, i, first, last):
            pe.wait_ge(S("h_lo"), i + (hb + 1))
            pe.wait_ge(lo_ready[GD], i + (b[GD] + 1))
            hi, lo = slab_views(GD, 2)
            for t in range(NT):
                for j in range(2):
                    ts = slice(t * P, (t + 1) * P)
                    for n in range(2):
                        ns = slice(n * 512, (n + 1) * 512)
                        ins = three(pe, acc[:, 2 * t + n, :], (h_hi[:, j, ts], h_lo[:, j, ts]),
                                    (hi[:, j, ns], lo[:, j, ns]), first and j == 0, last and j == 1)
            ins.then_inc(slab_used[GD], 1)

        def ff_pe(pe, name, n, hb, n_act, between=None):
            b = PLAN.base[name]
            pe.wait_ge(S("act_lo"), 4 * n_act + 4)
            ff_up(pe, b, hb, 0, True)
            if between:
                between(pe)
            ff_up(pe, b, hb, 1, False)
            ff_down(pe, b, hb, 0, True, False)
            with pe.Fori(2, n) as i:
                ff_up(pe, b, hb, i, False)
                ff_down(pe, b, hb, i - 1, False, False)
            ff_down(pe, b, hb, n - 1, False, True)

        def slab_at(name, j):
            return j % 2, PLAN.base[name][j % 2] + j // 2

        def head_act(act, name):
            for j in range(2):
                if name:
                    split_hi(act, *slab_at(name, j))

        def head_dve(dve, name):
            for j in range(2):
                if name:
                    split_lo(dve, *slab_at(name, j))

        def next_hi(act, name, j, n):
            if j + 2 < n:
                split_hi(act, *slab_at(name, j + 2))

        def next_lo(dve, name, j, n):
            if j + 2 < n:
                split_lo(dve, *slab_at(name, j + 2))

        def cols_load(sp, name, n, src):
            for j in range(n):
                load(sp, *slab_at(name, j), src(j))

        def cols_used(eng, name, j):
            s, n = slab_at(name, j)
            eng.wait_ge(slab_used[s], n + 1)

        def cols_pe(pe, name, n0, n1, kind, evac0):
            def one(i, s):
                pe.wait_ge(lo_ready[s], i + (PLAN.base[name][s] + 1))
                pe.wait_ge(S("proj_evac"), i * 2 + (evac0 + s - 1))
                if kind == "t":
                    last = proj_t(pe, s, 4 + s)
                else:
                    last = proj_n(pe, s, lambda t: psum[:, 4 + s, t * T:(t + 1) * T])
                last.then_inc(slab_used[s], 1)
            with pe.Fori(n0 // 2, n1 // 2) as i:
                one(i, 0)
                one(i, 1)

        def wo_pe(pe, name, n_act):
            pe.wait_ge(S("act_lo"), 4 * n_act + 4)
            for j in range(4):
                s, n = slab_at(name, j)
                pe.wait_ge(lo_ready[s], n + 1)
                proj_n(pe, s, lambda t: acc[:, 2 * t + j // 2, (j % 2) * T:(j % 2 + 1) * T]).then_inc(slab_used[s], 1)

        def wo_act(act, name, nxt):
            for j in range(4):
                next_hi(act, name, j, 4)
            head_act(act, nxt)

        def wo_dve(dve, name, nxt):
            for j in range(4):
                next_lo(dve, name, j, 4)
            head_dve(dve, nxt)
        at = [64]

        def tiny(n):
            at[0] += n
            return small[:, at[0] - n:at[0]]

        eps_col, one_col = tiny(1), tiny(1)
        c_act = tiny(KD)
        step_s, lr_s, rad_s, th_s, k_s, red_s, sin_s, cos_s, den_s, ca_s, cb_s, tmp_s = (tiny(16) for _ in range(12))
        turn_w = small[:, at[0]:at[0] + 32]
        g_s, beta_s, sp_s, e_s, gc_s, egc_s, bg_s, ea_s = (tiny(TH) for _ in range(8))
        tail_s = tiny(HEADS)
        f_sum, f_rstd = tiny(NT), tiny(NT)
        wsmall = sb("wsmall", [P, KD, 44])
        w_router, w_ab = wsmall[:, :, 0:36], wsmall[:, :, 36:44]

        mod = arena[:, 0:6 * D]
        cb_f = act_f[:, 0:4, :].rearrange("p k t -> p (k t)").rearrange("p (k n) -> p k n", k=KD)
        cb_hi = act_hi[:, 0:4, :].rearrange("p k t -> p (k t)").rearrange("p (k n) -> p k n", k=KD)
        cb_lo = act_lo[:, 0:4, :].rearrange("p k t -> p (k t)").rearrange("p (k n) -> p k n", k=KD)
        N_ADA = 6 * D // 256

        def ada_pe(pe):
            def one(i, s, first):
                pe.wait_ge(lo_ready[s], i + 1)
                if not first:
                    pe.wait_ge(S("proj_evac"), i * 2 + (s - 1))
                hi, lo = slab_views(s, KD)
                for k in range(KD):
                    last = three(pe, psum[:, 4 + s, 0:256], (cb_hi[:, k, :], cb_lo[:, k, :]), (hi[:, k, :], lo[:, k, :]),
                                 k == 0, k == KD - 1)
                last.then_inc(slab_used[s], 1)
            pe.wait_ge(S("cb_lo"), 1)
            one(0, 0, True)
            one(0, 1, True)
            with pe.Fori(1, N_ADA // 2) as i:
                one(i, 0, False)
                one(i, 1, False)

        def ada_act(act):
            with act.Fori(1, N_ADA // 2) as i:
                split_hi(act, 0, i)
                split_hi(act, 1, i)
            head_act(act, "w_in")

        def ada_dve(dve):
            def evac(i, s):
                dve.wait_ge(slab_used[s], i + 1)
                part = mod[:, bass.ds(i * 512 + s * 256, 256)] if not isinstance(i, int) else mod[:, i * 512 + s * 256:i * 512 + s * 256 + 256]
                dve.tensor_tensor(part, part, psum[:, 4 + s, 0:256], ALU.add).then_inc(S("proj_evac"), 1)
            dve.wait_ge(S("bias_loaded"), 16)
            with dve.Fori(1, N_ADA // 2) as i:
                evac(i - 1, 0)
                split_lo(dve, 0, i)
                evac(i - 1, 1)
                split_lo(dve, 1, i)
            evac(N_ADA // 2 - 1, 0)
            evac(N_ADA // 2 - 1, 1)
            head_dve(dve, "w_in")

        def mod_dve(dve, done):
            dve.wait_ge(S("proj_evac"), N_ADA)
            tmp = act_f[:, 4:8, :].rearrange("p k t -> p (k t)").rearrange("p (k n) -> p k n", k=KD)
            for q, (part, g) in enumerate(((0, None), (1, "norm1"), (3, None), (4, "norm2"))):
                done(dve.tensor_tensor(tmp, mod[:, part * D:(part + 1) * D].rearrange("p (k n) -> p k n", k=KD),
                                       rep(ident, KD), ALU.mult))
                done(dve.reduce_sum(modc[:, q, :], tmp, AX))
                if g:
                    done(dve.scalar_tensor_tensor(modc[:, q, :], modc[:, q, :], 1.0, col(g, 0, KD), ALU.add, ALU.mult))

        e_re = arena[:, 6 * 1024:10 * 1024].rearrange("p (j t) -> p j t", j=S5_TILES)
        e_im = arena[:, 10 * 1024:14 * 1024].rearrange("p (j t) -> p j t", j=S5_TILES)
        cx_re = col("c_re", 0, 512).rearrange("p (j h) -> p j h", j=S5_TILES)
        cx_nim = col("c_im", 0, 512).rearrange("p (j h) -> p j h", j=S5_TILES)
        TWO_PI = 2 * math.pi
        C1 = 6.28125

        def s5_param_act(act):
            act.wait_ge(S("cols_loaded"), 16)
            act.activation(c_act, col("c", 0, KD), ACT.Silu).then_inc(S("c_act"), 1)
            act.activation(step_s, col("log_step", 0, 16), ACT.Exp).then_inc(S("s5_step"), 1)
            act.wait_ge(S("s5_lr"), 1)
            act.activation(rad_s, lr_s, ACT.Exp).then_inc(S("s5_rad"), 1)
            act.wait_ge(S("s5_angle"), 1)
            act.activation(sin_s, red_s, ACT.Sin).then_inc(S("s5_turn"), 1)
            act.activation(cos_s, k_s, ACT.Sin).then_inc(S("s5_turn"), 1)

        def s5_param_dve(dve, done):
            dve.memset(eps_col, EPS)
            dve.memset(one_col, 1.0)
            dve.memset(half[:], -0.5).then_inc(S("half"), 1)
            dve.wait_ge(S("c_act"), 1)
            done(dve.tensor_copy(cb_f, bc(c_act, P)))
            done(dve.tensor_copy(cb_hi, cb_f))
            dve.tensor_tensor(cb_lo, cb_f, cb_hi.bitcast(F32), ALU.subtract).then_inc(S("cb_lo"), 1)
            dve.wait_ge(S("s5_step"), 1)
            dve.tensor_tensor(lr_s, col("lam_re", 0, 16), step_s, ALU.mult).then_inc(S("s5_lr"), 1)
            done(dve.tensor_tensor(th_s, col("lam_im", 0, 16), step_s, ALU.mult))
            done(dve.tensor_scalar(k_s, th_s, 1 / TWO_PI, 12582912.0, ALU.mult, ALU.add))
            done(dve.tensor_scalar(k_s, k_s, 12582912.0, None, ALU.subtract))
            done(dve.scalar_tensor_tensor(red_s, k_s, -C1, th_s, ALU.mult, ALU.add))
            done(dve.scalar_tensor_tensor(red_s, k_s, -(TWO_PI - C1), red_s, ALU.mult, ALU.add))
            done(dve.tensor_scalar(red_s, red_s, 3.1415925, -3.1415925, ALU.min, ALU.max))
            done(dve.tensor_scalar(k_s, red_s, -1.0, None, ALU.mult))
            done(dve.tensor_tensor(k_s, k_s, red_s, ALU.max))
            dve.tensor_scalar(k_s, k_s, -1.0, math.pi / 2, ALU.mult, ALU.add).then_inc(S("s5_angle"), 1)
            dve.wait_ge(S("s5_turn"), 2)
            dve.wait_ge(S("s5_rad"), 1)
            lre, lim = col("lam_re", 0, 16), col("lam_im", 0, 16)
            done(dve.tensor_tensor(ca_s, rad_s, cos_s, ALU.mult))
            done(dve.tensor_scalar(ca_s, ca_s, 1.0, None, ALU.subtract))
            done(dve.tensor_tensor(cb_s, rad_s, sin_s, ALU.mult))
            done(dve.tensor_tensor(den_s, lre, lre, ALU.mult))
            done(dve.tensor_tensor(tmp_s, lim, lim, ALU.mult))
            done(dve.tensor_tensor(den_s, den_s, tmp_s, ALU.add))
            done(dve.reciprocal(den_s, den_s))
            done(dve.tensor_tensor(tmp_s, ca_s, lre, ALU.mult))
            done(dve.tensor_tensor(k_s, cb_s, lim, ALU.mult))
            done(dve.tensor_tensor(k_s, k_s, tmp_s, ALU.add))
            done(dve.tensor_tensor(tmp_s, cb_s, lre, ALU.mult))
            done(dve.tensor_tensor(cb_s, ca_s, lim, ALU.mult))
            done(dve.tensor_tensor(cb_s, tmp_s, cb_s, ALU.subtract))
            done(dve.tensor_tensor(cb_s, cb_s, den_s, ALU.mult))
            dve.tensor_tensor(ca_s, k_s, den_s, ALU.mult).then_inc(S("s5_coef"), 1)

        def s5_tables_pool(pool, done):
            pool.wait_ge(S("s5_turn"), 2)
            wr, wi = turn_w[:, 0:16], turn_w[:, 16:32]
            w2, w3 = lr_s, th_s
            pool.memset(e_re[:, :, 0:1], 1.0)
            pool.memset(e_im[:, :, 0:1], 0.0)
            pool.tensor_copy(wr, cos_s)
            done(pool.tensor_copy(wi, sin_s))
            for d in (1, 2, 4, 8, 16, 32, 64, 128):
                for at0 in range(0, d, 64):
                    n = min(d, 64)
                    m1 = arena[:, 14336:14336 + 16 * n].rearrange("p (j t) -> p j t", j=16)
                    m2 = arena[:, 15360:15360 + 16 * n].rearrange("p (j t) -> p j t", j=16)
                    src, dst = slice(at0, at0 + n), slice(d + at0, d + at0 + n)
                    pool.tensor_tensor(m1, e_re[:, :, src], bc(wr, n), ALU.mult)
                    done(pool.tensor_tensor(m2, e_im[:, :, src], bc(wi, n), ALU.mult))
                    done(pool.tensor_tensor(e_re[:, :, dst], m1, m2, ALU.subtract))
                    pool.tensor_tensor(m1, e_re[:, :, src], bc(wi, n), ALU.mult)
                    done(pool.tensor_tensor(m2, e_im[:, :, src], bc(wr, n), ALU.mult))
                    done(pool.tensor_tensor(e_im[:, :, dst], m1, m2, ALU.add))
                pool.tensor_tensor(w2, wr, wr, ALU.mult)
                done(pool.tensor_tensor(w3, wi, wi, ALU.mult))
                done(pool.tensor_tensor(w2, w2, w3, ALU.subtract))
                done(pool.tensor_tensor(w3, wr, wi, ALU.mult))
                pool.tensor_tensor(wi, w3, w3, ALU.add)
                done(pool.tensor_copy(wr, w2))
            pool.wait_ge(S("s5_coef"), 1)
            m1 = arena[:, 14336:14336 + 512].rearrange("p (j t) -> p j t", j=16)
            m2 = arena[:, 14848:14848 + 512].rearrange("p (j t) -> p j t", j=16)
            pool.tensor_tensor(m1, cx_re, bc(cb_s, 32), ALU.mult)
            done(pool.tensor_tensor(m2, cx_nim, bc(cb_s, 32), ALU.mult))
            done(pool.tensor_tensor(cx_re, cx_re, bc(ca_s, 32), ALU.mult))
            done(pool.tensor_tensor(cx_re, cx_re, m2, ALU.subtract))
            done(pool.tensor_tensor(cx_nim, cx_nim, bc(ca_s, 32), ALU.mult))
            done(pool.tensor_tensor(cx_nim, cx_nim, m1, ALU.add))
            pool.tensor_scalar(cx_nim, cx_nim, -1.0, None, ALU.mult).then_inc(S("s5_tables"), 1)

        u = area(0, 1024).rearrange("p (c t) -> p c t", c=CS5)
        zs = area(1, 1024).rearrange("p (c t) -> p c t", c=HEADS)
        q_t = area(3, 1024).rearrange("p (c t) -> p c t", c=HEADS)
        k_t = area(4, 1024).rearrange("p (c t) -> p c t", c=HEADS)
        v_t = scratch[:, 1024:2048].rearrange("p (c t) -> p c t", c=HEADS)
        qkv = [q_t, k_t, v_t]
        PADT = T + CONV - 1
        pads = [scratch[:, 2048 + s * 2 * PADT:2048 + (s + 1) * 2 * PADT].rearrange("p (m t) -> p m t", m=2) for s in range(2)]
        ab_bank = psum[:, 7, 0:16].rearrange("p (t e) -> p t e", t=NT)

        def w_in_pe(pe):
            pe.wait_ge(S("act_lo"), 4)
            cols_pe(pe, "w_in", 0, 10, "t", N_ADA)
            pe.wait_ge(S("narrow_loaded"), 32)
            for t in range(NT):
                for k in range(KD):
                    last = pe.matmul(ab_bank[:, t, :], act_f[:, k, t * P:(t + 1) * P], w_ab[:, k, :], start=k == 0, stop=k == KD - 1)
            last.then_inc(S("gates_raw"), 1)

        def w_in_act(act):
            for j in range(10):
                s = j % 2
                cols_used(act, "w_in", j)
                bank = psum[:, 4 + s, :].rearrange("p (m t) -> p m t", m=2)
                if j < 2:
                    act.activation(u[:, 2 * j:2 * j + 2, :], bank, ACT.Copy).then_inc(S("proj_evac"), 1)
                elif j < 8:
                    act.wait_ge(S("pads_zero"), 1)
                    if j >= 4:
                        act.wait_ge(S("convolved"), j - 3)
                    act.activation(pads[s][:, :, CONV - 1:], bank, ACT.Copy).then_inc(S("proj_evac"), 1)
                else:
                    act.activation(zs[:, 2 * (j - 8):2 * (j - 8) + 2, :], bank, ACT.Silu).then_inc(S("proj_evac"), 1)
                next_hi(act, "w_in", j, 10)
            head_act(act, "w_out")
            split_hi(act, GD, PLAN.base["w_glu"][GD])

        def w_in_dve(dve, done):
            for s in range(2):
                last = dve.memset(pads[s][:, :, 0:CONV - 1], 0.0)
            last.then_inc(S("pads_zero"), 1)
            for j in range(10):
                if 2 <= j < 8:
                    jj = j - 2
                    dve.wait_ge(S("proj_evac"), N_ADA + j + 1)
                    dst = qkv[jj // 2][:, 2 * (jj % 2):2 * (jj % 2) + 2, :]
                    for i in range(CONV):
                        for m in range(2):
                            w = col("conv_w", (2 * jj + m) * CONV + i)
                            src = pads[j % 2][:, m, i:i + T]
                            if i == 0:
                                last = dve.tensor_scalar(dst[:, m, :], src, w, None, ALU.mult)
                            else:
                                last = dve.scalar_tensor_tensor(dst[:, m, :], src, w, dst[:, m, :], ALU.mult, ALU.add)
                        if i < CONV - 1:
                            done(last)
                    last.then_inc(S("convolved"), 1)
                next_lo(dve, "w_in", j, 10)
            head_dve(dve, "w_out")
            split_lo(dve, GD, PLAN.base["w_glu"][GD])

        parts = [[b[:, i * 512:(i + 1) * 512].rearrange("p (m t) -> p m t", m=2) for i in range(4)]
                 for b in (arena[:, 14336:16384], scratch[:, 2048:4096])]

        def s5_pe(pe):
            b_re = col("b_re", 0, 512).rearrange("p (c s) -> p c s", c=CS5)
            b_im = col("b_im", 0, 512).rearrange("p (c s) -> p c s", c=CS5)

            def bu(g):
                if g >= 2:
                    pe.wait_ge(S("s5_turned"), g - 1)
                for m in range(2):
                    j = 2 * g + m
                    r, c = 32 * (j % 4), j // 4
                    bank = psum[:, 2 * (g % 2) + m, :]
                    pe.matmul(bank[:, 0:T], b_re[r:r + 32, c, :], u[r:r + 32, c, :], start=True, stop=True)
                    last = pe.matmul(bank[:, T:2 * T], b_im[r:r + 32, c, :], u[r:r + 32, c, :], start=True, stop=True)
                last.then_inc(S("s5_bu"), 1)

            pe.wait_ge(S("proj_evac"), N_ADA + 10)
            pe.wait_ge(S("s5_tables"), 1)
            bu(0)
            for g in range(8):
                if g < 7:
                    bu(g + 1)
                pe.wait_ge(S("s5_states"), g + 1)
                q1, q4, q2, q3 = parts[g % 2]
                for m in range(2):
                    j = 2 * g + m
                    r, c = 32 * (j % 4), j // 4
                    y = psum[r:r + 32, 4 + c % 2, (c // 2) * T:(c // 2 + 1) * T]
                    pe.matmul(y, cx_re[:, j, :], q1[:, m, :], start=True, stop=False)
                    pe.matmul(y, cx_re[:, j, :], q2[:, m, :], start=False, stop=False)
                    pe.matmul(y, cx_nim[:, j, :], q3[:, m, :], start=False, stop=False)
                    last = pe.matmul(y, cx_nim[:, j, :], q4[:, m, :], start=False, stop=True)
                last.then_inc(S("s5_y"), 1)
            pe.wait_ge(S("glu_lo"), 2)
            pe.wait_ge(lo_ready[GD], PLAN.base["w_glu"][GD] + 1)
            for m in range(2):
                last = proj_t(pe, GD, m, act_k=CS5, m0=2 * m, k_cols=512)
            last.then_inc(slab_used[GD], 1)

        def s5_dve(dve, done):
            for g in range(8):
                p1, p2, p3, p4 = parts[g % 2]
                dve.wait_ge(S("s5_bu"), g + 1)
                if g >= 2:
                    dve.wait_ge(S("s5_y"), g - 1)
                b = psum[:, 2 * (g % 2):2 * (g % 2) + 2, :]
                er, ei = e_re[:, 2 * g:2 * g + 2, :], e_im[:, 2 * g:2 * g + 2, :]
                dve.tensor_tensor(p1, b[:, :, 0:T], er, ALU.mult)
                dve.tensor_tensor(p2, b[:, :, T:2 * T], ei, ALU.mult)
                dve.tensor_tensor(p3, b[:, :, T:2 * T], er, ALU.mult)
                ins = dve.tensor_tensor(p4, b[:, :, 0:T], ei, ALU.mult)
                ins.then_inc(S("s5_turned"), 1)
                dve.wait_ge(S("s5_turned"), g + 1)
                dve.tensor_tensor(p1, p1, p2, ALU.add)
                done(dve.tensor_tensor(p3, p3, p4, ALU.subtract))
                for m in range(2):
                    r = rad_s[:, 2 * g + m:2 * g + m + 1].to_broadcast([P, T])
                    dve.tensor_tensor_scan(p2[:, m, :], r, p1[:, m, :], 0.0, ALU.mult, ALU.add)
                    last = dve.tensor_tensor_scan(p4[:, m, :], r, p3[:, m, :], 0.0, ALU.mult, ALU.add)
                done(last)
                dve.tensor_tensor(p1, p2, er, ALU.mult)
                dve.scalar_tensor_tensor(p3, p4, -1.0, ei, ALU.mult, ALU.mult)
                dve.tensor_tensor(p4, p4, er, ALU.mult)
                dve.tensor_tensor(p2, p2, ei, ALU.mult).then_inc(S("s5_states"), 1)
            dve.wait_ge(S("s5_y"), 8)
            for c in range(CS5):
                y = psum[:, 4 + c % 2, (c // 2) * T:(c // 2 + 1) * T]
                dve.scalar_tensor_tensor(act_f[:, c, :], u[:, c, :], col("s5_d", c), y, ALU.mult, ALU.add).then_inc(S("s5_yd"), 1)
            for q in range(2):
                dve.wait_ge(S("glu_hi"), q + 1)
                dve.tensor_tensor(act_lo[:, 2 * q:2 * q + 2, :], act_f[:, 2 * q:2 * q + 2, :],
                                  act_hi[:, 2 * q:2 * q + 2, :].bitcast(F32), ALU.subtract).then_inc(S("glu_lo"), 1)
            sg = arena[:, 14336:15360].rearrange("p (m t) -> p m t", m=CS5)
            for m in range(CS5):
                dve.wait_ge(S("glu_gate"), m + 1)
                dve.tensor_tensor(act_f[:, m, :], act_f[:, m, :], sg[:, m, :], ALU.mult).then_inc(S("act_f"), 1)

        def s5_act(act):
            for q in range(2):
                act.wait_ge(S("s5_yd"), 2 * q + 2)
                act.activation(act_f[:, 2 * q:2 * q + 2, :], act_f[:, 2 * q:2 * q + 2, :], ACT.Gelu_apprx_tanh).then_inc(S("glu_f"), 1)
                act.wait_ge(S("glu_f"), q + 1)
                act.activation(act_hi[:, 2 * q:2 * q + 2, :], act_f[:, 2 * q:2 * q + 2, :], ACT.Copy).then_inc(S("glu_hi"), 1)
            sg = arena[:, 14336:15360].rearrange("p (m t) -> p m t", m=CS5)
            act.wait_ge(slab_used[GD], PLAN.base["w_glu"][GD] + 1)
            for m in range(CS5):
                act.activation(sg[:, m, :], psum[:, m // 2, (m % 2) * T:(m % 2 + 1) * T], ACT.Sigmoid, bias=col("b_glu", m))\
                   .then_inc(S("glu_gate"), 1)
        def blk(b):
            return area(b, 1024)

        def th_view(ap):
            return ap.rearrange("p (e n) -> p e n", n=P)

        def tok_view(ap):
            return ap.rearrange("p (c t) -> p c t", t=T)

        sq, rn = arena[:, 6 * 1024:8 * 1024], arena[:, 8 * 1024:10 * 1024]
        g_b, beta_b, kb_t, eg = blk(10), blk(11), blk(12), blk(13)
        diff = blk(6)
        n_t, qk_t = blk(7), blk(8)
        vb = blk(9)
        qd, kt = arena[:, 14336:14848], arena[:, 14848:15360]
        kbg = arena[:, 15360:15872]
        m_inv, mt_inv = blk(10), blk(11)
        p_sb = blk(0)
        scr_a, scr_b = scratch[:, 2048:3072], scratch[:, 3072:4096]
        nkc, vn0, s1, vn1 = scr_a[:, 0:512], scr_a[:, 512:1024], scr_b[:, 0:512], scr_b[:, 512:1024]
        o_f, o_sq, o_rn = blk(12), blk(13), blk(6)

        def banks(b, n=2):
            return psum[:, b:b + n, :].rearrange("p b n -> p (b n)")

        def gdn_pe(pe):
            ones, upto = mat("ones"), mat("upto")
            pe.wait_ge(S("qk_sq"), 2)
            pe.wait_ge(S("glu_gate"), CS5)
            for e in range(8):
                last = pe.matmul(psum[:, e // 2, (e % 2) * T:(e % 2 + 1) * T], ones, sq[:, e * T:(e + 1) * T], start=True, stop=True)
            last.then_inc(S("qk_sums"), 1)
            pe.wait_ge(S("g_rows"), 2)
            pe.matmul(psum[:, 7, 32:32 + TH], upto, g_s, start=True, stop=True).then_inc(S("g_cum"), 1)
            for e in range(TH):
                last = pe.matmul(banks(4)[:, e * P:(e + 1) * P], th_view(g_b)[:, e, :], upto, start=True, stop=True)
            last.then_inc(S("g_cum_rows"), 1)
            pe.wait_ge(S("qk_root"), 1)
            for e in range(TH):
                last = pe.matmul(banks(0)[:, e * P:(e + 1) * P], th_view(beta_b)[:, e, :], ident, start=True, stop=True)
            last.then_inc(S("beta_rows"), 1)
            pe.wait_ge(S("kb"), 1)
            pe.wait_ge(S("diff"), 1)
            kn, qn, kb = (tok_view(b) for b in (blk(4), blk(3), kb_t))
            for bank, rhs in ((2, kb), (4, qn)):
                for e in range(TH):
                    ts = slice((e % 2) * P, (e % 2 + 1) * P)
                    last = pe.matmul(banks(bank)[:, e * P:(e + 1) * P], kn[:, e // 2, ts], rhs[:, e // 2, ts], start=True, stop=True)
                last.then_inc(S("kk_qk"), 1)
            for e in range(TH):
                last = pe.transpose(banks(0)[:, e * P:(e + 1) * P], blk(4)[:, e * P:(e + 1) * P], ident)
            last.then_inc(S("k_nat"), 1)
            pe.wait_ge(S("n_qk"), 2)
            for e in range(TH):
                last = pe.transpose(banks(2)[:, e * P:(e + 1) * P], scratch[:, 1024 + e * P:1024 + (e + 1) * P], ident)
            last.then_inc(S("v_nat"), 1)
            pe.wait_ge(S("inv_start"), 1)
            pe.wait_ge(S("nat_read"), 1)
            m3, mt3, n3, p3 = (th_view(b) for b in (m_inv, mt_inv, n_t, p_sb))
            for lv in range(LEVELS):
                for hf in range(2):
                    es = range(4 * hf, 4 * hf + 4)
                    if lv:
                        pe.wait_ge(S("inv_done"), 2 * (lv - 1) + hf + 1)
                    for e in es:
                        last = pe.matmul(psum[:, hf, (e % 4) * P:(e % 4 + 1) * P], n3[:, e, :], m3[:, e, :], start=True, stop=True)
                    last.then_inc(S("inv_p"), 1)
                for hf in range(2):
                    es = range(4 * hf, 4 * hf + 4)
                    pe.wait_ge(S("inv_masked"), 2 * lv + hf + 1)
                    for e in es:
                        pe.matmul(psum[:, 2 + hf, (e % 4) * P:(e % 4 + 1) * P], mt3[:, e, :], p3[:, e, :], start=True, stop=True)
                    for e in es:
                        last = pe.matmul(psum[:, 4 + hf, (e % 4) * P:(e % 4 + 1) * P], p3[:, e, :], mt3[:, e, :], start=True, stop=True)
                    last.then_inc(S("inv_q"), 1)
            pe.wait_ge(S("inv_done"), 2 * LEVELS)
            kbg3, kt3, vn03, s13, vn13, nkc3, qd3 = (th_view(b) for b in (kbg, kt, vn0, s1, vn1, nkc, qd))
            vb3, qk3 = th_view(vb), th_view(qk_t)

            def hp(h):
                return slice(h * P, (h + 1) * P)
            for h in range(HEADS):
                last = pe.matmul(psum[:, 0, hp(h)], kbg3[:, h, :], mt3[:, 2 * h + 1, :], start=True, stop=True)
            last.then_inc(S("kc"), 1)
            for h in range(HEADS):
                last = pe.matmul(psum[:, 1, hp(h)], mt3[:, 2 * h, :], vb3[:, 2 * h, :], start=True, stop=True)
            last.then_inc(S("v_new"), 1)
            pe.wait_ge(S("vn_read"), 1)
            for h in range(HEADS):
                last = pe.matmul(psum[:, 6, hp(h)], kt3[:, h, :], vn03[:, h, :], start=True, stop=True)
            last.then_inc(S("state"), 1)
            pe.wait_ge(S("state_read"), 1)
            pe.wait_ge(S("kc_read"), 1)
            for h in range(HEADS):
                pe.matmul(psum[:, 7, hp(h)], mt3[:, 2 * h + 1, :], vb3[:, 2 * h + 1, :], start=True, stop=False)
                last = pe.matmul(psum[:, 7, hp(h)], nkc3[:, h, :], s13[:, h, :], start=False, stop=True)
            last.then_inc(S("v_new"), 1)
            pe.wait_ge(S("vn_read"), 2)
            for h in range(HEADS):
                o0, o1 = banks(2)[:, 2 * h * P:(2 * h + 1) * P], banks(2)[:, (2 * h + 1) * P:(2 * h + 2) * P]
                pe.matmul(o0, vn03[:, h, :], qk3[:, 2 * h, :], start=True, stop=True)
                pe.matmul(o1, s13[:, h, :], qd3[:, h, :], start=True, stop=False)
                last = pe.matmul(o1, vn13[:, h, :], qk3[:, 2 * h + 1, :], start=False, stop=True)
            last.then_inc(S("gdn_o"), 1)
            pe.wait_ge(S("gdn_sq"), 1)
            for b in range(2):
                last = pe.matmul(psum[:, 4 + b, :], ones, o_sq[:, b * 512:(b + 1) * 512], start=True, stop=True)
            last.then_inc(S("gdn_sums"), 1)

        def gdn_act(act):
            for i in range(3):
                act.wait_ge(S("convolved"), 2 * i + 2)
                act.activation(qkv[i], qkv[i], ACT.Silu).then_inc(S("qkv"), 1)
            for i in range(2):
                act.wait_ge(S("qkv"), i + 1)
                act.activation(sq[:, i * 1024:(i + 1) * 1024], blk(3 + i), ACT.Square).then_inc(S("qk_sq"), 1)
            act.wait_ge(S("gate_in"), 1)
            act.activation(e_s, e_s, ACT.Exp, scale=-1.0).then_inc(S("gate_exp"), 1)
            act.activation(bg_s, bg_s, ACT.Exp, scale=-1.0).then_inc(S("gate_exp"), 1)
            act.activation(ea_s, col("a_log", 0, TH), ACT.Exp).then_inc(S("gate_exp"), 1)
            act.wait_ge(S("gate_exp"), 1)
            act.activation(e_s, e_s, ACT.Ln, bias=one_col).then_inc(S("gate_ln"), 1)
            act.wait_ge(S("qk_sums"), 1)
            act.activation(rn, banks(0, 4), ACT.Sqrt, bias=eps_col).then_inc(S("qk_root"), 1)
            act.wait_ge(S("g_cum_rows"), 1)
            act.activation(eg, banks(4), ACT.Exp).then_inc(S("eg"), 1)
            act.wait_ge(S("gc"), 1)
            act.activation(egc_s, gc_s, ACT.Exp).then_inc(S("egc"), 1)
            act.wait_ge(S("tail"), 1)
            act.activation(tail_s, tail_s, ACT.Exp).then_inc(S("tail_exp"), 1)
            act.wait_ge(S("diff"), 1)
            act.activation(diff, diff, ACT.Exp).then_inc(S("decay_exp"), 1)
            act.wait_ge(S("kc"), 1)
            act.activation(nkc, psum[:, 0, :], ACT.Copy, scale=-1.0).then_inc(S("kc_read"), 1)
            act.wait_ge(S("v_new"), 1)
            act.activation(vn0, psum[:, 1, :], ACT.Copy).then_inc(S("vn_read"), 1)
            act.wait_ge(S("state"), 1)
            act.activation(s1, psum[:, 6, :], ACT.Copy).then_inc(S("state_read"), 1)
            act.wait_ge(S("v_new"), 2)
            act.activation(vn1, psum[:, 7, :], ACT.Copy).then_inc(S("vn_read"), 1)
            act.wait_ge(S("gdn_o"), 1)
            act.activation(o_sq, banks(2), ACT.Square).then_inc(S("gdn_sq"), 1)
            act.activation(o_f, banks(2), ACT.Copy).then_inc(S("gdn_of"), 1)
            act.wait_ge(S("gdn_sums"), 1)
            act.activation(o_rn, banks(4), ACT.Sqrt, bias=eps_col, scale=1.0 / DK).then_inc(S("gdn_root"), 1)

        def gdn_dve(dve, done):
            dve.wait_ge(S("gates_raw"), 1)
            a_v = psum[:, 7, 0:16].rearrange("p (t e) -> p e t", t=NT)
            heads_v = [ap.rearrange("p (h t) -> p h t", h=HEADS) for ap in (g_s, bg_s)]
            done(dve.tensor_tensor(heads_v[0], a_v[:, 0:4, :], col("dt_bias", 0, TH).rearrange("p (h t) -> p h t", h=HEADS), ALU.add))
            done(dve.tensor_copy(heads_v[1], a_v[:, 4:8, :]))
            done(dve.tensor_scalar(e_s, g_s, -1.0, None, ALU.mult))
            done(dve.tensor_scalar(sp_s, g_s, 0.0, None, ALU.max))
            dve.tensor_tensor(e_s, e_s, g_s, ALU.max).then_inc(S("gate_in"), 1)
            dve.wait_ge(S("gate_exp"), 3)
            done(dve.tensor_scalar(bg_s, bg_s, 1.0, None, ALU.add))
            done(dve.reciprocal(beta_s, bg_s))
            dve.wait_ge(S("gate_ln"), 1)
            done(dve.tensor_tensor(sp_s, sp_s, e_s, ALU.add))
            done(dve.scalar_tensor_tensor(g_s, sp_s, -1.0, ea_s, ALU.mult, ALU.mult))
            dve.tensor_copy(th_view(g_b), bc(g_s, P)).then_inc(S("g_rows"), 1)
            dve.tensor_copy(th_view(beta_b), bc(beta_s, P)).then_inc(S("g_rows"), 1)
            dve.wait_ge(S("g_cum"), 1)
            dve.tensor_copy(gc_s, psum[:, 7, 32:32 + TH]).then_inc(S("gc"), 1)
            dve.wait_ge(S("qk_root"), 1)
            done(dve.reciprocal(rn, rn))
            done(dve.scalar_tensor_tensor(blk(3), blk(3), DK ** -0.5, rn[:, 0:1024], ALU.mult, ALU.mult))
            done(dve.tensor_tensor(blk(4), blk(4), rn[:, 1024:2048], ALU.mult))
            dve.wait_ge(S("beta_rows"), 1)
            dve.tensor_tensor(kb_t, blk(4), banks(0), ALU.mult).then_inc(S("kb"), 1)
            dve.wait_ge(S("eg"), 1)
            dve.wait_ge(S("gc"), 1)
            cum = th_view(banks(4))
            done(dve.tensor_tensor(th_view(diff), cum, bc(gc_s, P), ALU.subtract))
            last_g = banks(4).rearrange("p (h t n) -> p h t n", h=HEADS, t=NT)[:, :, 0, P - 1]
            dve.tensor_tensor(tail_s, last_g, gc_s.rearrange("p (h t) -> p h t", h=HEADS)[:, :, 0], ALU.subtract).then_inc(S("tail"), 1)
            dve.tensor_scalar(diff, diff, 0.0, None, ALU.min).then_inc(S("diff"), 1)
            dve.tensor_tensor(qd.rearrange("p (h n) -> p h n", h=HEADS), tok_view(blk(3))[:, :, P:T], tok_view(eg)[:, :, P:T], ALU.mult)
            dve.wait_ge(S("decay_exp"), 1)
            done(dve.tensor_tensor(th_view(diff), th_view(diff), rep(mat("upto"), TH), ALU.mult))
            dve.wait_ge(S("kk_qk"), 1)
            dve.tensor_tensor(n_t, banks(2), diff, ALU.mult).then_inc(S("n_qk"), 1)
            dve.wait_ge(S("kk_qk"), 2)
            dve.tensor_tensor(qk_t, banks(4), diff, ALU.mult).then_inc(S("n_qk"), 1)
            dve.wait_ge(S("egc"), 1)
            done(dve.tensor_tensor(bg_s, beta_s, egc_s, ALU.mult))
            dve.wait_ge(S("k_nat"), 1)
            dve.wait_ge(S("tail_exp"), 1)
            k_nat = banks(0).rearrange("p (h t n) -> p h t n", h=HEADS, t=NT)
            bg1 = bg_s.rearrange("p (h t) -> p h t", h=HEADS)[:, :, 1]
            dve.tensor_tensor(kbg.rearrange("p (h n) -> p h n", h=HEADS), k_nat[:, :, 1, :], bc(bg1, P), ALU.mult)
            dve.tensor_tensor(kt.rearrange("p (h n) -> p h n", h=HEADS), k_nat[:, :, 0, :], bc(tail_s, P), ALU.mult)
            dve.wait_ge(S("v_nat"), 1)
            dve.tensor_tensor(th_view(vb), th_view(banks(2)), bc(beta_s, P), ALU.mult).then_inc(S("nat_read"), 1)
            dve.tensor_copy(th_view(m_inv), rep(ident, TH))
            dve.tensor_copy(th_view(mt_inv), rep(ident, TH)).then_inc(S("inv_start"), 1)
            dve.wait_ge(S("inv_start"), 1)
            halves = [[ap[:, hf * 512:(hf + 1) * 512] for ap in (m_inv, mt_inv, p_sb)] for hf in range(2)]
            for lv in range(LEVELS):
                for hf in range(2):
                    dve.wait_ge(S("inv_p"), 2 * lv + hf + 1)
                    dve.tensor_tensor(th_view(halves[hf][2]), th_view(psum[:, hf, :]), rep(mat(f"level{lv}"), 4), ALU.mult)\
                       .then_inc(S("inv_masked"), 1)
                for hf in range(2):
                    dve.wait_ge(S("inv_q"), 2 * lv + hf + 1)
                    dve.tensor_tensor(halves[hf][0], halves[hf][0], psum[:, 2 + hf, :], ALU.subtract)
                    dve.tensor_tensor(halves[hf][1], halves[hf][1], psum[:, 4 + hf, :], ALU.subtract).then_inc(S("inv_done"), 1)
            dve.wait_ge(S("gdn_root"), 1)
            done(dve.reciprocal(o_rn, o_rn))
            dve.wait_ge(S("gdn_of"), 1)
            done(dve.tensor_tensor(o_f, o_f, o_rn, ALU.mult))
            for h in range(HEADS):
                dve.scalar_tensor_tensor(act_f[:, CS5 + h, :], tok_view(o_f)[:, h, :], col("gdn_g"), zs[:, h, :], ALU.mult, ALU.mult)\
                   .then_inc(S("act_f"), 1)

        lg = arena[:, 0:72].rearrange("p (t n) -> p t n", t=NT)
        comb = arena[:, 128:192].rearrange("p (t n) -> p t n", t=NT)
        sel4 = arena[:, 256:320].rearrange("p (t e g) -> p t e g", t=NT, e=PER_GROUP)
        gates = arena[:, 6 * 1024:14 * 1024]

        def router_pe(pe):
            pe.wait_ge(S("act_f"), 8 * 3)
            for t in range(NT):
                for k in range(KD):
                    last = pe.matmul(psum[:, 3, t * 36:(t + 1) * 36], act_f[:, k, t * P:(t + 1) * P], w_router[:, k, :],
                                     start=k == 0, stop=k == KD - 1)
            last.then_inc(S("router_raw"), 1)

        def gates_pe(pe):
            pe.wait_ge(S("combine"), 1)
            for b in range(4):
                if b:
                    pe.wait_ge(S("gates_read"), b)
                for e in range(8):
                    for t in range(NT):
                        dst = psum[:, e // 2, (e % 2) * T + t * P:(e % 2) * T + (t + 1) * P]
                        last = pe.matmul(dst, comb[:, t, 8 * b + e:8 * b + e + 1].to_broadcast([P, P]), ident, start=True, stop=True)
                last.then_inc(S("gates_raw4"), 1)

        def router_act(act):
            act.wait_ge(S("group_diff"), 1)
            act.activation(gexp, gexp, ACT.Exp).then_inc(S("group_exp"), 1)
            act.wait_ge(S("pair_diff"), 1)
            act.activation(pair_e, pair_e, ACT.Exp).then_inc(S("pair_exp"), 1)
            for b in range(4):
                act.wait_ge(S("gates_raw4"), b + 1)
                act.activation(gates[:, b * 2048:(b + 1) * 2048], banks(0, 4), ACT.Copy).then_inc(S("gates_read"), 1)

        gexp = tiny(NT * N_GROUPS)
        geq = tiny(NT * N_GROUPS)
        gmax, gden, wmax, m1, m2, pair_e, w1, w2 = (tiny(NT) for _ in range(8))
        sel, eq8, oh1, oh2 = (tiny(NT * PER_GROUP) for _ in range(4))

        def router_dve(dve, done):
            def by(ap, n):
                return ap.rearrange("p (t n) -> p t n", n=n)

            def best(src, n, mx, onehot, order):
                done(dve.reduce_max(mx, by(src, n), AX))
                done(dve.tensor_tensor(by(eq8[:, 0:NT * n], n), by(src, n), bc(mx, n), ALU.is_equal))
                done(dve.tensor_tensor(by(eq8[:, 0:NT * n], n), by(eq8[:, 0:NT * n], n), rep(order, NT), ALU.mult))
                done(dve.reduce_max(wmax, by(eq8[:, 0:NT * n], n), AX))
                done(dve.tensor_tensor(by(onehot, n), by(eq8[:, 0:NT * n], n), bc(wmax, n), ALU.is_equal))

            dve.wait_ge(S("router_raw"), 1)
            done(dve.tensor_copy(lg, psum[:, 3, 0:72].rearrange("p (t n) -> p t n", t=NT)))
            done(dve.tensor_copy(by(gexp, 4), lg[:, :, 0:4]))
            best(gexp, N_GROUPS, gmax, geq, first[:, 4:8])
            dve.tensor_tensor(by(gexp, 4), by(gexp, 4), bc(gmax, 4), ALU.subtract).then_inc(S("group_diff"), 1)
            for t in range(NT):
                ex = lg[:, t, 4:36].rearrange("p (g e) -> p e g", g=N_GROUPS)
                done(dve.tensor_tensor(sel4[:, t, :, :], ex, rep(by(geq, 4)[:, t, :], PER_GROUP), ALU.mult))
            done(dve.reduce_sum(by(sel, 8), sel4, AX))
            best(sel, PER_GROUP, m1, oh1, first[:])
            done(dve.scalar_tensor_tensor(sel, oh1, -3.0e38, sel, ALU.mult, ALU.add))
            best(sel, PER_GROUP, m2, oh2, first[:])
            dve.tensor_tensor(pair_e, m2, m1, ALU.subtract).then_inc(S("pair_diff"), 1)
            dve.wait_ge(S("group_exp"), 1)
            done(dve.reduce_sum(gden, by(gexp, 4), AX))
            done(dve.reciprocal(gden, gden))
            dve.wait_ge(S("pair_exp"), 1)
            done(dve.tensor_scalar(w1, pair_e, 1.0, None, ALU.add))
            done(dve.reciprocal(w1, w1))
            done(dve.tensor_tensor(w1, w1, gden, ALU.mult))
            done(dve.tensor_tensor(w2, w1, pair_e, ALU.mult))
            done(dve.tensor_tensor(by(oh1, 8), by(oh1, 8), bc(w1, 8), ALU.mult))
            done(dve.tensor_tensor(by(oh2, 8), by(oh2, 8), bc(w2, 8), ALU.mult))
            done(dve.tensor_tensor(oh1, oh1, oh2, ALU.add))
            for t in range(NT):
                dst = comb[:, t, :].rearrange("p (g e) -> p g e", g=N_GROUPS)
                last = dve.tensor_tensor(dst, bc(by(geq, 4)[:, t, :], PER_GROUP), rep(by(oh1, 8)[:, t, :], N_GROUPS), ALU.mult)
            last.then_inc(S("combine"), 1)
            dve.wait_ge(S("gates_read"), 4)

        def residual_dve(dve, done, s, used, part, final):
            dve.wait_ge(slab_used[s], used)
            gate = mod[:, part * D:(part + 1) * D].rearrange("p (b n) -> p b n", b=2)
            for t in range(NT):
                done(dve.tensor_tensor(xn(t).rearrange("p (b n) -> p b n", b=2), acc[:, 2 * t:2 * t + 2, :], gate, ALU.mult))
                dve.tensor_tensor(x[:, t, :], x[:, t, :], xn(t), ALU.add).then_inc(S("moe_x" if final else "x_ready"), 1)

        def final_act(act):
            for t in range(NT):
                act.wait_ge(S("moe_x"), t + 1)
                if t:
                    act.wait_ge(S("final_sums"), t)
                act.activation(junk, x[:, t, :], ACT.Square, accum_out=f_sum[:, t:t + 1]).then_inc(S("final_sums"), 1)

        def final_pool(pool):
            pool.wait_ge(S("final_sums"), NT)
            rstd(pool, f_rstd, f_sum, 1.0 / D, EPS, S("final_rstd"))

        def final_dve(dve):
            dve.wait_ge(S("row_loaded0"), 16)
            dve.wait_ge(S("final_rstd"), 1)
            for t in range(NT):
                dve.scalar_tensor_tensor(x[:, t, :], x[:, t, :], f_rstd[:, t:t + 1], rows[:, 0, :], ALU.mult, ALU.mult)\
                   .then_inc(S("x_ready"), 1)
        ATT = [l for l in range(LAYERS) if KINDS[l] != 1]
        SC = T + P
        q_a = arena[:, 0:2048].rearrange("p (c t) -> p c t", t=T)
        k_a = arena[:, 2048:4096].rearrange("p (c t) -> p c t", t=T)
        v_a = arena[:, 4096:6144].rearrange("p (t n) -> p t n", t=NT)
        bias_a = [arena[:, 6144 + i * 4 * T:6144 + (i + 1) * 4 * T].rearrange("p (h n) -> p h n", h=4) for i in range(2)]
        prob_a = [arena[:, 9216 + i * 4 * SC:9216 + (i + 1) * 4 * SC].rearrange("p (h n) -> p h n", h=4) for i in range(2)]
        pt_a = arena[:, 12288:12288 + 4 * SC]
        mx_a = [tiny(8) for _ in range(2)]
        sum_a = [tiny(8) for _ in range(2)]
        lam_p, lam_e, nlam, subg = tiny(2), tiny(2), tiny(1), tiny(1)
        o2, o2_rn = arena[:, 0:2048], arena[:, 2048:4096]

        def same_before(l):
            return KINDS[:l].count(KINDS[l])

        def n_proj(l):
            return 8 if KINDS[l] == 1 else 12

        def proj_base(l):
            return N_ADA + 10 + sum(n_proj(i) for i in range(l))

        def act_index(l, which):
            return 3 + 4 * l + which

        def qkv_act(act, l):
            name = f"mix{l}"
            for j in range(12):
                cols_used(act, name, j)
                bank = psum[:, 4 + j % 2, :].rearrange("p (m t) -> p m t", m=2)
                if j < 4:
                    act.activation(q_a[:, 2 * j:2 * j + 2, :], bank, ACT.Copy, scale=0.125).then_inc(S("proj_evac"), 1)
                elif j < 8:
                    act.activation(k_a[:, 2 * j - 8:2 * j - 6, :], bank, ACT.Copy).then_inc(S("proj_evac"), 1)
                else:
                    act.activation(v_a[:, :, (j - 8) * 256:(j - 7) * 256], bank, ACT.Copy).then_inc(S("proj_evac"), 1)
                next_hi(act, name, j, 12)
            head_act(act, f"wo{l}")

        def cols_dve(dve, l):
            name = f"mix{l}"
            for j in range(n_proj(l)):
                next_lo(dve, name, j, n_proj(l))
            head_dve(dve, f"wo{l}")

        def bias_pool(pool, l):
            n = ATT.index(l)
            pool.wait_ge(S("pre_rstd"), NT * (4 + 3 * l))
            for b in range(4):
                bt = 4 * n + b
                s = bt % 2
                if bt >= 2:
                    pool.wait_ge(S("scores"), bt - 1)
                if KINDS[l] == 2:
                    pool.dma_start(bias_a[s], a["alibi"][:, 4 * b:4 * b + 4, :]).then_inc(S(f"bias_in{s}"), 16)
                else:
                    tab = a["rel_rows"]
                    base = tab.offset + ((l // 3) * 16 + 4 * b) * 512
                    pool.dma_start(bias_a[s], bass.AP(tensor=tab.tensor, offset=base, ap=[[1, P], [512, 4], [1, T]]))\
                        .then_inc(S(f"bias_in{s}"), 16)
                    pool.wait_ge(S(f"bias_in{s}"), 16 * (bt // 2 + 1))
                    pool.memset(bias_a[s][64:P, :, 192:256], -1e30).then_inc(S("bias_ready"), 1)
            if KINDS[l] == 0:
                pool.wait_ge(S("bias_ready"), 4 * same_before(l) + 4)

        def att_pe(pe, l):
            n = ATT.index(l)
            turn = mat("ident") if KINDS[l] == 2 else mat("flip")
            pe.wait_ge(S("proj_evac"), proj_base(l) + 12)

            def scores(b):
                bt = 4 * n + b
                if KINDS[l] == 0:
                    pe.wait_ge(S("bias_ready"), 4 * same_before(l) + b + 1)
                else:
                    pe.wait_ge(S(f"bias_in{bt % 2}"), 16 * (bt // 2 + 1))
                pe.wait_ge(S("exp"), 8 * bt)
                for hh in range(4):
                    h = 4 * b + hh
                    r, c = (h % 2) * 64, h // 2
                    pe.matmul(psum[:, hh, 0:T], turn, bias_a[bt % 2][:, hh, :], start=True, stop=False)
                    pe.matmul(psum[:, hh, 0:T], q_a[r:r + 64, c, P:T], k_a[r:r + 64, c, :], start=False, stop=True)
                    pe.matmul(psum[:, hh, T:SC], turn, bias_a[bt % 2][:, hh, P:T], start=True, stop=False)
                    last = pe.matmul(psum[:, hh, T:SC], q_a[r:r + 64, c, 0:P], k_a[r:r + 64, c, 0:P], start=False, stop=True)
                last.then_inc(S("scores"), 1)

            def turned(b):
                bt = 4 * n + b
                pe.wait_ge(S("prob"), 2 * bt + 2)
                pe.wait_ge(S("pt"), bt)
                for hh in range(4):
                    for i, at0 in enumerate((T, 0, P)):
                        e = 3 * hh + i
                        last = pe.transpose(psum[:, 4 + e // 4, (e % 4) * P:(e % 4 + 1) * P], prob_a[bt % 2][:, hh, at0:at0 + P], ident)
                last.then_inc(S("pt_raw"), 1)

            def out_of(b):
                bt = 4 * n + b
                pe.wait_ge(S("pt"), bt + 1)
                if b:
                    if KINDS[l] == 0:
                        pe.wait_ge(S("act_f"), 8 * act_index(l, 2) + 2 * b)
                    else:
                        pe.wait_ge(S("att_read"), 4 * same_before(l) + b)
                for hh in range(4):
                    cc = hh // 2
                    p0, p1 = pt_a[:, hh * SC:hh * SC + T], pt_a[:, hh * SC + T:(hh + 1) * SC]
                    if KINDS[l] == 0:
                        h = 4 * b + hh
                        r = (h % 2) * 64
                        dst = psum[r:r + 64, 7, cc * T:(cc + 1) * T]
                        vs = slice(h * 64, (h + 1) * 64)
                        pe.matmul(dst, v_a[:, 0, vs], p0, start=True, stop=False)
                        last = pe.matmul(dst[:, P:T], v_a[:, 1, vs], p1, start=False, stop=True)
                    else:
                        dst = psum[:, 7, cc * T:(cc + 1) * T]
                        vs = slice((2 * b + cc) * P, (2 * b + cc + 1) * P)
                        pe.matmul(dst, v_a[:, 0, vs], p0, start=hh % 2 == 0, stop=False)
                        last = pe.matmul(dst[:, P:T], v_a[:, 1, vs], p1, start=False, stop=hh % 2 == 1)
                last.then_inc(S("att_o"), 1)

            if KINDS[l] == 2:
                pe.wait_ge(S("lam_prod"), 1)
                pe.matmul(psum[:, 7, 0:2], mat("ones"), lam_p, start=True, stop=True).then_inc(S("lam_sum"), 1)
                pe.wait_ge(S("lam_exp"), 1)
            scores(0)
            for b in range(4):
                if b < 3:
                    scores(b + 1)
                turned(b)
                out_of(b)
            if KINDS[l] == 2:
                pe.wait_ge(S("sub_sq"), 4)
                pe.wait_ge(S("exp"), 8 * (4 * n + 4))
                for h in range(8):
                    last = pe.matmul(psum[:, h // 2, (h % 2) * T:(h % 2 + 1) * T], mat("ones"), o2[:, h * T:(h + 1) * T], start=True, stop=True)
                last.then_inc(S("sub_sums"), 1)

        def att_act(act, l):
            n = ATT.index(l)
            if KINDS[l] == 2:
                act.wait_ge(S("lam_sum"), 1)
                act.activation(lam_e, psum[:, 7, 0:2], ACT.Exp).then_inc(S("lam_exp"), 1)

            def exps(b):
                bt = 4 * n + b
                act.wait_ge(S("nmax"), bt + 1)
                if bt >= 2:
                    act.wait_ge(S("pt_raw"), bt - 1)
                for i in range(2):
                    for hh in range(4):
                        cols_ = slice(0, T) if i == 0 else slice(T, SC)
                        e = 4 * i + hh
                        act.activation(prob_a[bt % 2][:, hh, cols_], psum[:, hh, cols_], ACT.Exp, bias=mx_a[bt % 2][:, e:e + 1],
                                       accum_out=sum_a[bt % 2][:, e:e + 1]).then_inc(S("exp"), 1)

            def read_out(b):
                bt = 4 * n + b
                act.wait_ge(S("att_o"), bt + 1)
                o = psum[:, 7, :].rearrange("p (c t) -> p c t", c=2)
                if KINDS[l] == 0:
                    for c in range(2):
                        act.activation(act_f[:, 2 * b + c, :], o[:, c, :], ACT.Copy).then_inc(S("act_f"), 1)
                else:
                    act.activation(act_f[:, 2 * b:2 * b + 2, :], o, ACT.Copy).then_inc(S("att_read"), 1)

            exps(0)
            for b in range(4):
                bt = 4 * n + b
                act.wait_ge(S("pt_raw"), bt + 1)
                act.wait_ge(S("att_o"), bt)
                act.activation(pt_a, banks(4, 3), ACT.Copy).then_inc(S("pt"), 1)
                if b < 3:
                    exps(b + 1)
                read_out(b)
            if KINDS[l] == 2:
                act.wait_ge(S("att_read"), 4 * same_before(l) + 4)
                for q in range(4):
                    act.activation(o2[:, q * 512:(q + 1) * 512], act_f[:, 2 * q:2 * q + 2, :].rearrange("p c t -> p (c t)"), ACT.Square)\
                       .then_inc(S("sub_sq"), 1)
                act.wait_ge(S("sub_sums"), 1)
                act.activation(o2_rn, banks(0, 4), ACT.Sqrt, bias=eps_col, scale=1.0 / P).then_inc(S("sub_root"), 1)

        def att_dve(dve, l, done):
            n = ATT.index(l)
            if KINDS[l] == 2:
                lam = col("lam_c", 0, 4).rearrange("p (a b) -> p a b", b=2)
                dve.tensor_tensor(lam_p, lam[:, :, 0], lam[:, :, 1], ALU.mult).then_inc(S("lam_prod"), 1)
                done(dve.tensor_scalar(subg, col("subln"), 1.0 - LAMBDA_INIT, None, ALU.mult))
                dve.wait_ge(S("lam_exp"), 1)
                done(dve.tensor_tensor(nlam, lam_e[:, 1:2], lam_e[:, 0:1], ALU.subtract))
                done(dve.tensor_scalar(nlam, nlam, LAMBDA_INIT, None, ALU.subtract))

            def maxes(b):
                bt = 4 * n + b
                mx = mx_a[bt % 2]
                dve.wait_ge(S("scores"), bt + 1)
                dve.reduce_max(mx[:, 0:4], psum[:, 0:4, 0:T], AX)
                done(dve.reduce_max(mx[:, 4:8], psum[:, 0:4, T:SC], AX))
                dve.tensor_scalar(mx, mx, -1.0, None, ALU.mult).then_inc(S("nmax"), 1)

            def normalise(b):
                bt = 4 * n + b
                inv, pr = sum_a[bt % 2], prob_a[bt % 2]
                dve.wait_ge(S("exp"), 8 * bt + 8)
                done(dve.reciprocal(inv, inv))
                if KINDS[l] == 2:
                    odd = inv.rearrange("p (e m) -> p e m", m=2)[:, :, 1]
                    done(dve.tensor_scalar(odd, odd, nlam, None, ALU.mult))
                dve.tensor_tensor(pr[:, :, 0:T], pr[:, :, 0:T], bc(inv[:, 0:4], T), ALU.mult).then_inc(S("prob"), 1)
                dve.tensor_tensor(pr[:, :, T:SC], pr[:, :, T:SC], bc(inv[:, 4:8], P), ALU.mult).then_inc(S("prob"), 1)

            maxes(0)
            for b in range(4):
                normalise(b)
                if b < 3:
                    maxes(b + 1)
            if KINDS[l] == 2:
                dve.wait_ge(S("sub_root"), 1)
                done(dve.reciprocal(o2_rn, o2_rn))
                for h in range(8):
                    dve.scalar_tensor_tensor(act_f[:, h, :], act_f[:, h, :], subg, o2_rn[:, h * T:(h + 1) * T], ALU.mult, ALU.mult)\
                       .then_inc(S("act_f"), 1)

        GROUPS = 8
        u_b, v_b = tok_view(arena[:, 0:2048]), arena[:, 2048:4096].rearrange("p (t n) -> p t n", t=NT)
        ws_t, ws_in = th_view(blk(4)), th_view(blk(5))
        ln_g, ln_b, bs_b, vc_sq = blk(6), blk(7), blk(8), blk(9)
        v_sum, v_var, v_rstd = tiny(NT), tiny(NT), tiny(NT)

        def gmlp_loads(pool):
            pool.dma_start(ws_in, a["b_w_s"].rearrange("g t s -> t g s")).then_inc(S("ws_in"), 16)
            for name, dst in (("b_ln_g", ln_g), ("b_ln_b", ln_b), ("b_b_s", bs_b)):
                pool.dma_start(dst, a[name].to_broadcast([P, D])).then_inc(S("b_rows"), 16)

        def gmlp_pe(pe):
            pe.wait_ge(S("ws_in"), 16)
            for g in range(GROUPS):
                last = pe.transpose(banks(0)[:, g * P:(g + 1) * P], ws_in[:, g, :], ident)
            last.then_inc(S("ws_turned"), 1)
            pe.wait_ge(S("ws_t"), 1)
            pe.wait_ge(S("v_normed"), NT)
            for g in range(GROUPS):
                for t in range(NT):
                    last = pe.matmul(psum[:, g // 2, (g % 2) * T + t * P:(g % 2) * T + (t + 1) * P],
                                     v_b[:, t, g * P:(g + 1) * P], ws_t[:, g, :], start=True, stop=True)
            last.then_inc(S("spatial"), 1)

        def gmlp_act(act, l):
            name = f"mix{l}"
            for j in range(8):
                cols_used(act, name, j)
                bank = psum[:, 4 + j % 2, :].rearrange("p (m t) -> p m t", m=2)
                dst = u_b[:, 2 * j:2 * j + 2, :] if j < 4 else v_b[:, :, (j - 4) * 256:(j - 3) * 256]
                act.activation(dst, bank, ACT.Gelu).then_inc(S("proj_evac"), 1)
                next_hi(act, name, j, 8)
            head_act(act, f"wo{l}")
            for t in range(NT):
                act.wait_ge(S("v_centred"), t + 1)
                if t:
                    act.wait_ge(S("v_sq"), t)
                act.activation(vc_sq, v_b[:, t, :], ACT.Square, accum_out=v_var[:, t:t + 1]).then_inc(S("v_sq"), 1)

        def gmlp_pool(pool):
            pool.wait_ge(S("v_sq"), NT)
            rstd(pool, v_rstd, v_var, 1.0 / D, EPS, S("v_rstd"))

        def gmlp_dve(dve, l, done):
            cols_dve(dve, l)
            dve.wait_ge(S("ws_turned"), 1)
            dve.tensor_tensor(ws_t, th_view(banks(0)), rep(mat("upto"), GROUPS), ALU.mult).then_inc(S("ws_t"), 1)
            dve.wait_ge(S("proj_evac"), proj_base(l) + 8)
            for t in range(NT):
                done(dve.reduce_sum(v_sum[:, t:t + 1], v_b[:, t, :], AX))
                done(dve.tensor_scalar(v_sum[:, t:t + 1], v_sum[:, t:t + 1], -1.0 / D, None, ALU.mult))
                dve.tensor_scalar(v_b[:, t, :], v_b[:, t, :], v_sum[:, t:t + 1], None, ALU.add).then_inc(S("v_centred"), 1)
            dve.wait_ge(S("b_rows"), 48)
            dve.wait_ge(S("v_rstd"), 1)
            for t in range(NT):
                done(dve.scalar_tensor_tensor(v_b[:, t, :], v_b[:, t, :], v_rstd[:, t:t + 1], ln_g, ALU.mult, ALU.mult))
                dve.tensor_tensor(v_b[:, t, :], v_b[:, t, :], ln_b, ALU.add).then_inc(S("v_normed"), 1)
            dve.wait_ge(S("spatial"), 1)
            for g in range(GROUPS):
                sv = psum[:, g // 2, (g % 2) * T:(g % 2 + 1) * T].rearrange("p (t n) -> p t n", t=NT)
                y = act_f[:, g, :].rearrange("p (t n) -> p t n", t=NT)
                done(dve.tensor_tensor(y, sv, rep(bs_b[:, g * P:(g + 1) * P], NT), ALU.add))
                dve.tensor_tensor(act_f[:, g, :], act_f[:, g, :], u_b[:, g, :], ALU.mult).then_inc(S("act_f"), 1)

        def ff_hb(l, which):
            return N_EXPERTS + (2 * l + which) * FF_STEPS

        def pre_cols(l, i):
            return lambda k: col("pre", (3 * l + i) * KD + k)

        def row_load(pool, r):
            if r >= 2:
                pool.wait_ge(S("x_ready"), NT * r)
            pool.dma_start(rows[:, r % 2, :], a["rows"][r:r + 1, :].to_broadcast([P, D])).then_inc(S(f"row_loaded{r % 2}"), 16)

        @block.sync
        def _(sp):
            w_ada, w_in = a["w_ada"], a["w_in"]
            load(sp, 0, 0, col_slab(w_ada, 0))
            load(sp, 1, 0, col_slab(w_ada, 256))
            with sp.Fori(1, N_ADA // 2) as i:
                for s in range(2):
                    load(sp, s, i, w_ada[:, bass.ds(i * 512 + s * 256, 256)].rearrange("(k p) n -> p k n", p=P))
            cols_load(sp, "w_in", 10, lambda j: col_slab(w_in, 256 * j))
            load(sp, GD, PLAN.base["w_glu"][GD], a["w_glu"].rearrange("(k p) n -> p k n", p=P))
            cols_load(sp, "w_out", 4, lambda j: col_slab(a["w_out"], 256 * j))

            def expert(name, p):
                def src(i):
                    w = a[name][bass.ds(i, 1), :, :] if not isinstance(i, int) else a[name][i:i + 1, :, :]
                    return w.rearrange("o (k p) n -> p (o k) n", p=p)
                return src
            ff_load(sp, "moe", N_EXPERTS, expert("w_gate", P), expert("w_up", P), expert("w_down", P))

            def ff_src(w, l, c0):
                def src(i):
                    return w[l, :, bass.ds(i * HID + c0, HID)].rearrange("(k p) n -> p k n", p=P) if not isinstance(i, int) \
                        else w[l, :, i * HID + c0:(i + 1) * HID + c0].rearrange("(k p) n -> p k n", p=P)
                return src

            def ff_row(w, l):
                def src(i):
                    r = w[l, bass.ds(i * HID, HID), :] if not isinstance(i, int) else w[l, i * HID:(i + 1) * HID, :]
                    return r.rearrange("(j p) n -> p j n", p=P)
                return src
            for l in range(LAYERS):
                for which, half_ff in (("a", "ff1"), ("b", "ff2")):
                    wi, wo = a[f"{half_ff}_w_in"], a[f"{half_ff}_w_out"]
                    ff_load(sp, f"ff{l}{which}", FF_STEPS, ff_src(wi, l, 0), ff_src(wi, l, D_FF), ff_row(wo, l))
                    if which == "a":
                        kind, m = "abc"[KINDS[l]], l // 3
                        w = a["b_w_in" if kind == "b" else f"{kind}_w_qkv"]
                        cols_load(sp, f"mix{l}", n_proj(l), lambda j: col_slab(w[m], 256 * j))
                        cols_load(sp, f"wo{l}", 4, lambda j: col_slab(a[f"{kind}_w_o"][m], 256 * j))
            for t in range(NT):
                sp.wait_ge(S("x_ready"), NT * (2 + 3 * LAYERS))
                sp.dma_start(out[t * P:(t + 1) * P, :], x[:, t, :]).then_inc(S("stored"), 16)
            sp.wait_ge(S("stored"), 32)

        @block.gpsimd
        def _(pool):
            done = steps(pool, "pool_order")
            pool.dma_start(wsmall[:, :, 0:36], a["w_router"].rearrange("(k p) n -> p k n", p=P)).then_inc(S("narrow_loaded"), 16)
            pool.dma_start(wsmall[:, :, 36:44], a["w_in"][:, 2560:2568].rearrange("(k p) n -> p k n", p=P)).then_inc(S("narrow_loaded"), 16)
            pool.dma_start(first[:], a["first"]).then_inc(S("first_loaded"), 16)
            s5_tables_pool(pool, done)
            pool.wait_ge(S("half"), 1)
            pre_pool(pool, 0)
            pre_pool(pool, 1)
            row_load(pool, 0)
            row_load(pool, 1)
            final_pool(pool)
            for l in range(LAYERS):
                pre_pool(pool, 2 + 3 * l)
                if KINDS[l] == 1:
                    gmlp_loads(pool)
                post_pool(pool, 3 * l, 0.5)
                row_load(pool, 3 * l + 2)
                pre_pool(pool, 3 + 3 * l)
                if KINDS[l] == 1:
                    gmlp_pool(pool)
                else:
                    bias_pool(pool, l)
                post_pool(pool, 3 * l + 1, 1.0)
                row_load(pool, 3 * l + 3)
                pre_pool(pool, 4 + 3 * l)
                post_pool(pool, 3 * l + 2, 0.5)
                if l < LAYERS - 1:
                    row_load(pool, 3 * l + 4)

        @block.scalar
        def _(act):
            act.dma_start(cols[:], a["cols"]).then_inc(S("cols_loaded"), 16)
            act.dma_start(mats[:].rearrange("p m n -> p (m n)"), a["mats"]).then_inc(S("mats_loaded"), 16)
            act.dma_start(x[:], a["x"].rearrange("(t p) n -> p t n", p=P)).then_inc(S("x_loaded"), 16)
            act.dma_start(mod, a["b_ada"].to_broadcast([P, 6 * D])).then_inc(S("bias_loaded"), 16)
            s5_param_act(act)
            head_act(act, "ada")
            ada_act(act)
            pre_act(act, 0)
            split_act(act, 0)
            w_in_act(act)
            s5_act(act)
            gdn_act(act)
            split_act(act, 1)
            wo_act(act, "w_out", "moe")
            pre_act(act, 1)
            split_act(act, 2)
            router_act(act)
            ff_act(act, "moe", N_EXPERTS, 0, "ff0a")
            final_act(act)
            for l in range(LAYERS):
                pre_act(act, 2 + 3 * l)
                split_act(act, act_index(l, 0))
                ff_act(act, f"ff{l}a", FF_STEPS, ff_hb(l, 0), f"mix{l}")
                post_act(act, 3 * l, GD, PLAN.base[f"ff{l}a"][GD] + FF_STEPS)
                pre_act(act, 3 + 3 * l)
                split_act(act, act_index(l, 1))
                if KINDS[l] == 1:
                    gmlp_act(act, l)
                else:
                    qkv_act(act, l)
                    att_act(act, l)
                split_act(act, act_index(l, 2))
                wo_act(act, f"wo{l}", f"ff{l}b")
                post_act(act, 3 * l + 1, 1, PLAN.base[f"wo{l}"][1] + 2)
                pre_act(act, 4 + 3 * l)
                split_act(act, act_index(l, 3))
                ff_act(act, f"ff{l}b", FF_STEPS, ff_hb(l, 1), f"ff{l + 1}a" if l < LAYERS - 1 else None)
                post_act(act, 3 * l + 2, GD, PLAN.base[f"ff{l}b"][GD] + FF_STEPS)

        @block.vector
        def _(dve):
            done = steps(dve, "dve_order")
            dve.wait_ge(S("cols_loaded"), 16)
            dve.wait_ge(S("mats_loaded"), 16)
            s5_param_dve(dve, done)
            head_dve(dve, "ada")
            ada_dve(dve)
            mod_dve(dve, done)
            dve.wait_ge(S("s5_tables"), 1)
            dve.wait_ge(S("x_loaded"), 16)
            pre_dve(dve, 0, lambda k: modc[:, 1, k:k + 1], lambda k: modc[:, 0, k:k + 1])
            pre_split_dve(dve, 0)
            w_in_dve(dve, done)
            s5_dve(dve, done)
            gdn_dve(dve, done)
            pre_split_dve(dve, 1)
            wo_dve(dve, "w_out", "moe")
            residual_dve(dve, done, 1, PLAN.base["w_out"][1] + 2, 2, False)
            pre_dve(dve, 1, lambda k: modc[:, 3, k:k + 1], lambda k: modc[:, 2, k:k + 1])
            pre_split_dve(dve, 2)
            dve.wait_ge(S("first_loaded"), 16)
            router_dve(dve, done)
            ff_dve(dve, "moe", N_EXPERTS, 0, "ff0a", gates)
            residual_dve(dve, done, GD, PLAN.base["moe"][GD] + N_EXPERTS, 5, True)
            final_dve(dve)
            for l in range(LAYERS):
                pre_dve(dve, 2 + 3 * l, pre_cols(l, 0))
                pre_split_dve(dve, act_index(l, 0))
                ff_dve(dve, f"ff{l}a", FF_STEPS, ff_hb(l, 0), f"mix{l}")
                post_dve(dve, 3 * l, 3 * l + 1)
                pre_dve(dve, 3 + 3 * l, pre_cols(l, 1))
                pre_split_dve(dve, act_index(l, 1))
                if KINDS[l] == 1:
                    gmlp_dve(dve, l, done)
                else:
                    cols_dve(dve, l)
                    att_dve(dve, l, done)
                pre_split_dve(dve, act_index(l, 2))
                wo_dve(dve, f"wo{l}", f"ff{l}b")
                post_dve(dve, 3 * l + 1, 3 * l + 2)
                pre_dve(dve, 4 + 3 * l, pre_cols(l, 2))
                pre_split_dve(dve, act_index(l, 3))
                ff_dve(dve, f"ff{l}b", FF_STEPS, ff_hb(l, 1), f"ff{l + 1}a" if l < LAYERS - 1 else None)
                post_dve(dve, 3 * l + 2, 3 * l + 3)

        @block.tensor
        def _(pe):
            pe.wait_ge(S("mats_loaded"), 16)
            ada_pe(pe)
            pre_pe(pe, 0)
            w_in_pe(pe)
            s5_pe(pe)
            gdn_pe(pe)
            wo_pe(pe, "w_out", 1)
            pre_pe(pe, 1)
            router_pe(pe)
            ff_pe(pe, "moe", N_EXPERTS, 0, 2, gates_pe)
            for l in range(LAYERS):
                pre_pe(pe, 2 + 3 * l)
                ff_pe(pe, f"ff{l}a", FF_STEPS, ff_hb(l, 0), act_index(l, 0))
                pre_pe(pe, 3 + 3 * l)
                pe.wait_ge(S("act_lo"), 4 * act_index(l, 1) + 4)
                nt = 4 if KINDS[l] == 1 else 8
                cols_pe(pe, f"mix{l}", 0, nt, "t", proj_base(l))
                cols_pe(pe, f"mix{l}", nt, nt + 4, "n", proj_base(l))
                if KINDS[l] == 1:
                    gmlp_pe(pe)
                else:
                    att_pe(pe, l)
                wo_pe(pe, f"wo{l}", act_index(l, 2))
                pre_pe(pe, 4 + 3 * l)
                ff_pe(pe, f"ff{l}b", FF_STEPS, ff_hb(l, 1), act_index(l, 3))


def kernel(**inputs):
    import concourse.bacc as bacc
    from concourse.bass_utils import run_bass_kernel_spmd

    v = {k: np.asarray(a) for k, a in inputs.items()}

    def chunks(row):
        return row.reshape(-1, P).T

    mats, alibi, first = constants()

    def states(m):
        return m.reshape(S5_TILES, P).T

    def inputs_of_state(m):
        z = np.zeros((CS5, 4, 2, 16, 2, 64), m.dtype)
        b = m.reshape(CS5, 4, 2, 64, 16)
        for g in range(2):
            z[:, :, g, :, g, :] = b[:, :, g].transpose(0, 1, 3, 2)
        return z.reshape(CS5, P, P).transpose(1, 0, 2).reshape(P, -1)

    def outputs_of_state(m):
        z = np.zeros((2, 64, S5_TILES, 2, 16), m.dtype)
        b = m.reshape(S5_TILES, 2, 16, 64)
        for g in range(2):
            z[g, :, :, g, :] = b[:, g].transpose(2, 0, 1)
        return z.reshape(P, -1)

    def over_all(row):
        return np.broadcast_to(row.reshape(1, -1), (P, row.size))

    pre = v["norm_g_2"][:, [0, 2, 4], :].reshape(-1, P).T
    lam = v["c_lambda_2"][0]
    parts = {
        "lam_re": states(v["lam_re"][0]), "lam_im": states(v["lam_im"][0]),
        "log_step": states(np.repeat(v["log_step"][0][:, None], 64, 1)),
        "s5_d": chunks(v["s5_d"][0]), "b_glu": chunks(v["b_glu"][0]),
        "conv_w": v["conv_w"][0].reshape(CONV, 12, P).transpose(2, 1, 0).reshape(P, -1),
        "norm1": chunks(v["norm1_g"][0]), "norm2": chunks(v["norm2_g"][0]), "pre": pre,
        "gdn_g": chunks(v["gdn_norm_g"][0]), "subln": chunks(v["c_subln_g_2"][0]), "c": chunks(v["c"][0]),
        "dt_bias": over_all(np.repeat(v["dt_bias"][0], NT)), "a_log": over_all(np.repeat(v["a_log"][0], NT)),
        "lam_c": np.concatenate([lam.T, np.zeros((P - lam.shape[1], 4), lam.dtype)], 0),
        "b_re": inputs_of_state(v["s5_b_re"][0]), "b_im": inputs_of_state(v["s5_b_im"][0]),
        "c_re": outputs_of_state(v["s5_c_re"][0]), "c_im": outputs_of_state(v["s5_c_im"][0]),
    }
    cols = np.zeros((P, NCOLS), np.float32)
    for name, part in parts.items():
        cols[:, COLS[name][0]:COLS[name][1]] = part
    rel = v["a_rel_bias_2"][:, :, np.clip(255 - np.arange(512), -128, 128) + 128]
    rows = np.concatenate([v["normf_g"][None], v["norm_g_2"][:, [1, 3, 5], :].reshape(-1, D)], 0)
    arrays = {
        "x": v["x"][0], "w_ada": v["w_ada"][0], "b_ada": v["b_ada"], "w_in": v["w_in"][0], "w_glu": v["w_glu"][0],
        "w_out": v["w_out"][0], "w_router": np.concatenate([v["w_router_grp"][0], v["w_router_exp"][0]], 1),
        "w_gate": v["w_gate"][0], "w_up": v["w_up"][0], "w_down": v["w_down"][0],
        "ff1_w_in": v["ff1_w_in_2"], "ff1_w_out": v["ff1_w_out_2"], "ff2_w_in": v["ff2_w_in_2"], "ff2_w_out": v["ff2_w_out_2"],
        "a_w_qkv": v["a_w_qkv_2"], "a_w_o": v["a_w_o_2"], "b_w_in": v["b_w_in_2"], "b_w_o": v["b_w_o_2"],
        "c_w_qkv": v["c_w_qkv_2"], "c_w_o": v["c_w_o_2"], "b_w_s": v["b_w_s_2"][0], "b_ln_g": v["b_ln_g_2"], "b_ln_b": v["b_ln_b_2"],
        "b_b_s": v["b_b_s_2"].reshape(1, -1), "cols": cols, "rows": rows, "rel_rows": rel.reshape(-1, 512), "mats": mats,
        "alibi": alibi, "first": first,
    }
    nc = bacc.Bacc("TRN2", target_bir_lowering=False, num_devices=1)
    args, feeds = {}, {}
    for name, arr in arrays.items():
        arr = np.ascontiguousarray(arr)
        feeds[f"in_{name}"] = arr
        args[name] = nc.dram_tensor(f"in_{name}", arr.shape, mybir.dt.from_np(arr.dtype), kind="ExternalInput").ap()
    result = nc.dram_tensor("result", (T, D), F32, kind="ExternalOutput").ap()
    build(nc, args, result)
    r = run_bass_kernel_spmd(nc, [feeds], core_ids=[0])
    return r.results[0]["result"].reshape(1, T, D)
```

```python
import math
from contextlib import ExitStack

import numpy as np

import concourse.bass as bass
from concourse import mybir

F32 = mybir.dt.float32
F32R = mybir.dt.float32r
ALU = mybir.AluOpType
ACT = mybir.ActivationFunctionType
AX = mybir.AxisListType.X

P = 128
D = 1024
T = 256
KD = D // P
NT = T // P
EPS = 1e-6
N_EXPERTS = 32
N_GROUPS = 4
PER_GROUP = 8
D_FF = 2816
HID = 256
FF_STEPS = D_FF // HID
LAYERS = 4
KINDS = [i % 3 for i in range(LAYERS)]
D_S5 = 512
CS5 = D_S5 // P
HEADS = 4
DK = 128
TH = HEADS * NT
CONV = 4
S5_TILES = 16
LEVELS = 7
LAMBDA_INIT = 0.8 - 0.6 * math.exp(-0.3 * 2)
GA, GU, GD = 0, 1, 2

COLS = {}


def _cols(spec):
    at = 0
    for name, n in spec:
        COLS[name] = (at, at + n)
        at += n
    return at


NCOLS = _cols([("lam_re", 16), ("lam_im", 16), ("log_step", 16), ("s5_d", CS5), ("b_glu", CS5),
               ("conv_w", 12 * CONV), ("norm1", KD), ("norm2", KD), ("pre", LAYERS * 3 * KD), ("gdn_g", 1),
               ("subln", 1), ("c", KD), ("dt_bias", TH), ("a_log", TH), ("lam_c", 4), ("b_ada", 4 * KD),
               ("c_re", S5_TILES * 32), ("c_im", S5_TILES * 32)])

MATS = {name: i for i, name in enumerate(["ident", "upto", "ones", "flip"] + [f"level{k}" for k in range(LEVELS)])}


def constants():
    i, j = np.arange(P)[:, None], np.arange(P)[None, :]
    mats = [i == j, i <= j, np.ones((P, P), bool), i + j == P - 1]
    for k in range(LEVELS):
        s = 1 << k
        mats.append((i // (2 * s) == j // (2 * s)) & (i // s % 2 == 1) & (j // s % 2 == 0))
    mats = np.stack(mats, 1).astype(np.float32).reshape(P, -1)
    slopes = (2.0 ** (-8.0 * (np.arange(8, dtype=np.float32) + 1.0) / 8)).astype(np.float32)
    q = np.arange(P)
    k1 = np.arange(T)
    dist = np.abs(q[:, None] + P - k1).astype(np.float32)
    barred = k1 >= ((q[:, None] + P) // 64 + 1) * 64
    alibi = np.where(barred, np.float32(-1e30), -slopes[:, None, None] * dist)
    alibi = np.repeat(alibi, 2, 0).transpose(1, 0, 2)
    first = np.tile(np.array([8, 7, 6, 5, 4, 3, 2, 1], np.float32), (P, 1))
    return mats, np.ascontiguousarray(alibi.astype(np.float32)), first


class Plan:

    def __init__(self):
        self.base = {}
        self.at = [0, 0, 0]

    def add(self, name, *counts):
        self.base[name] = tuple(self.at)
        self.at = [a + n for a, n in zip(self.at, counts)]


PLAN = Plan()
PLAN.add("w_in", 5, 5, 0)
PLAN.add("w_glu", 0, 0, 1)
PLAN.add("w_out", 2, 2, 0)
PLAN.add("moe", N_EXPERTS, N_EXPERTS, N_EXPERTS)
for _l in range(LAYERS):
    PLAN.add(f"ff{_l}a", FF_STEPS, FF_STEPS, FF_STEPS)
    PLAN.add(f"mix{_l}", *((4, 4, 0) if KINDS[_l] == 1 else (6, 6, 0)))
    PLAN.add(f"wo{_l}", 2, 2, 0)
    PLAN.add(f"ff{_l}b", FF_STEPS, FF_STEPS, FF_STEPS)


def build(nc, a, out):
    ctx = ExitStack()
    sems = {}

    def S(name):
        if name not in sems:
            sems[name] = ctx.enter_context(nc.semaphore(name))
        return sems[name]

    def sb(name, shape, dt=F32):
        return ctx.enter_context(nc.sbuf_tensor(name, shape, dt))

    with ctx:
        raw = [sb(f"raw{s}", [P, 2048]) for s in range(3)]
        whi = [sb(f"whi{s}", [P, 2048], F32R) for s in range(3)]
        wlo = [sb(f"wlo{s}", [P, 2048], F32R) for s in range(3)]
        x = sb("x", [P, NT, D])
        act_f = sb("act_f", [P, KD, T])
        act_hi = sb("act_hi", [P, KD, T], F32R)
        act_lo = sb("act_lo", [P, KD, T], F32R)
        h_hi = sb("h_hi", [P, 2, T], F32R)
        h_lo = sb("h_lo", [P, 2, T], F32R)
        tail_h_hi = sb("tail_h_hi", [P, 2, T], F32R)
        tail_h_lo = sb("tail_h_lo", [P, 2, T], F32R)
        scratch = sb("scratch", [P, 4096])
        junk = scratch[:, 0:1024]
        rows = scratch[:, 1024:3072].rearrange("p (s n) -> p s n", s=2)
        sil = scratch[:, 3072:3584]
        h_raw = scratch[:, 3584:4096]
        mats = sb("mats", [P, len(MATS), P])
        cols = sb("cols", [P, NCOLS])
        modc = sb("modc", [P, 4, KD])
        first = sb("first", [P, PER_GROUP])
        small = sb("small", [P, 512])
        half = sb("half", [P, 8])
        diag = sb("diag", [P, NT, P])
        arena = sb("arena", [P, 16384])
        psum = ctx.enter_context(nc.psum_tensor("psum", [P, 8, 512], F32))
        acc = psum[:, 0:4, :]
        gu = psum[:, 4:8, :]

        def mat(name):
            return mats[:, MATS[name], :]

        def col(name, k=0, n=1):
            at = COLS[name][0] + k
            return cols[:, at:at + n]

        def area(block, n, blocks=1):
            return arena[:, 1024 * block:1024 * block + n]

        ident = mat("ident")

        raw_loaded = [S(f"raw_loaded{s}") for s in range(3)]
        hi_ready = [S(f"hi_ready{s}") for s in range(3)]
        lo_ready = [S(f"lo_ready{s}") for s in range(3)]
        slab_used = [S(f"slab_used{s}") for s in range(3)]

        block = ctx.enter_context(nc.Block())

        def col_slab(w, c0):
            return w[:, c0:c0 + 256].rearrange("(k p) n -> p k n", p=P)

        def load(sp, s, n, src):
            if not (isinstance(n, int) and n == 0):
                sp.wait_ge(lo_ready[s], n)
            k = src.shape[1]
            sp.dma_start(raw[s][:, :k * src.shape[2]].rearrange("p (k n) -> p k n", k=k), src).then_inc(raw_loaded[s], 16)

        def split_hi(act, s, n):
            act.wait_ge(raw_loaded[s], n * 16 + 16)
            if not (isinstance(n, int) and n == 0):
                act.wait_ge(slab_used[s], n)
            act.activation(whi[s][:], raw[s][:], ACT.Copy).then_inc(hi_ready[s], 1)

        def split_lo(dve, s, n):
            dve.wait_ge(hi_ready[s], n + 1)
            dve.tensor_tensor(wlo[s][:], raw[s][:], whi[s][:].bitcast(F32), ALU.subtract).then_inc(lo_ready[s], 1)

        def slab_views(s, k):
            return (whi[s][:].rearrange("p (k n) -> p k n", k=k), wlo[s][:].rearrange("p (k n) -> p k n", k=k))

        def three(pe, out_ap, lhs, rhs, first, last):
            pe.matmul(out_ap, lhs[0], rhs[0], start=first, stop=False)
            pe.matmul(out_ap, lhs[0], rhs[1], start=False, stop=False)
            return pe.matmul(out_ap, lhs[1], rhs[0], start=False, stop=last)

        def proj_t(pe, s, bank, act_k=KD, m0=0, ms=2, k_cols=256, act_all=None):
            hi, lo = slab_views(s, 2048 // k_cols)
            for m in range(ms):
                for k in range(act_k):
                    if act_all and m == 0 and k == 4:
                        pe.wait_ge(S("act_lo"), act_all)
                    c = (m0 + m) * P
                    last = three(pe, psum[:, bank, m * T:(m + 1) * T], (hi[:, k, c:c + P], lo[:, k, c:c + P]),
                                 (act_hi[:, k, :], act_lo[:, k, :]), k == 0, k == act_k - 1)
            return last

        def proj_n(pe, s, out_of, first_done=None):
            hi, lo = slab_views(s, KD)
            for t in range(NT):
                for k in range(KD):
                    last = three(pe, out_of(t), (act_hi[:, k, t * P:(t + 1) * P], act_lo[:, k, t * P:(t + 1) * P]),
                                 (hi[:, k, :], lo[:, k, :]), k == 0, k == KD - 1)
                if first_done and t == 0:
                    last.then_inc(first_done, 1)
            return last

        ss_pre, ss_post = small[:, 0:2 * NT], small[:, 16:16 + 2 * NT]
        r_pre, r_post = small[:, 8:8 + NT], small[:, 24:24 + NT]
        HALF = D // 2

        def pre_act(act, n):
            for t in range(NT):
                for h in range(2):
                    if n == 0:
                        act.wait_ge(S("x_loaded"), 16)
                    elif n <= 2:
                        act.wait_ge(S("x_ready"), NT * (n - 1) + t + 1)
                    else:
                        act.wait_ge(S("x_half"), 2 * NT * (n - 3) + 2 * t + h + 1)
                    if n:
                        act.wait_ge(S("pre_rstd"), NT * (n - 1) + t + 1)
                    if t:
                        act.wait_ge(S("pre_sums"), 2 * NT * n + h + 1)
                    elif n == 1:
                        act.wait_ge(S("pre_sums"), 2 * NT)
                    elif n == 2:
                        act.wait_ge(S("final_sums"), NT)
                    elif n > 2:
                        act.wait_ge(S("post_sums"), 2 * NT * (n - 2))
                    act.activation(junk[:, h * HALF:(h + 1) * HALF], x[:, t, h * HALF:(h + 1) * HALF], ACT.Square,
                                   scale=D ** -0.5, accum_out=ss_pre[:, 2 * t + h:2 * t + h + 1]).then_inc(S("pre_sums"), 1)

        pool_steps = [0]

        def power(pool, out_ap, ins, sem):
            ins.then_inc(S("pool_step"), 1)
            pool_steps[0] += 1
            pool.wait_ge(S("pool_step"), pool_steps[0])
            pool.tensor_tensor(out_ap, out_ap, half[:, 0:out_ap.shape[1]], ALU.pow).then_inc(sem, 1)

        def rstd(pool, out_ap, in_ap, scale, eps, sem):
            power(pool, out_ap, pool.tensor_scalar(out_ap, in_ap, scale, eps, ALU.mult, ALU.add), sem)

        def rstd_of_halves(pool, out_ap, means, eps, sem):
            power(pool, out_ap, pool.tensor_scalar(out_ap, means[:, 0:1], means[:, 1:2], eps, ALU.add, ALU.add), sem)

        def pre_pool(pool, n):
            for t in range(NT):
                pool.wait_ge(S("pre_sums"), 2 * NT * n + 2 * t + 2)
                if n:
                    pool.wait_ge(S("diag"), NT * (n - 1) + t + 1)
                rstd_of_halves(pool, r_pre[:, t:t + 1], ss_pre[:, 2 * t:2 * t + 2], EPS, S("pre_rstd"))

        def pre_pe(pe, n):
            for t in range(NT):
                pe.wait_ge(S("diag"), NT * n + t + 1)
                for k in range(KD):
                    last = pe.matmul(gu[:, 2 * t + k // 4, (k % 4) * P:(k % 4 + 1) * P], x[:, t, k * P:(k + 1) * P], diag[:, t, :],
                                     start=True, stop=True)
                    if k % 4 == 3:
                        last.then_inc(S("transposed"), 1)

        def act_quarter(ap, t, b):
            return ap[:, 4 * b:4 * b + 4, t * P:(t + 1) * P]

        def pre_diag_dve(dve, n):
            for t in range(NT):
                dve.wait_ge(S("pre_rstd"), NT * n + t + 1)
                if n:
                    dve.wait_ge(S("transposed"), 2 * NT * n)
                dve.tensor_scalar(diag[:, t, :], ident, r_pre[:, t:t + 1], None, ALU.mult).then_inc(S("diag"), 1)

        def pre_dve(dve, n, n_act, scales, shifts=None):
            quarters = [(t, b) for t in range(NT) for b in range(2)]
            if shifts:
                for q, (t, b) in enumerate(quarters):
                    dve.wait_ge(S("transposed"), 2 * NT * n + q + 1)
                    for c in range(4):
                        k = 4 * b + c
                        last = dve.tensor_scalar(act_f[:, k, t * P:(t + 1) * P], gu[:, q, c * P:(c + 1) * P], scales(k), shifts(k),
                                                 ALU.mult, ALU.add)
                    last.then_inc(S("act_f"), 2)
            for q, (t, b) in enumerate(quarters):
                dve.wait_ge(S("act_hi"), 4 * n_act + q + 1)
                if shifts:
                    dve.tensor_tensor(act_quarter(act_lo, t, b), act_quarter(act_f, t, b), act_quarter(act_hi, t, b).bitcast(F32),
                                      ALU.subtract).then_inc(S("act_lo"), 1)
                else:
                    for c in range(4):
                        k, ts = 4 * b + c, slice(t * P, (t + 1) * P)
                        last = dve.scalar_tensor_tensor(act_lo[:, k, ts], gu[:, q, c * P:(c + 1) * P], scales(k),
                                                        act_hi[:, k, ts].bitcast(F32), ALU.mult, ALU.subtract)
                    last.then_inc(S("act_lo"), 1)

        def pre_hi_act(act, n, n_act, scales=None, n_f=None):
            for t in range(NT):
                for b in range(2):
                    q = 2 * t + b
                    if scales is None:
                        act.wait_ge(S("act_f"), 8 * n_f + 2 * q + 2)
                        act.activation(act_quarter(act_hi, t, b), act_quarter(act_f, t, b), ACT.Copy).then_inc(S("act_hi"), 1)
                    else:
                        act.wait_ge(S("transposed"), 2 * NT * n + q + 1)
                        for c in range(4):
                            k = 4 * b + c
                            last = act.activation(act_hi[:, k, t * P:(t + 1) * P], gu[:, q, c * P:(c + 1) * P], ACT.Copy, scale=scales(k))
                        last.then_inc(S("act_hi"), 1)

        def split_dve(dve, n_act):
            for q in range(4):
                dve.wait_ge(S("act_hi"), 4 * n_act + q + 1)
                dve.tensor_tensor(act_lo[:, 2 * q:2 * q + 2, :], act_f[:, 2 * q:2 * q + 2, :],
                                  act_hi[:, 2 * q:2 * q + 2, :].bitcast(F32), ALU.subtract).then_inc(S("act_lo"), 1)

        def split_act(act, n_act, n_f):
            for q in range(4):
                act.wait_ge(S("act_f"), 8 * n_f + 2 * q + 2)
                act.activation(act_hi[:, 2 * q:2 * q + 2, :], act_f[:, 2 * q:2 * q + 2, :], ACT.Copy)\
                   .then_inc(S("act_hi"), 1)

        def xn(t):
            return arena[:, 14336 + t * D:14336 + (t + 1) * D]

        def steps(eng, name):
            count = [0]

            def done(ins):
                ins.then_inc(S(name), 1)
                count[0] += 1
                eng.wait_ge(S(name), count[0])
            return done

        def bc(ap, n):
            return ap.unsqueeze(2).to_broadcast([P, ap.shape[1], n])

        def rep(ap, m):
            return ap.unsqueeze(1).to_broadcast([P, m, ap.shape[1]])

        def y_before(n):
            return 8 * (n // 3) + (0, 3, 5)[n % 3]

        def y_wait(eng, n, t, h):
            l, part = divmod(n, 3)
            if part == 1:
                if t:
                    eng.wait_ge(slab_used[1], PLAN.base[f"wo{l}"][1] + h + 1)
                else:
                    eng.wait_ge(S("y_ready"), y_before(n) + h + 1)
            elif t and h:
                eng.wait_ge(slab_used[GD], PLAN.base[f"ff{l}{'ab'[part // 2]}"][GD] + FF_STEPS)
            else:
                eng.wait_ge(S("y_ready"), y_before(n) + 2 * t + h + 1)

        def post_act(act, n, f):
            for t in range(NT):
                for h in range(2):
                    y_wait(act, n, t, h)
                    if n:
                        act.wait_ge(S("post_rstd"), NT * (n - 1) + t + 1)
                    if t:
                        act.wait_ge(S("post_sums"), 2 * NT * n + h + 1)
                    else:
                        act.wait_ge(S("pre_sums"), 2 * NT * (n + 3))
                    act.activation(junk[:, h * HALF:(h + 1) * HALF], acc[:, 2 * t + h, :], ACT.Square, scale=D ** -0.5 / f,
                                   accum_out=ss_post[:, 2 * t + h:2 * t + h + 1]).then_inc(S("post_sums"), 1)

        def post_pool(pool, n, f):
            for t in range(NT):
                pool.wait_ge(S("post_sums"), 2 * NT * n + 2 * t + 2)
                if n:
                    pool.wait_ge(S("x_half"), 2 * NT * (n - 1) + 2 * t + 2)
                rstd_of_halves(pool, r_post[:, t:t + 1], ss_post[:, 2 * t:2 * t + 2], EPS / (f * f), S("post_rstd"))

        def post_dve(dve, n, row):
            dve.wait_ge(S(f"row_loaded{row % 2}"), 16 * (row // 2 + 1))
            g = rows[:, row % 2, :].rearrange("p (b n) -> p b n", b=2)
            for t in range(NT):
                dve.wait_ge(S("post_sums"), 2 * NT * n + 2 * t + 2)
                if n:
                    dve.wait_ge(S("x_half"), 2 * NT * n)
                dve.tensor_tensor(xn(t).rearrange("p (b n) -> p b n", b=2), acc[:, 2 * t:2 * t + 2, :], g, ALU.mult).then_inc(S("y_gained"), 1)
                dve.wait_ge(S("y_gained"), NT * n + t + 1)
                dve.wait_ge(S("post_rstd"), NT * n + t + 1)
                for h in range(2):
                    hs = slice(h * HALF, (h + 1) * HALF)
                    dve.scalar_tensor_tensor(x[:, t, hs], xn(t)[:, hs], r_post[:, t:t + 1], x[:, t, hs], ALU.mult, ALU.add)\
                       .then_inc(S("x_half"), 1)

        gate_bank = psum[:, 6, 0:T]
        lg = arena[:, 0:72].rearrange("p (t n) -> p t n", t=NT)
        comb = arena[:, 128:192].rearrange("p (t n) -> p t n", t=NT)
        sel4 = arena[:, 256:320].rearrange("p (t e g) -> p t e g", t=NT, e=PER_GROUP)
        tail_hi, tail_lo = (ap[:].rearrange("p k t -> p (k t)") for ap in (act_hi, act_lo))

        def ff_load(sp, name, n, g_src, u_src, d_src, nxt):
            b = PLAN.base[name]
            with sp.Fori(1, n) as i:
                load(sp, GA, i + b[GA], g_src(i))
                load(sp, GU, i + b[GU], u_src(i))
                load(sp, GD, i + (b[GD] - 1), d_src(i - 1))
            nxt()
            load(sp, GD, b[GD] + n - 1, d_src(n - 1))

        def step_banks(i, gates):
            return (6, 7) if gates is None and isinstance(i, int) and i == 0 else (4, 5)

        def silu_step(act, b, hb, i, gates=None):
            act.wait_ge(slab_used[GU], i + (b[GU] + 1))
            act.wait_ge(S("h_raw"), i + hb)
            act.activation(sil, psum[:, step_banks(i, gates)[0], :], ACT.Silu).then_inc(S("sil"), 1)

        def h_hi_step(act, b, hb, i):
            act.wait_ge(S("h_raw"), i + (hb + 1))
            act.wait_ge(slab_used[GD], i + b[GD])
            act.activation(h_hi[:].rearrange("p m t -> p (m t)"), h_raw, ACT.Copy).then_inc(S("h_hi"), 1)

        def ff_act(act, name, n, hb, nxt, gates=None):
            b = PLAN.base[name]

            def step(i):
                split_hi(act, GA, i + b[GA])
                silu_step(act, b, hb, i - 1, gates)
                split_hi(act, GU, i + b[GU])
                h_hi_step(act, b, hb, i - 1)
                split_hi(act, GD, i + (b[GD] - 1))
            step(1)
            with act.Fori(2, n) as i:
                step(i)
            head_act(act, nxt, 0)
            silu_step(act, b, hb, n - 1, gates)
            act.wait_ge(raw_loaded[GD], 16 * (b[GD] + n))
            act.activation(tail_hi, raw[GD][:], ACT.Copy).then_inc(hi_ready[GD], 1)
            act.wait_ge(S("h_raw"), hb + n)
            act.activation(tail_h_hi[:].rearrange("p m t -> p (m t)"), h_raw, ACT.Copy).then_inc(S("h_hi"), 1)
            head_act(act, nxt, 1)

        def gate_diag(dve, w):
            dve.tensor_tensor(diag[:], rep(ident, NT), w.to_broadcast([P, NT, P]), ALU.mult).then_inc(S("gate_diag"), 1)

        def h_step(dve, b, hb, i, gates):
            dve.wait_ge(S("sil"), i + (hb + 1))
            dve.wait_ge(S("h_lo"), i + hb)
            if gates is None:
                dve.tensor_tensor(h_raw, sil, psum[:, step_banks(i, gates)[1], :], ALU.mult).then_inc(S("h_raw"), 1)
            else:
                dve.tensor_tensor(h_raw, sil, psum[:, step_banks(i, gates)[1], :], ALU.mult).then_inc(S("h_ungated"), 1)
                dve.wait_ge(S("h_ungated"), i + 1)
                v = h_raw.rearrange("p (m t) -> p m t", m=2)
                dve.wait_ge(S("gate_row"), i + 1)
                dve.tensor_tensor(v, v, rep(gates, 2), ALU.mult).then_inc(S("h_raw"), 1)
                if not (isinstance(i, int) and i == N_EXPERTS - 1):
                    gate_diag(dve, comb[:, :, bass.ds(i + 1, 1)])

        def h_lo_step(dve, b, hb, i):
            dve.wait_ge(S("h_hi"), i + (hb + 1))
            dve.tensor_tensor(h_lo[:].rearrange("p m t -> p (m t)"), h_raw,
                              h_hi[:].rearrange("p m t -> p (m t)").bitcast(F32), ALU.subtract).then_inc(S("h_lo"), 1)

        def ff_dve(dve, name, n, hb, nxt, gates=None):
            b = PLAN.base[name]

            def step(i):
                split_lo(dve, GA, i + b[GA])
                h_step(dve, b, hb, i - 1, gates)
                split_lo(dve, GU, i + b[GU])
                h_lo_step(dve, b, hb, i - 1)
                split_lo(dve, GD, i + (b[GD] - 1))
            step(1)
            with dve.Fori(2, n) as i:
                step(i)
            head_dve(dve, nxt, 0)
            h_step(dve, b, hb, n - 1, gates)
            dve.wait_ge(hi_ready[GD], b[GD] + n)
            dve.tensor_tensor(tail_lo, raw[GD][:], tail_hi.bitcast(F32), ALU.subtract).then_inc(lo_ready[GD], 1)
            dve.wait_ge(S("h_hi"), hb + n)
            dve.tensor_tensor(tail_h_lo[:].rearrange("p m t -> p (m t)"), h_raw,
                              tail_h_hi[:].rearrange("p m t -> p (m t)").bitcast(F32), ALU.subtract).then_inc(S("h_lo"), 1)
            head_dve(dve, nxt, 1)

        def ff_up(pe, b, hb, i, gate, act_all=None):
            pe.wait_ge(lo_ready[GA], i + (b[GA] + 1))
            g, u = step_banks(i, gate)
            if not isinstance(i, int) or i >= (1 if gate else 2):
                pe.wait_ge(S("h_raw"), i + hb)
            proj_t(pe, GA, g, act_all=act_all).then_inc(slab_used[GA], 1)
            pe.wait_ge(lo_ready[GU], i + (b[GU] + 1))
            proj_t(pe, GU, u).then_inc(slab_used[GU], 1)
            if gate:
                gate(pe, i)

        def ff_down(pe, b, hb, i, first, last, n_post=None):
            pe.wait_ge(S("h_lo"), i + (hb + 1))
            pe.wait_ge(lo_ready[GD], i + (b[GD] + 1))
            hi, lo = slab_views(GD, 2)
            hh, hl = h_hi, h_lo
            if last:
                hh, hl = tail_h_hi, tail_h_lo
                hi, lo = (w.rearrange("p (k n) -> p k n", k=2) for w in (tail_hi, tail_lo))
            for t in range(NT):
                ts = slice(t * P, (t + 1) * P)
                for n in range(2):
                    ns = slice(n * 512, (n + 1) * 512)
                    for j in range(2):
                        ins = three(pe, acc[:, 2 * t + n, :], (hh[:, j, ts], hl[:, j, ts]),
                                    (hi[:, j, ns], lo[:, j, ns]), first and j == 0, last and j == 1)
                    if n_post is not None and not (t and n):
                        ins.then_inc(S("y_ready"), 1)
            ins.then_inc(slab_used[GD], 1)

        def ff_pe(pe, name, n, hb, n_act, n_post=None, gate=None):
            b = PLAN.base[name]
            pe.wait_ge(S("act_lo"), 4 * n_act + 3)
            ff_up(pe, b, hb, 0, gate, 4 * n_act + 4)
            ff_up(pe, b, hb, 1, gate)
            ff_down(pe, b, hb, 0, True, False)
            with pe.Fori(2, n) as i:
                ff_up(pe, b, hb, i, gate)
                ff_down(pe, b, hb, i - 1, False, False)
            ff_down(pe, b, hb, n - 1, False, True, n_post)

        def slab_at(name, j):
            return j % 2, PLAN.base[name][j % 2] + j // 2

        def head_act(act, name, *which):
            for j in which or range(2):
                if name:
                    split_hi(act, *slab_at(name, j))

        def head_dve(dve, name, *which):
            for j in which or range(2):
                if name:
                    split_lo(dve, *slab_at(name, j))

        def next_hi(act, name, j, n):
            if j + 2 < n:
                split_hi(act, *slab_at(name, j + 2))

        def next_lo(dve, name, j, n):
            if j + 2 < n:
                split_lo(dve, *slab_at(name, j + 2))

        def cols_load(sp, name, src, *which):
            for j in which:
                load(sp, *slab_at(name, j), src(j))

        def cols_used(eng, name, j):
            s, n = slab_at(name, j)
            eng.wait_ge(slab_used[s], n + 1)

        def cols_pe(pe, name, n0, n1, kind, evac0, act0=None):
            def one(i, s, act_all=None):
                pe.wait_ge(lo_ready[s], i + (PLAN.base[name][s] + 1))
                pe.wait_ge(S("proj_evac"), i * 2 + (evac0 + s - 1))
                if kind == "t":
                    last = proj_t(pe, s, 4 + s, act_all=act_all)
                else:
                    last = proj_n(pe, s, lambda t: psum[:, 4 + s, t * T:(t + 1) * T])
                last.then_inc(slab_used[s], 1)
            first = n0 // 2
            if act0 is not None:
                pe.wait_ge(S("act_lo"), act0 + 3)
                one(first, 0, act0 + 4)
                one(first, 1)
                first += 1
            with pe.Fori(first, n1 // 2) as i:
                one(i, 0)
                one(i, 1)

        def wo_pe(pe, name, n_act, post=False):
            pe.wait_ge(S("act_lo"), 4 * n_act + 4)
            for j in range(4):
                s, n = slab_at(name, j)
                pe.wait_ge(lo_ready[s], n + 1)
                proj_n(pe, s, lambda t: acc[:, 2 * t + j // 2, (j % 2) * T:(j % 2 + 1) * T], S("y_ready") if post and j % 2 else None)\
                    .then_inc(slab_used[s], 1)

        def wo_act(act, name, nxt):
            act.activation(warm, warm, ACT.Silu)
            for j in range(4):
                next_hi(act, name, j, 4)
            head_act(act, nxt, 0)

        def wo_dve(dve, name, nxt):
            for j in range(4):
                next_lo(dve, name, j, 4)
            head_dve(dve, nxt, 0)
        at = [64]

        def tiny(n):
            at[0] += n
            return small[:, at[0] - n:at[0]]

        eps_col, one_col, warm = tiny(1), tiny(1), tiny(1)
        c_act = tiny(KD)
        step_s, lr_s, rad_s, th_s, k_s, red_s, sin_s, cos_s, den_s, ca_s, cb_s, tmp_s = (tiny(16) for _ in range(12))
        turn_w = small[:, at[0]:at[0] + 32]
        g_s, beta_s, sp_s, e_s, gc_s, egc_s, bg_s, ea_s = (tiny(TH) for _ in range(8))
        tail_s = tiny(HEADS)
        f_sum, f_rstd = tiny(NT), tiny(NT)
        wsmall = sb("wsmall", [P, KD, 44])
        w_router, w_ab = wsmall[:, :, 0:36], wsmall[:, :, 36:44]

        N_ADA, ADA_FIRST = 6 * D // 256, 2 * D // 256
        mod = arena[:, 0:6 * D]
        ada_tiles = [raw[0][:], raw[1][:], raw[2][:], act_f[:].rearrange("p k t -> p (k t)"), scratch[:, 2048:4096],
                     arena[:, 0:2048], arena[:, 3072:5120]]
        ADA_RING = (2, 0, 1)

        def ada_place(j):
            if j < ADA_FIRST:
                return (j, 1) if j < 7 else (2, 2)
            turn, i = divmod(j - ADA_FIRST, 3)
            return ADA_RING[i], turn + (3 if i == 0 else 2)

        def ada_load(sp, j):
            b, _ = ada_place(j)
            if j == 7:
                sp.wait_ge(S("ada_used"), 3)
            elif j >= ADA_FIRST + 3:
                sp.wait_ge(S("ada_used"), j - 2)
            elif j >= ADA_FIRST:
                sp.wait_ge(lo_ready[b], PLAN.base["w_out" if b < GD else "moe"][b])
            sp.dma_start(ada_tiles[b].rearrange("p (k n) -> p k n", k=KD), col_slab(a["w_ada"], 256 * j)).then_inc(S(f"ada_loaded{b}"), 16)

        def ada_bank(j):
            return psum[:, 4 + j % 2 if j < ADA_FIRST else 6, 0:256]

        def ada_pe(pe, j):
            b, uses = ada_place(j)
            pe.wait_ge(S(f"ada_loaded{b}"), 16 * uses)
            if 2 <= j < ADA_FIRST:
                pe.wait_ge(S("proj_evac"), j - 1)
            elif j > ADA_FIRST:
                pe.wait_ge(S("ada_evac"), j - ADA_FIRST)
            slab = ada_tiles[b].rearrange("p (k n) -> p k n", k=KD)
            for k in range(KD):
                last = pe.matmul(ada_bank(j), c_act[:, k:k + 1].to_broadcast([P, P]), slab[:, k, :], start=k == 0, stop=k == KD - 1)
            last.then_inc(S("ada_used"), 1)

        def ada_dve(dve, done, j):
            dve.wait_ge(S("ada_used"), j + 1)
            sem = S("proj_evac" if j < ADA_FIRST else "ada_evac")
            part, c = divmod(j, D // 256)
            if part in (2, 5):
                dve.wait_ge(S("bias_loaded"), 32)
                row = mod[:, j * 256:(j + 1) * 256]
                dve.tensor_tensor(row, row, ada_bank(j), ALU.add).then_inc(sem, 1)
            else:
                dve.tensor_tensor(diag[:], ada_bank(j).rearrange("p (k n) -> p k n", k=2), rep(ident, 2), ALU.mult).then_inc(sem, 1)
                dve.wait_ge(sem, j + 1 if j < ADA_FIRST else j - ADA_FIRST + 1)
                done(dve.reduce_sum(modc[:, (0, 1, None, 2, 3)[part], 2 * c:2 * c + 2], diag[:], AX))

        def mod_dve(dve, done, shift, norm):
            for q in (shift, shift + 1):
                done(dve.tensor_tensor(modc[:, q, :], modc[:, q, :], col("b_ada", q * KD, KD), ALU.add))
            done(dve.scalar_tensor_tensor(modc[:, shift + 1, :], modc[:, shift + 1, :], 1.0, col(norm, 0, KD), ALU.add, ALU.mult))

        e_re = arena[:, 6 * 1024:10 * 1024].rearrange("p (j t) -> p j t", j=S5_TILES)
        e_im = arena[:, 10 * 1024:14 * 1024].rearrange("p (j t) -> p j t", j=S5_TILES)
        cx_re = col("c_re", 0, 512).rearrange("p (j h) -> p j h", j=S5_TILES)
        cx_nim = col("c_im", 0, 512).rearrange("p (j h) -> p j h", j=S5_TILES)
        TWO_PI = 2 * math.pi
        C1 = 6.28125

        def s5_param_act(act):
            act.wait_ge(S("cols_loaded"), 16)
            act.activation(c_act, col("c", 0, KD), ACT.Silu).then_inc(S("c_act"), 1)
            act.activation(step_s, col("log_step", 0, 16), ACT.Exp).then_inc(S("s5_step"), 1)
            act.wait_ge(S("s5_lr"), 1)
            act.activation(rad_s, lr_s, ACT.Exp).then_inc(S("s5_rad"), 1)
            act.wait_ge(S("s5_angle"), 1)
            act.activation(sin_s, red_s, ACT.Sin).then_inc(S("s5_turn"), 1)
            act.activation(cos_s, k_s, ACT.Sin).then_inc(S("s5_turn"), 1)

        def s5_param_dve(dve, done):
            dve.memset(eps_col, EPS)
            dve.memset(one_col, 1.0)
            dve.memset(warm, 0.0)
            dve.memset(half[:], -0.5).then_inc(S("half"), 1)
            dve.wait_ge(S("s5_step"), 1)
            dve.tensor_tensor(lr_s, col("lam_re", 0, 16), step_s, ALU.mult).then_inc(S("s5_lr"), 1)
            done(dve.tensor_tensor(th_s, col("lam_im", 0, 16), step_s, ALU.mult))
            done(dve.tensor_scalar(k_s, th_s, 1 / TWO_PI, 12582912.0, ALU.mult, ALU.add))
            done(dve.tensor_scalar(k_s, k_s, 12582912.0, None, ALU.subtract))
            done(dve.scalar_tensor_tensor(red_s, k_s, -C1, th_s, ALU.mult, ALU.add))
            done(dve.scalar_tensor_tensor(red_s, k_s, -(TWO_PI - C1), red_s, ALU.mult, ALU.add))
            done(dve.tensor_scalar(red_s, red_s, 3.1415925, -3.1415925, ALU.min, ALU.max))
            done(dve.tensor_scalar(k_s, red_s, -1.0, None, ALU.mult))
            done(dve.tensor_tensor(k_s, k_s, red_s, ALU.max))
            dve.tensor_scalar(k_s, k_s, -1.0, math.pi / 2, ALU.mult, ALU.add).then_inc(S("s5_angle"), 1)
            dve.wait_ge(S("s5_turn"), 2)
            dve.wait_ge(S("s5_rad"), 1)
            lre, lim = col("lam_re", 0, 16), col("lam_im", 0, 16)
            done(dve.tensor_tensor(ca_s, rad_s, cos_s, ALU.mult))
            done(dve.tensor_scalar(ca_s, ca_s, 1.0, None, ALU.subtract))
            done(dve.tensor_tensor(cb_s, rad_s, sin_s, ALU.mult))
            done(dve.tensor_tensor(den_s, lre, lre, ALU.mult))
            done(dve.tensor_tensor(tmp_s, lim, lim, ALU.mult))
            done(dve.tensor_tensor(den_s, den_s, tmp_s, ALU.add))
            done(dve.reciprocal(den_s, den_s))
            done(dve.tensor_tensor(tmp_s, ca_s, lre, ALU.mult))
            done(dve.tensor_tensor(k_s, cb_s, lim, ALU.mult))
            done(dve.tensor_tensor(k_s, k_s, tmp_s, ALU.add))
            done(dve.tensor_tensor(tmp_s, cb_s, lre, ALU.mult))
            done(dve.tensor_tensor(cb_s, ca_s, lim, ALU.mult))
            done(dve.tensor_tensor(cb_s, tmp_s, cb_s, ALU.subtract))
            done(dve.tensor_tensor(cb_s, cb_s, den_s, ALU.mult))
            dve.tensor_tensor(ca_s, k_s, den_s, ALU.mult).then_inc(S("s5_coef"), 1)

        def s5_tables_pool(pool, done):
            pool.wait_ge(S("s5_turn"), 2)
            wr, wi = turn_w[:, 0:16], turn_w[:, 16:32]
            w2, w3 = lr_s, th_s
            pool.memset(e_re[:, :, 0:1], 1.0)
            pool.memset(e_im[:, :, 0:1], 0.0)
            pool.tensor_copy(wr, cos_s)
            done(pool.tensor_copy(wi, sin_s))
            for d in (1, 2, 4, 8, 16, 32, 64, 128):
                for at0 in range(0, d, 64):
                    n = min(d, 64)
                    m1 = arena[:, 14336:14336 + 16 * n].rearrange("p (j t) -> p j t", j=16)
                    m2 = arena[:, 15360:15360 + 16 * n].rearrange("p (j t) -> p j t", j=16)
                    src, dst = slice(at0, at0 + n), slice(d + at0, d + at0 + n)
                    pool.tensor_tensor(m1, e_re[:, :, src], bc(wr, n), ALU.mult)
                    done(pool.tensor_tensor(m2, e_im[:, :, src], bc(wi, n), ALU.mult))
                    done(pool.tensor_tensor(e_re[:, :, dst], m1, m2, ALU.subtract))
                    pool.tensor_tensor(m1, e_re[:, :, src], bc(wi, n), ALU.mult)
                    done(pool.tensor_tensor(m2, e_im[:, :, src], bc(wr, n), ALU.mult))
                    done(pool.tensor_tensor(e_im[:, :, dst], m1, m2, ALU.add))
                pool.tensor_tensor(w2, wr, wr, ALU.mult)
                done(pool.tensor_tensor(w3, wi, wi, ALU.mult))
                done(pool.tensor_tensor(w2, w2, w3, ALU.subtract))
                done(pool.tensor_tensor(w3, wr, wi, ALU.mult))
                pool.tensor_tensor(wi, w3, w3, ALU.add)
                done(pool.tensor_copy(wr, w2))
            pool.wait_ge(S("s5_coef"), 1)
            m1 = arena[:, 14336:14336 + 512].rearrange("p (j t) -> p j t", j=16)
            m2 = arena[:, 14848:14848 + 512].rearrange("p (j t) -> p j t", j=16)
            pool.tensor_tensor(m1, cx_re, bc(cb_s, 32), ALU.mult)
            done(pool.tensor_tensor(m2, cx_nim, bc(cb_s, 32), ALU.mult))
            done(pool.tensor_tensor(cx_re, cx_re, bc(ca_s, 32), ALU.mult))
            done(pool.tensor_tensor(cx_re, cx_re, m2, ALU.subtract))
            done(pool.tensor_tensor(cx_nim, cx_nim, bc(ca_s, 32), ALU.mult))
            done(pool.tensor_tensor(cx_nim, cx_nim, m1, ALU.add))
            pool.tensor_scalar(cx_nim, cx_nim, -1.0, None, ALU.mult).then_inc(S("s5_tables"), 1)

        u = area(0, 1024).rearrange("p (c t) -> p c t", c=CS5)
        zs = area(1, 1024).rearrange("p (c t) -> p c t", c=HEADS)
        q_t = area(3, 1024).rearrange("p (c t) -> p c t", c=HEADS)
        k_t = area(4, 1024).rearrange("p (c t) -> p c t", c=HEADS)
        v_t = scratch[:, 1024:2048].rearrange("p (c t) -> p c t", c=HEADS)
        qkv = [q_t, k_t, v_t]
        PADT = T + CONV - 1
        pads = [scratch[:, 2048 + s * 2 * PADT:2048 + (s + 1) * 2 * PADT].rearrange("p (m t) -> p m t", m=2) for s in range(2)]
        ab_bank = psum[:, 7, 0:16].rearrange("p (t e) -> p t e", t=NT)

        def w_in_pe(pe):
            cols_pe(pe, "w_in", 0, 10, "t", ADA_FIRST, 0)
            pe.wait_ge(S("narrow_loaded"), 32)
            for t in range(NT):
                for k in range(KD):
                    last = pe.matmul(ab_bank[:, t, :], act_f[:, k, t * P:(t + 1) * P], w_ab[:, k, :], start=k == 0, stop=k == KD - 1)
            last.then_inc(S("gates_raw"), 1)

        def w_in_act(act):
            for j in range(10):
                s = j % 2
                cols_used(act, "w_in", j)
                bank = psum[:, 4 + s, :].rearrange("p (m t) -> p m t", m=2)
                if j < 2:
                    act.activation(u[:, 2 * j:2 * j + 2, :], bank, ACT.Copy).then_inc(S("proj_evac"), 1)
                elif j < 8:
                    act.wait_ge(S("pads_zero"), 1)
                    if j >= 4:
                        act.wait_ge(S("convolved"), j - 3)
                    act.activation(pads[s][:, :, CONV - 1:], bank, ACT.Copy).then_inc(S("proj_evac"), 1)
                else:
                    act.activation(zs[:, 2 * (j - 8):2 * (j - 8) + 2, :], bank, ACT.Silu).then_inc(S("proj_evac"), 1)
                next_hi(act, "w_in", j, 10)
            split_hi(act, GD, PLAN.base["w_glu"][GD])

        def w_in_dve(dve, done):
            for s in range(2):
                last = dve.memset(pads[s][:, :, 0:CONV - 1], 0.0)
            last.then_inc(S("pads_zero"), 1)
            for j in range(10):
                if 2 <= j < 8:
                    jj = j - 2
                    dve.wait_ge(S("proj_evac"), ADA_FIRST + j + 1)
                    dst = qkv[jj // 2][:, 2 * (jj % 2):2 * (jj % 2) + 2, :]
                    for i in range(CONV):
                        for m in range(2):
                            w = col("conv_w", (2 * jj + m) * CONV + i)
                            src = pads[j % 2][:, m, i:i + T]
                            if i == 0:
                                last = dve.tensor_scalar(dst[:, m, :], src, w, None, ALU.mult)
                            else:
                                last = dve.scalar_tensor_tensor(dst[:, m, :], src, w, dst[:, m, :], ALU.mult, ALU.add)
                        if i < CONV - 1:
                            done(last)
                    last.then_inc(S("convolved"), 1)
                next_lo(dve, "w_in", j, 10)
            split_lo(dve, GD, PLAN.base["w_glu"][GD])

        parts = [[b[:, i * 512:(i + 1) * 512].rearrange("p (m t) -> p m t", m=2) for i in range(4)]
                 for b in (arena[:, 14336:16384], scratch[:, 2048:4096])]

        def s5_pe(pe):
            b_re, b_im = (junk[:, i * 512:(i + 1) * 512].rearrange("p (c s) -> p c s", c=CS5) for i in range(2))
            pe.wait_ge(S("s5_b_loaded"), 16)

            def bu(g):
                if g >= 2:
                    pe.wait_ge(S("s5_turned"), g - 1)
                for m in range(2):
                    j = 2 * g + m
                    r, c = 32 * (j % 4), j // 4
                    bank = psum[:, 2 * (g % 2) + m, :]
                    pe.matmul(bank[:, 0:T], b_re[r:r + 32, c, :], u[r:r + 32, c, :], start=True, stop=True)
                    last = pe.matmul(bank[:, T:2 * T], b_im[r:r + 32, c, :], u[r:r + 32, c, :], start=True, stop=True)
                last.then_inc(S("s5_bu"), 1)

            pe.wait_ge(S("proj_evac"), ADA_FIRST + 10)
            pe.wait_ge(S("s5_tables"), 1)
            bu(0)
            for g in range(8):
                if g < 7:
                    bu(g + 1)
                ada_pe(pe, ADA_FIRST + g)
                pe.wait_ge(S("s5_states"), g + 1)
                q1, q4, q2, q3 = parts[g % 2]
                for m in range(2):
                    j = 2 * g + m
                    r, c = 32 * (j % 4), j // 4
                    y = psum[r:r + 32, 4 + c % 2, (c // 2) * T:(c // 2 + 1) * T]
                    pe.matmul(y, cx_re[:, j, :], q1[:, m, :], start=True, stop=False)
                    pe.matmul(y, cx_re[:, j, :], q2[:, m, :], start=False, stop=False)
                    pe.matmul(y, cx_nim[:, j, :], q3[:, m, :], start=False, stop=False)
                    last = pe.matmul(y, cx_nim[:, j, :], q4[:, m, :], start=False, stop=True)
                last.then_inc(S("s5_y"), 1)
            ada_pe(pe, ADA_FIRST + 8)
            pe.wait_ge(S("glu_lo"), 2)
            pe.wait_ge(lo_ready[GD], PLAN.base["w_glu"][GD] + 1)
            for m in range(2):
                last = proj_t(pe, GD, m, act_k=CS5, m0=2 * m, k_cols=512)
            last.then_inc(slab_used[GD], 1)
            ada_pe(pe, ADA_FIRST + 9)

        def s5_dve(dve, done):
            for g in range(8):
                p1, p2, p3, p4 = parts[g % 2]
                dve.wait_ge(S("s5_bu"), g + 1)
                if g >= 2:
                    dve.wait_ge(S("s5_y"), g - 1)
                b = psum[:, 2 * (g % 2):2 * (g % 2) + 2, :]
                er, ei = e_re[:, 2 * g:2 * g + 2, :], e_im[:, 2 * g:2 * g + 2, :]
                dve.tensor_tensor(p1, b[:, :, 0:T], er, ALU.mult)
                dve.tensor_tensor(p2, b[:, :, T:2 * T], ei, ALU.mult)
                dve.tensor_tensor(p3, b[:, :, T:2 * T], er, ALU.mult)
                ins = dve.tensor_tensor(p4, b[:, :, 0:T], ei, ALU.mult)
                ins.then_inc(S("s5_turned"), 1)
                dve.wait_ge(S("s5_turned"), g + 1)
                dve.tensor_tensor(p1, p1, p2, ALU.add)
                done(dve.tensor_tensor(p3, p3, p4, ALU.subtract))
                for m in range(2):
                    r = rad_s[:, 2 * g + m:2 * g + m + 1].to_broadcast([P, T])
                    dve.tensor_tensor_scan(p2[:, m, :], r, p1[:, m, :], 0.0, ALU.mult, ALU.add)
                    last = dve.tensor_tensor_scan(p4[:, m, :], r, p3[:, m, :], 0.0, ALU.mult, ALU.add)
                done(last)
                dve.tensor_tensor(p1, p2, er, ALU.mult)
                dve.scalar_tensor_tensor(p3, p4, -1.0, ei, ALU.mult, ALU.mult)
                dve.tensor_tensor(p4, p4, er, ALU.mult)
                dve.tensor_tensor(p2, p2, ei, ALU.mult).then_inc(S("s5_states"), 1)
                ada_dve(dve, done, ADA_FIRST + g)
            dve.wait_ge(S("s5_y"), 8)
            for c in range(CS5):
                y = psum[:, 4 + c % 2, (c // 2) * T:(c // 2 + 1) * T]
                dve.scalar_tensor_tensor(act_f[:, c, :], u[:, c, :], col("s5_d", c), y, ALU.mult, ALU.add).then_inc(S("s5_yd"), 1)
            ada_dve(dve, done, ADA_FIRST + 8)
            for q in range(2):
                dve.wait_ge(S("glu_hi"), q + 1)
                dve.tensor_tensor(act_lo[:, 2 * q:2 * q + 2, :], act_f[:, 2 * q:2 * q + 2, :],
                                  act_hi[:, 2 * q:2 * q + 2, :].bitcast(F32), ALU.subtract).then_inc(S("glu_lo"), 1)
            sg = arena[:, 14336:15360].rearrange("p (m t) -> p m t", m=CS5)
            for m in range(CS5):
                dve.wait_ge(S("glu_gate"), m + 1)
                dve.tensor_tensor(act_f[:, m, :], act_f[:, m, :], sg[:, m, :], ALU.mult).then_inc(S("act_f"), 1)
            ada_dve(dve, done, ADA_FIRST + 9)

        def s5_act(act):
            for q in range(2):
                act.wait_ge(S("s5_yd"), 2 * q + 2)
                act.activation(act_f[:, 2 * q:2 * q + 2, :], act_f[:, 2 * q:2 * q + 2, :], ACT.Gelu_apprx_tanh).then_inc(S("glu_f"), 1)
                act.wait_ge(S("glu_f"), q + 1)
                act.activation(act_hi[:, 2 * q:2 * q + 2, :], act_f[:, 2 * q:2 * q + 2, :], ACT.Copy).then_inc(S("glu_hi"), 1)
            sg = arena[:, 14336:15360].rearrange("p (m t) -> p m t", m=CS5)
            act.wait_ge(slab_used[GD], PLAN.base["w_glu"][GD] + 1)
            for m in range(CS5):
                act.activation(sg[:, m, :], psum[:, m // 2, (m % 2) * T:(m % 2 + 1) * T], ACT.Sigmoid, bias=col("b_glu", m))\
                   .then_inc(S("glu_gate"), 1)
        def blk(b):
            return area(b, 1024)

        def th_view(ap):
            return ap.rearrange("p (e n) -> p e n", n=P)

        def tok_view(ap):
            return ap.rearrange("p (c t) -> p c t", t=T)

        sq, rn = arena[:, 6 * 1024:8 * 1024], arena[:, 8 * 1024:10 * 1024]
        g_b, beta_b, kb_t, eg = blk(10), blk(11), blk(12), blk(13)
        diff = blk(6)
        n_t, qk_t = blk(7), blk(8)
        vb = blk(9)
        qd, kt = arena[:, 14336:14848], arena[:, 14848:15360]
        kbg = arena[:, 15360:15872]
        m_inv, mt_inv = blk(10), blk(11)
        p_sb = blk(0)
        scr_a, scr_b = scratch[:, 2048:3072], scratch[:, 3072:4096]
        nkc, vn0, s1, vn1 = scr_a[:, 0:512], scr_a[:, 512:1024], scr_b[:, 0:512], scr_b[:, 512:1024]
        o_f, o_sq, o_rn = blk(12), blk(13), blk(6)

        def banks(b, n=2):
            return psum[:, b:b + n, :].rearrange("p b n -> p (b n)")

        def gdn_pe(pe):
            ones, upto = mat("ones"), mat("upto")
            pe.wait_ge(S("qk_sq"), 2)
            pe.wait_ge(S("glu_gate"), CS5)
            for e in range(8):
                last = pe.matmul(psum[:, e // 2, (e % 2) * T:(e % 2 + 1) * T], ones, sq[:, e * T:(e + 1) * T], start=True, stop=True)
            last.then_inc(S("qk_sums"), 1)
            ada_pe(pe, ADA_FIRST + 10)
            pe.wait_ge(S("g_rows"), 2)
            pe.matmul(psum[:, 7, 32:32 + TH], upto, g_s, start=True, stop=True).then_inc(S("g_cum"), 1)
            for e in range(TH):
                last = pe.matmul(banks(4)[:, e * P:(e + 1) * P], th_view(g_b)[:, e, :], upto, start=True, stop=True)
            last.then_inc(S("g_cum_rows"), 1)
            ada_pe(pe, ADA_FIRST + 11)
            pe.wait_ge(S("qk_root"), 1)
            for e in range(TH):
                last = pe.matmul(banks(0)[:, e * P:(e + 1) * P], th_view(beta_b)[:, e, :], ident, start=True, stop=True)
            last.then_inc(S("beta_rows"), 1)
            ada_pe(pe, ADA_FIRST + 12)
            pe.wait_ge(S("kb"), 1)
            pe.wait_ge(S("diff"), 1)
            kn, qn, kb = (tok_view(b) for b in (blk(4), blk(3), kb_t))
            for bank, rhs in ((2, kb), (4, qn)):
                for e in range(TH):
                    ts = slice((e % 2) * P, (e % 2 + 1) * P)
                    last = pe.matmul(banks(bank)[:, e * P:(e + 1) * P], kn[:, e // 2, ts], rhs[:, e // 2, ts], start=True, stop=True)
                last.then_inc(S("kk_qk"), 1)
            ada_pe(pe, ADA_FIRST + 13)
            for e in range(TH):
                last = pe.transpose(banks(0)[:, e * P:(e + 1) * P], blk(4)[:, e * P:(e + 1) * P], ident)
            last.then_inc(S("k_nat"), 1)
            ada_pe(pe, ADA_FIRST + 14)
            pe.wait_ge(S("n_qk"), 2)
            for e in range(TH):
                last = pe.transpose(banks(2)[:, e * P:(e + 1) * P], scratch[:, 1024 + e * P:1024 + (e + 1) * P], ident)
            last.then_inc(S("v_nat"), 1)
            ada_pe(pe, ADA_FIRST + 15)
            pe.wait_ge(S("inv_start"), 1)
            pe.wait_ge(S("nat_read"), 1)
            m3, mt3, n3, p3 = (th_view(b) for b in (m_inv, mt_inv, n_t, p_sb))
            for lv in range(LEVELS):
                for hf in range(2):
                    es = range(4 * hf, 4 * hf + 4)
                    if lv:
                        pe.wait_ge(S("inv_done"), 2 * (lv - 1) + hf + 1)
                    for e in es:
                        last = pe.matmul(psum[:, hf, (e % 4) * P:(e % 4 + 1) * P], n3[:, e, :], m3[:, e, :], start=True, stop=True)
                    last.then_inc(S("inv_p"), 1)
                for hf in range(2):
                    es = range(4 * hf, 4 * hf + 4)
                    pe.wait_ge(S("inv_masked"), 2 * lv + hf + 1)
                    for e in es:
                        pe.matmul(psum[:, 2 + hf, (e % 4) * P:(e % 4 + 1) * P], mt3[:, e, :], p3[:, e, :], start=True, stop=True)
                    for e in es:
                        last = pe.matmul(psum[:, 4 + hf, (e % 4) * P:(e % 4 + 1) * P], p3[:, e, :], mt3[:, e, :], start=True, stop=True)
                    last.then_inc(S("inv_q"), 1)
            pe.wait_ge(S("inv_done"), 2 * LEVELS)
            kbg3, kt3, vn03, s13, vn13, nkc3, qd3 = (th_view(b) for b in (kbg, kt, vn0, s1, vn1, nkc, qd))
            vb3, qk3 = th_view(vb), th_view(qk_t)

            def hp(h):
                return slice(h * P, (h + 1) * P)
            for h in range(HEADS):
                last = pe.matmul(psum[:, 0, hp(h)], kbg3[:, h, :], mt3[:, 2 * h + 1, :], start=True, stop=True)
            last.then_inc(S("kc"), 1)
            for h in range(HEADS):
                last = pe.matmul(psum[:, 1, hp(h)], mt3[:, 2 * h, :], vb3[:, 2 * h, :], start=True, stop=True)
            last.then_inc(S("v_new"), 1)
            pe.wait_ge(S("vn_read"), 1)
            for h in range(HEADS):
                last = pe.matmul(psum[:, 6, hp(h)], kt3[:, h, :], vn03[:, h, :], start=True, stop=True)
            last.then_inc(S("state"), 1)
            pe.wait_ge(S("state_read"), 1)
            pe.wait_ge(S("kc_read"), 1)
            for h in range(HEADS):
                pe.matmul(psum[:, 7, hp(h)], mt3[:, 2 * h + 1, :], vb3[:, 2 * h + 1, :], start=True, stop=False)
                last = pe.matmul(psum[:, 7, hp(h)], nkc3[:, h, :], s13[:, h, :], start=False, stop=True)
            last.then_inc(S("v_new"), 1)
            pe.wait_ge(S("vn_read"), 2)
            for h in range(HEADS):
                o0, o1 = banks(2)[:, 2 * h * P:(2 * h + 1) * P], banks(2)[:, (2 * h + 1) * P:(2 * h + 2) * P]
                pe.matmul(o0, vn03[:, h, :], qk3[:, 2 * h, :], start=True, stop=True)
                pe.matmul(o1, s13[:, h, :], qd3[:, h, :], start=True, stop=False)
                last = pe.matmul(o1, vn13[:, h, :], qk3[:, 2 * h + 1, :], start=False, stop=True)
            last.then_inc(S("gdn_o"), 1)
            pe.wait_ge(S("gdn_sq"), 1)
            for b in range(2):
                last = pe.matmul(psum[:, 4 + b, :], ones, o_sq[:, b * 512:(b + 1) * 512], start=True, stop=True)
            last.then_inc(S("gdn_sums"), 1)

        def gdn_act(act):
            for i in range(3):
                act.wait_ge(S("convolved"), 2 * i + 2)
                act.activation(qkv[i], qkv[i], ACT.Silu).then_inc(S("qkv"), 1)
            for i in range(2):
                act.wait_ge(S("qkv"), i + 1)
                act.activation(sq[:, i * 1024:(i + 1) * 1024], blk(3 + i), ACT.Square).then_inc(S("qk_sq"), 1)
            act.wait_ge(S("gate_in"), 1)
            act.activation(e_s, e_s, ACT.Exp, scale=-1.0).then_inc(S("gate_exp"), 1)
            act.activation(bg_s, bg_s, ACT.Exp, scale=-1.0).then_inc(S("gate_exp"), 1)
            act.activation(ea_s, col("a_log", 0, TH), ACT.Exp).then_inc(S("gate_exp"), 1)
            act.wait_ge(S("gate_exp"), 1)
            act.activation(e_s, e_s, ACT.Ln, bias=one_col).then_inc(S("gate_ln"), 1)
            act.wait_ge(S("qk_sums"), 1)
            act.activation(rn, banks(0, 4), ACT.Sqrt, bias=eps_col).then_inc(S("qk_root"), 1)
            act.wait_ge(S("g_cum_rows"), 1)
            act.activation(eg, banks(4), ACT.Exp).then_inc(S("eg"), 1)
            act.wait_ge(S("gc"), 1)
            act.activation(egc_s, gc_s, ACT.Exp).then_inc(S("egc"), 1)
            act.wait_ge(S("tail"), 1)
            act.activation(tail_s, tail_s, ACT.Exp).then_inc(S("tail_exp"), 1)
            act.wait_ge(S("diff"), 1)
            act.activation(diff, diff, ACT.Exp).then_inc(S("decay_exp"), 1)
            head_act(act, "w_out")
            act.wait_ge(S("kc"), 1)
            act.activation(nkc, psum[:, 0, :], ACT.Copy, scale=-1.0).then_inc(S("kc_read"), 1)
            act.wait_ge(S("v_new"), 1)
            act.activation(vn0, psum[:, 1, :], ACT.Copy).then_inc(S("vn_read"), 1)
            act.wait_ge(S("state"), 1)
            act.activation(s1, psum[:, 6, :], ACT.Copy).then_inc(S("state_read"), 1)
            act.wait_ge(S("v_new"), 2)
            act.activation(vn1, psum[:, 7, :], ACT.Copy).then_inc(S("vn_read"), 1)
            act.wait_ge(S("gdn_o"), 1)
            act.activation(o_sq, banks(2), ACT.Square).then_inc(S("gdn_sq"), 1)
            act.activation(o_f, banks(2), ACT.Copy).then_inc(S("gdn_of"), 1)
            act.wait_ge(S("gdn_sums"), 1)
            act.activation(o_rn, banks(4), ACT.Sqrt, bias=eps_col, scale=1.0 / DK).then_inc(S("gdn_root"), 1)

        def gdn_dve(dve, done):
            dve.wait_ge(S("gates_raw"), 1)
            a_v = psum[:, 7, 0:16].rearrange("p (t e) -> p e t", t=NT)
            heads_v = [ap.rearrange("p (h t) -> p h t", h=HEADS) for ap in (g_s, bg_s)]
            done(dve.tensor_tensor(heads_v[0], a_v[:, 0:4, :], col("dt_bias", 0, TH).rearrange("p (h t) -> p h t", h=HEADS), ALU.add))
            done(dve.tensor_copy(heads_v[1], a_v[:, 4:8, :]))
            done(dve.tensor_scalar(e_s, g_s, -1.0, None, ALU.mult))
            done(dve.tensor_scalar(sp_s, g_s, 0.0, None, ALU.max))
            dve.tensor_tensor(e_s, e_s, g_s, ALU.max).then_inc(S("gate_in"), 1)
            dve.wait_ge(S("gate_exp"), 3)
            done(dve.tensor_scalar(bg_s, bg_s, 1.0, None, ALU.add))
            done(dve.reciprocal(beta_s, bg_s))
            dve.wait_ge(S("gate_ln"), 1)
            done(dve.tensor_tensor(sp_s, sp_s, e_s, ALU.add))
            done(dve.scalar_tensor_tensor(g_s, sp_s, -1.0, ea_s, ALU.mult, ALU.mult))
            dve.tensor_copy(th_view(g_b), bc(g_s, P)).then_inc(S("g_rows"), 1)
            dve.tensor_copy(th_view(beta_b), bc(beta_s, P)).then_inc(S("g_rows"), 1)
            ada_dve(dve, done, ADA_FIRST + 10)
            dve.wait_ge(S("g_cum"), 1)
            dve.tensor_copy(gc_s, psum[:, 7, 32:32 + TH]).then_inc(S("gc"), 1)
            ada_dve(dve, done, ADA_FIRST + 11)
            dve.wait_ge(S("qk_root"), 1)
            done(dve.reciprocal(rn, rn))
            done(dve.scalar_tensor_tensor(blk(3), blk(3), DK ** -0.5, rn[:, 0:1024], ALU.mult, ALU.mult))
            done(dve.tensor_tensor(blk(4), blk(4), rn[:, 1024:2048], ALU.mult))
            dve.wait_ge(S("beta_rows"), 1)
            dve.tensor_tensor(kb_t, blk(4), banks(0), ALU.mult).then_inc(S("kb"), 1)
            ada_dve(dve, done, ADA_FIRST + 12)
            dve.wait_ge(S("eg"), 1)
            dve.wait_ge(S("gc"), 1)
            cum = th_view(banks(4))
            done(dve.tensor_tensor(th_view(diff), cum, bc(gc_s, P), ALU.subtract))
            last_g = banks(4).rearrange("p (h t n) -> p h t n", h=HEADS, t=NT)[:, :, 0, P - 1]
            dve.tensor_tensor(tail_s, last_g, gc_s.rearrange("p (h t) -> p h t", h=HEADS)[:, :, 0], ALU.subtract).then_inc(S("tail"), 1)
            dve.tensor_scalar(diff, diff, 0.0, None, ALU.min).then_inc(S("diff"), 1)
            dve.tensor_tensor(qd.rearrange("p (h n) -> p h n", h=HEADS), tok_view(blk(3))[:, :, P:T], tok_view(eg)[:, :, P:T], ALU.mult)
            ada_dve(dve, done, ADA_FIRST + 13)
            dve.wait_ge(S("decay_exp"), 1)
            done(dve.tensor_tensor(th_view(diff), th_view(diff), rep(mat("upto"), TH), ALU.mult))
            dve.wait_ge(S("kk_qk"), 1)
            dve.tensor_tensor(n_t, banks(2), diff, ALU.mult).then_inc(S("n_qk"), 1)
            dve.wait_ge(S("kk_qk"), 2)
            dve.tensor_tensor(qk_t, banks(4), diff, ALU.mult).then_inc(S("n_qk"), 1)
            ada_dve(dve, done, ADA_FIRST + 14)
            dve.wait_ge(S("egc"), 1)
            done(dve.tensor_tensor(bg_s, beta_s, egc_s, ALU.mult))
            dve.wait_ge(S("k_nat"), 1)
            dve.wait_ge(S("tail_exp"), 1)
            k_nat = banks(0).rearrange("p (h t n) -> p h t n", h=HEADS, t=NT)
            bg1 = bg_s.rearrange("p (h t) -> p h t", h=HEADS)[:, :, 1]
            dve.tensor_tensor(kbg.rearrange("p (h n) -> p h n", h=HEADS), k_nat[:, :, 1, :], bc(bg1, P), ALU.mult)
            dve.tensor_tensor(kt.rearrange("p (h n) -> p h n", h=HEADS), k_nat[:, :, 0, :], bc(tail_s, P), ALU.mult)
            dve.wait_ge(S("v_nat"), 1)
            dve.tensor_tensor(th_view(vb), th_view(banks(2)), bc(beta_s, P), ALU.mult).then_inc(S("nat_read"), 1)
            dve.tensor_copy(th_view(m_inv), rep(ident, TH))
            dve.tensor_copy(th_view(mt_inv), rep(ident, TH)).then_inc(S("inv_start"), 1)
            ada_dve(dve, done, ADA_FIRST + 15)
            dve.wait_ge(S("inv_start"), 1)
            halves = [[ap[:, hf * 512:(hf + 1) * 512] for ap in (m_inv, mt_inv, p_sb)] for hf in range(2)]
            for lv in range(LEVELS):
                for hf in range(2):
                    dve.wait_ge(S("inv_p"), 2 * lv + hf + 1)
                    dve.tensor_tensor(th_view(halves[hf][2]), th_view(psum[:, hf, :]), rep(mat(f"level{lv}"), 4), ALU.mult)\
                       .then_inc(S("inv_masked"), 1)
                for hf in range(2):
                    dve.wait_ge(S("inv_q"), 2 * lv + hf + 1)
                    dve.tensor_tensor(halves[hf][0], halves[hf][0], psum[:, 2 + hf, :], ALU.subtract)
                    dve.tensor_tensor(halves[hf][1], halves[hf][1], psum[:, 4 + hf, :], ALU.subtract).then_inc(S("inv_done"), 1)
            head_dve(dve, "w_out")
            mod_dve(dve, done, 2, "norm2")
            dve.wait_ge(S("gdn_root"), 1)
            done(dve.reciprocal(o_rn, o_rn))
            dve.wait_ge(S("gdn_of"), 1)
            done(dve.tensor_tensor(o_f, o_f, o_rn, ALU.mult))
            for h in range(HEADS):
                dve.scalar_tensor_tensor(act_f[:, CS5 + h, :], tok_view(o_f)[:, h, :], col("gdn_g"), zs[:, h, :], ALU.mult, ALU.mult)\
                   .then_inc(S("act_f"), 1)


        def router_pe(pe):
            pe.wait_ge(S("act_f"), 8 * 3)
            for t in range(NT):
                for k in range(KD):
                    last = pe.matmul(psum[:, 3, t * 36:(t + 1) * 36], act_f[:, k, t * P:(t + 1) * P], w_router[:, k, :],
                                     start=k == 0, stop=k == KD - 1)
            last.then_inc(S("router_raw"), 1)

        def gate_row(pe, i):
            pe.wait_ge(S("gate_diag"), i + 1)
            for t in range(NT):
                last = pe.matmul(gate_bank[:, t * P:(t + 1) * P], mat("ones"), diag[:, t, :], start=True, stop=True)
            last.then_inc(S("gate_row"), 1)

        def router_act(act):
            act.wait_ge(S("group_diff"), 1)
            act.activation(gexp, gexp, ACT.Exp).then_inc(S("group_exp"), 1)
            act.wait_ge(S("pair_diff"), 1)
            act.activation(pair_e, pair_e, ACT.Exp).then_inc(S("pair_exp"), 1)

        gexp = tiny(NT * N_GROUPS)
        geq = tiny(NT * N_GROUPS)
        gmax, gden, wmax, m1, m2, pair_e, w1, w2 = (tiny(NT) for _ in range(8))
        sel, eq8, oh1, oh2 = (tiny(NT * PER_GROUP) for _ in range(4))

        def router_dve(dve, done):
            def by(ap, n):
                return ap.rearrange("p (t n) -> p t n", n=n)

            def best(src, n, mx, onehot, order):
                done(dve.reduce_max(mx, by(src, n), AX))
                done(dve.tensor_tensor(by(eq8[:, 0:NT * n], n), by(src, n), bc(mx, n), ALU.is_equal))
                done(dve.tensor_tensor(by(eq8[:, 0:NT * n], n), by(eq8[:, 0:NT * n], n), rep(order, NT), ALU.mult))
                done(dve.reduce_max(wmax, by(eq8[:, 0:NT * n], n), AX))
                done(dve.tensor_tensor(by(onehot, n), by(eq8[:, 0:NT * n], n), bc(wmax, n), ALU.is_equal))

            dve.wait_ge(S("router_raw"), 1)
            done(dve.tensor_copy(lg, psum[:, 3, 0:72].rearrange("p (t n) -> p t n", t=NT)))
            done(dve.tensor_copy(by(gexp, 4), lg[:, :, 0:4]))
            best(gexp, N_GROUPS, gmax, geq, first[:, 4:8])
            dve.tensor_tensor(by(gexp, 4), by(gexp, 4), bc(gmax, 4), ALU.subtract).then_inc(S("group_diff"), 1)
            for t in range(NT):
                ex = lg[:, t, 4:36].rearrange("p (g e) -> p e g", g=N_GROUPS)
                done(dve.tensor_tensor(sel4[:, t, :, :], ex, rep(by(geq, 4)[:, t, :], PER_GROUP), ALU.mult))
            done(dve.reduce_sum(by(sel, 8), sel4, AX))
            best(sel, PER_GROUP, m1, oh1, first[:])
            done(dve.scalar_tensor_tensor(sel, oh1, -3.0e38, sel, ALU.mult, ALU.add))
            best(sel, PER_GROUP, m2, oh2, first[:])
            dve.tensor_tensor(pair_e, m2, m1, ALU.subtract).then_inc(S("pair_diff"), 1)
            dve.wait_ge(S("group_exp"), 1)
            done(dve.reduce_sum(gden, by(gexp, 4), AX))
            done(dve.reciprocal(gden, gden))
            dve.wait_ge(S("pair_exp"), 1)
            done(dve.tensor_scalar(w1, pair_e, 1.0, None, ALU.add))
            done(dve.reciprocal(w1, w1))
            done(dve.tensor_tensor(w1, w1, gden, ALU.mult))
            done(dve.tensor_tensor(w2, w1, pair_e, ALU.mult))
            done(dve.tensor_tensor(by(oh1, 8), by(oh1, 8), bc(w1, 8), ALU.mult))
            done(dve.tensor_tensor(by(oh2, 8), by(oh2, 8), bc(w2, 8), ALU.mult))
            done(dve.tensor_tensor(oh1, oh1, oh2, ALU.add))
            for t in range(NT):
                dst = comb[:, t, :].rearrange("p (g e) -> p g e", g=N_GROUPS)
                last = dve.tensor_tensor(dst, bc(by(geq, 4)[:, t, :], PER_GROUP), rep(by(oh1, 8)[:, t, :], N_GROUPS), ALU.mult)
            done(last)
            gate_diag(dve, comb[:, :, 0:1])

        def residual_dve(dve, done, s, used, part, final):
            dve.wait_ge(slab_used[s], used)
            gate = mod[:, part * D:(part + 1) * D].rearrange("p (b n) -> p b n", b=2)
            for t in range(NT):
                done(dve.tensor_tensor(xn(t).rearrange("p (b n) -> p b n", b=2), acc[:, 2 * t:2 * t + 2, :], gate, ALU.mult))
                dve.tensor_tensor(x[:, t, :], x[:, t, :], xn(t), ALU.add).then_inc(S("moe_x" if final else "x_ready"), 1)

        def final_act(act):
            for t in range(NT):
                act.wait_ge(S("moe_x"), t + 1)
                if t:
                    act.wait_ge(S("final_sums"), t)
                act.activation(junk, x[:, t, :], ACT.Square, accum_out=f_sum[:, t:t + 1]).then_inc(S("final_sums"), 1)

        def final_pool(pool):
            pool.wait_ge(S("final_sums"), NT)
            rstd(pool, f_rstd, f_sum, 1.0 / D, EPS, S("final_rstd"))

        def final_dve(dve):
            dve.wait_ge(S("row_loaded0"), 16)
            dve.wait_ge(S("final_rstd"), 1)
            for t in range(NT):
                dve.scalar_tensor_tensor(x[:, t, :], x[:, t, :], f_rstd[:, t:t + 1], rows[:, 0, :], ALU.mult, ALU.mult)\
                   .then_inc(S("x_ready"), 1)
        ATT = [l for l in range(LAYERS) if KINDS[l] != 1]
        SC = T + P
        q_a = arena[:, 0:2048].rearrange("p (c t) -> p c t", t=T)
        k_a = arena[:, 2048:4096].rearrange("p (c t) -> p c t", t=T)
        v_a = arena[:, 4096:6144].rearrange("p (t n) -> p t n", t=NT)
        bias_a = [arena[:, 6144 + i * 4 * T:6144 + (i + 1) * 4 * T].rearrange("p (h n) -> p h n", h=4) for i in range(2)]
        prob_a = [arena[:, 9216 + i * 4 * SC:9216 + (i + 1) * 4 * SC].rearrange("p (h n) -> p h n", h=4) for i in range(2)]
        pt_a = arena[:, 12288:12288 + 4 * SC]
        mx_a = [tiny(8) for _ in range(2)]
        sum_a = [tiny(8) for _ in range(2)]
        lam_p, lam_e, nlam, subg = tiny(2), tiny(2), tiny(1), tiny(1)
        o2, o2_rn = arena[:, 0:2048], arena[:, 2048:4096]

        def same_before(l):
            return KINDS[:l].count(KINDS[l])

        def n_proj(l):
            return 8 if KINDS[l] == 1 else 12

        def order(l, j):
            return j

        def proj_base(l):
            return ADA_FIRST + 10 + sum(n_proj(i) for i in range(l))

        def act_index(l, which):
            return 3 + 4 * l + which

        def f_index(l):
            return 3 + l

        def qkv_act(act, l):
            name = f"mix{l}"
            for j in range(12):
                cols_used(act, name, j)
                bank = psum[:, 4 + j % 2, :].rearrange("p (m t) -> p m t", m=2)
                if j < 4:
                    act.activation(q_a[:, 2 * j:2 * j + 2, :], bank, ACT.Copy, scale=0.125).then_inc(S("proj_evac"), 1)
                elif j < 8:
                    act.activation(k_a[:, 2 * j - 8:2 * j - 6, :], bank, ACT.Copy).then_inc(S("proj_evac"), 1)
                else:
                    act.activation(v_a[:, :, (j - 8) * 256:(j - 7) * 256], bank, ACT.Copy).then_inc(S("proj_evac"), 1)
                next_hi(act, name, j, 12)
            head_act(act, f"wo{l}")

        def cols_dve(dve, l):
            name = f"mix{l}"
            for j in range(n_proj(l)):
                next_lo(dve, name, j, n_proj(l))
            head_dve(dve, f"wo{l}")

        def bias_pool(pool, l):
            n = ATT.index(l)
            pool.wait_ge(S("pre_rstd"), NT * (4 + 3 * l))
            for b in range(4):
                bt = 4 * n + b
                s = bt % 2
                if bt >= 2:
                    pool.wait_ge(S("scores"), bt - 1)
                if KINDS[l] == 2:
                    pool.dma_start(bias_a[s], a["alibi"][:, 4 * b:4 * b + 4, :]).then_inc(S(f"bias_in{s}"), 16)
                else:
                    tab = a["rel_rows"]
                    base = tab.offset + ((l // 3) * 16 + 4 * b) * 512
                    pool.dma_start(bias_a[s], bass.AP(tensor=tab.tensor, offset=base, ap=[[1, P], [512, 4], [1, T]]))\
                        .then_inc(S(f"bias_in{s}"), 16)
                    pool.wait_ge(S(f"bias_in{s}"), 16 * (bt // 2 + 1))
                    pool.memset(bias_a[s][64:P, :, 192:256], -1e30).then_inc(S("bias_ready"), 1)
            if KINDS[l] == 0:
                pool.wait_ge(S("bias_ready"), 4 * same_before(l) + 4)

        def att_pe(pe, l):
            n = ATT.index(l)
            turn = mat("ident") if KINDS[l] == 2 else mat("flip")
            pe.wait_ge(S("proj_evac"), proj_base(l) + 12)

            def scores(b):
                bt = 4 * n + b
                if KINDS[l] == 0:
                    pe.wait_ge(S("bias_ready"), 4 * same_before(l) + b + 1)
                else:
                    pe.wait_ge(S(f"bias_in{bt % 2}"), 16 * (bt // 2 + 1))
                pe.wait_ge(S("exp"), 8 * bt)
                for hh in range(4):
                    h = 4 * b + hh
                    r, c = (h % 2) * 64, h // 2
                    pe.matmul(psum[:, hh, 0:T], turn, bias_a[bt % 2][:, hh, :], start=True, stop=False)
                    pe.matmul(psum[:, hh, 0:T], q_a[r:r + 64, c, P:T], k_a[r:r + 64, c, :], start=False, stop=True)
                    pe.matmul(psum[:, hh, T:SC], turn, bias_a[bt % 2][:, hh, P:T], start=True, stop=False)
                    last = pe.matmul(psum[:, hh, T:SC], q_a[r:r + 64, c, 0:P], k_a[r:r + 64, c, 0:P], start=False, stop=True)
                last.then_inc(S("scores"), 1)

            def turned(b):
                bt = 4 * n + b
                pe.wait_ge(S("prob"), 2 * bt + 2)
                pe.wait_ge(S("pt"), bt)
                for hh in range(4):
                    for i, at0 in enumerate((T, 0, P)):
                        e = 3 * hh + i
                        last = pe.transpose(psum[:, 4 + e // 4, (e % 4) * P:(e % 4 + 1) * P], prob_a[bt % 2][:, hh, at0:at0 + P], ident)
                last.then_inc(S("pt_raw"), 1)

            def out_of(b):
                bt = 4 * n + b
                pe.wait_ge(S("pt"), bt + 1)
                if b:
                    if KINDS[l] == 0:
                        pe.wait_ge(S("act_f"), 8 * f_index(l) + 2 * b)
                    else:
                        pe.wait_ge(S("att_read"), 4 * same_before(l) + b)
                for hh in range(4):
                    cc = hh // 2
                    p0, p1 = pt_a[:, hh * SC:hh * SC + T], pt_a[:, hh * SC + T:(hh + 1) * SC]
                    if KINDS[l] == 0:
                        h = 4 * b + hh
                        r = (h % 2) * 64
                        dst = psum[r:r + 64, 7, cc * T:(cc + 1) * T]
                        vs = slice(h * 64, (h + 1) * 64)
                        pe.matmul(dst, v_a[:, 0, vs], p0, start=True, stop=False)
                        last = pe.matmul(dst[:, P:T], v_a[:, 1, vs], p1, start=False, stop=True)
                    else:
                        dst = psum[:, 7, cc * T:(cc + 1) * T]
                        vs = slice((2 * b + cc) * P, (2 * b + cc + 1) * P)
                        pe.matmul(dst, v_a[:, 0, vs], p0, start=hh % 2 == 0, stop=False)
                        last = pe.matmul(dst[:, P:T], v_a[:, 1, vs], p1, start=False, stop=hh % 2 == 1)
                last.then_inc(S("att_o"), 1)

            if KINDS[l] == 2:
                pe.wait_ge(S("lam_prod"), 1)
                pe.matmul(psum[:, 7, 0:2], mat("ones"), lam_p, start=True, stop=True).then_inc(S("lam_sum"), 1)
                pe.wait_ge(S("lam_exp"), 1)
            scores(0)
            for b in range(4):
                if b < 3:
                    scores(b + 1)
                turned(b)
                out_of(b)
            if KINDS[l] == 2:
                pe.wait_ge(S("sub_sq"), 4)
                pe.wait_ge(S("exp"), 8 * (4 * n + 4))
                for h in range(8):
                    last = pe.matmul(psum[:, h // 2, (h % 2) * T:(h % 2 + 1) * T], mat("ones"), o2[:, h * T:(h + 1) * T], start=True, stop=True)
                last.then_inc(S("sub_sums"), 1)

        def att_act(act, l):
            n = ATT.index(l)
            if KINDS[l] == 2:
                act.wait_ge(S("lam_sum"), 1)
                act.activation(lam_e, psum[:, 7, 0:2], ACT.Exp).then_inc(S("lam_exp"), 1)

            def exps(b):
                bt = 4 * n + b
                act.wait_ge(S("nmax"), bt + 1)
                if bt >= 2:
                    act.wait_ge(S("pt_raw"), bt - 1)
                for i in range(2):
                    for hh in range(4):
                        cols_ = slice(0, T) if i == 0 else slice(T, SC)
                        e = 4 * i + hh
                        act.activation(prob_a[bt % 2][:, hh, cols_], psum[:, hh, cols_], ACT.Exp, bias=mx_a[bt % 2][:, e:e + 1],
                                       accum_out=sum_a[bt % 2][:, e:e + 1]).then_inc(S("exp"), 1)

            def read_out(b):
                bt = 4 * n + b
                act.wait_ge(S("att_o"), bt + 1)
                o = psum[:, 7, :].rearrange("p (c t) -> p c t", c=2)
                if KINDS[l] == 0:
                    for c in range(2):
                        act.activation(act_f[:, 2 * b + c, :], o[:, c, :], ACT.Copy).then_inc(S("act_f"), 1)
                else:
                    act.activation(act_f[:, 2 * b:2 * b + 2, :], o, ACT.Copy).then_inc(S("att_read"), 1)

            exps(0)
            for b in range(4):
                bt = 4 * n + b
                act.wait_ge(S("pt_raw"), bt + 1)
                act.wait_ge(S("att_o"), bt)
                act.activation(pt_a, banks(4, 3), ACT.Copy).then_inc(S("pt"), 1)
                if b < 3:
                    exps(b + 1)
                read_out(b)
            if KINDS[l] == 2:
                act.wait_ge(S("att_read"), 4 * same_before(l) + 4)
                for q in range(4):
                    act.activation(o2[:, q * 512:(q + 1) * 512], act_f[:, 2 * q:2 * q + 2, :].rearrange("p c t -> p (c t)"), ACT.Square)\
                       .then_inc(S("sub_sq"), 1)
                act.wait_ge(S("sub_sums"), 1)
                act.activation(o2_rn, banks(0, 4), ACT.Sqrt, bias=eps_col, scale=1.0 / P).then_inc(S("sub_root"), 1)

        def att_dve(dve, l, done):
            n = ATT.index(l)
            if KINDS[l] == 2:
                lam = col("lam_c", 0, 4).rearrange("p (a b) -> p a b", b=2)
                dve.tensor_tensor(lam_p, lam[:, :, 0], lam[:, :, 1], ALU.mult).then_inc(S("lam_prod"), 1)
                done(dve.tensor_scalar(subg, col("subln"), 1.0 - LAMBDA_INIT, None, ALU.mult))
                dve.wait_ge(S("lam_exp"), 1)
                done(dve.tensor_tensor(nlam, lam_e[:, 1:2], lam_e[:, 0:1], ALU.subtract))
                done(dve.tensor_scalar(nlam, nlam, LAMBDA_INIT, None, ALU.subtract))

            def maxes(b):
                bt = 4 * n + b
                mx = mx_a[bt % 2]
                dve.wait_ge(S("scores"), bt + 1)
                dve.reduce_max(mx[:, 0:4], psum[:, 0:4, 0:T], AX)
                done(dve.reduce_max(mx[:, 4:8], psum[:, 0:4, T:SC], AX))
                dve.tensor_scalar(mx, mx, -1.0, None, ALU.mult).then_inc(S("nmax"), 1)

            def normalise(b):
                bt = 4 * n + b
                inv, pr = sum_a[bt % 2], prob_a[bt % 2]
                dve.wait_ge(S("exp"), 8 * bt + 8)
                done(dve.reciprocal(inv, inv))
                if KINDS[l] == 2:
                    odd = inv.rearrange("p (e m) -> p e m", m=2)[:, :, 1]
                    done(dve.tensor_scalar(odd, odd, nlam, None, ALU.mult))
                dve.tensor_tensor(pr[:, :, 0:T], pr[:, :, 0:T], bc(inv[:, 0:4], T), ALU.mult).then_inc(S("prob"), 1)
                dve.tensor_tensor(pr[:, :, T:SC], pr[:, :, T:SC], bc(inv[:, 4:8], P), ALU.mult).then_inc(S("prob"), 1)

            maxes(0)
            for b in range(4):
                normalise(b)
                if b < 3:
                    maxes(b + 1)
            if KINDS[l] == 2:
                dve.wait_ge(S("sub_root"), 1)
                done(dve.reciprocal(o2_rn, o2_rn))
                for h in range(8):
                    dve.scalar_tensor_tensor(act_f[:, h, :], act_f[:, h, :], subg, o2_rn[:, h * T:(h + 1) * T], ALU.mult, ALU.mult)\
                       .then_inc(S("act_f"), 1)

        GROUPS = 8
        u_b, v_b = tok_view(arena[:, 0:2048]), arena[:, 2048:4096].rearrange("p (t n) -> p t n", t=NT)
        ws_t, ws_in = th_view(blk(4)), th_view(blk(5))
        ln_g, ln_b, bs_b, vc_sq = blk(6), blk(7), blk(8), blk(9)
        v_sum, v_var, v_rstd = tiny(NT), tiny(NT), tiny(NT)

        def gmlp_loads(pool):
            pool.dma_start(ws_in, a["b_w_s"].rearrange("g t s -> t g s")).then_inc(S("ws_in"), 16)
            for name, dst in (("b_ln_g", ln_g), ("b_ln_b", ln_b), ("b_b_s", bs_b)):
                pool.dma_start(dst, a[name].to_broadcast([P, D])).then_inc(S("b_rows"), 16)

        def gmlp_pe(pe):
            pe.wait_ge(S("ws_in"), 16)
            for g in range(GROUPS):
                last = pe.transpose(banks(0)[:, g * P:(g + 1) * P], ws_in[:, g, :], ident)
            last.then_inc(S("ws_turned"), 1)
            pe.wait_ge(S("ws_t"), 1)
            pe.wait_ge(S("v_normed"), NT)
            for g in range(GROUPS):
                for t in range(NT):
                    last = pe.matmul(psum[:, g // 2, (g % 2) * T + t * P:(g % 2) * T + (t + 1) * P],
                                     v_b[:, t, g * P:(g + 1) * P], ws_t[:, g, :], start=True, stop=True)
            last.then_inc(S("spatial"), 1)

        def gmlp_act(act, l):
            name = f"mix{l}"
            for j in range(8):
                cols_used(act, name, j)
                bank = psum[:, 4 + j % 2, :].rearrange("p (m t) -> p m t", m=2)
                dst = u_b[:, 2 * j:2 * j + 2, :] if j < 4 else v_b[:, :, (j - 4) * 256:(j - 3) * 256]
                act.activation(dst, bank, ACT.Gelu).then_inc(S("proj_evac"), 1)
                next_hi(act, name, j, 8)
            head_act(act, f"wo{l}")
            for t in range(NT):
                act.wait_ge(S("v_centred"), t + 1)
                if t:
                    act.wait_ge(S("v_sq"), t)
                act.activation(vc_sq, v_b[:, t, :], ACT.Square, accum_out=v_var[:, t:t + 1]).then_inc(S("v_sq"), 1)

        def gmlp_pool(pool):
            pool.wait_ge(S("v_sq"), NT)
            rstd(pool, v_rstd, v_var, 1.0 / D, EPS, S("v_rstd"))

        def gmlp_dve(dve, l, done):
            cols_dve(dve, l)
            dve.wait_ge(S("ws_turned"), 1)
            dve.tensor_tensor(ws_t, th_view(banks(0)), rep(mat("upto"), GROUPS), ALU.mult).then_inc(S("ws_t"), 1)
            dve.wait_ge(S("proj_evac"), proj_base(l) + 8)
            for t in range(NT):
                done(dve.reduce_sum(v_sum[:, t:t + 1], v_b[:, t, :], AX))
                done(dve.tensor_scalar(v_sum[:, t:t + 1], v_sum[:, t:t + 1], -1.0 / D, None, ALU.mult))
                dve.tensor_scalar(v_b[:, t, :], v_b[:, t, :], v_sum[:, t:t + 1], None, ALU.add).then_inc(S("v_centred"), 1)
            dve.wait_ge(S("b_rows"), 48)
            dve.wait_ge(S("v_rstd"), 1)
            for t in range(NT):
                done(dve.scalar_tensor_tensor(v_b[:, t, :], v_b[:, t, :], v_rstd[:, t:t + 1], ln_g, ALU.mult, ALU.mult))
                dve.tensor_tensor(v_b[:, t, :], v_b[:, t, :], ln_b, ALU.add).then_inc(S("v_normed"), 1)
            dve.wait_ge(S("spatial"), 1)
            for g in range(GROUPS):
                sv = psum[:, g // 2, (g % 2) * T:(g % 2 + 1) * T].rearrange("p (t n) -> p t n", t=NT)
                y = act_f[:, g, :].rearrange("p (t n) -> p t n", t=NT)
                done(dve.tensor_tensor(y, sv, rep(bs_b[:, g * P:(g + 1) * P], NT), ALU.add))
                dve.tensor_tensor(act_f[:, g, :], act_f[:, g, :], u_b[:, g, :], ALU.mult).then_inc(S("act_f"), 1)

        def ff_hb(l, which):
            return N_EXPERTS + (2 * l + which) * FF_STEPS

        def pre_cols(l, i):
            return lambda k: col("pre", (3 * l + i) * KD + k)

        def row_load(pool, r):
            if r == 2:
                pool.wait_ge(S("x_ready"), 2 * NT)
            elif r > 2:
                pool.wait_ge(S("x_half"), 2 * NT * (r - 2))
            pool.dma_start(rows[:, r % 2, :], a["rows"][r:r + 1, :].to_broadcast([P, D])).then_inc(S(f"row_loaded{r % 2}"), 16)

        @block.sync
        def _(sp):
            for j in range(ADA_FIRST):
                ada_load(sp, j)
            sp.wait_ge(S("ada_used"), 2)
            cols_load(sp, "w_in", lambda j: col_slab(a["w_in"], 256 * j), *range(10))
            sp.wait_ge(S("ada_used"), ADA_FIRST)
            load(sp, GD, PLAN.base["w_glu"][GD], a["w_glu"].rearrange("(k p) n -> p k n", p=P))
            w_out = lambda j: col_slab(a["w_out"], 256 * j)
            for j in range(ADA_FIRST, N_ADA):
                ada_load(sp, j)
            sp.wait_ge(S("ada_used"), N_ADA)
            cols_load(sp, "w_out", w_out, *range(4))

            def expert(name):
                def src(i):
                    w = a[name][bass.ds(i, 1), :, :] if not isinstance(i, int) else a[name][i:i + 1, :, :]
                    return w.rearrange("o (k p) n -> p (o k) n", p=P)
                return src

            def ff_src(w, l, c0):
                def src(i):
                    return w[l, :, bass.ds(i * HID + c0, HID)].rearrange("(k p) n -> p k n", p=P) if not isinstance(i, int) \
                        else w[l, :, i * HID + c0:(i + 1) * HID + c0].rearrange("(k p) n -> p k n", p=P)
                return src

            def ff_row(w, l):
                def src(i):
                    r = w[l, bass.ds(i * HID, HID), :] if not isinstance(i, int) else w[l, i * HID:(i + 1) * HID, :]
                    return r.rearrange("(j p) n -> p j n", p=P)
                return src

            def layer_ff(l, half_ff):
                wi, wo = a[f"{half_ff}_w_in"], a[f"{half_ff}_w_out"]
                return ff_src(wi, l, 0), ff_src(wi, l, D_FF), ff_row(wo, l)

            def mixer_src(l):
                w = a["b_w_in" if KINDS[l] == 1 else f"{'abc'[KINDS[l]]}_w_qkv"]
                return lambda j: col_slab(w[l // 3], 256 * order(l, j))

            experts = expert("w_gate"), expert("w_up"), expert("w_down")
            cols_load(sp, "moe", lambda j: experts[j](0), 0, 1)
            ff_load(sp, "moe", N_EXPERTS, *experts, lambda: cols_load(sp, "ff0a", lambda j: layer_ff(0, "ff1")[j](0), 0, 1))
            for l in range(LAYERS):
                ff_load(sp, f"ff{l}a", FF_STEPS, *layer_ff(l, "ff1"), lambda: cols_load(sp, f"mix{l}", mixer_src(l), 0, 1))
                cols_load(sp, f"mix{l}", mixer_src(l), *range(2, n_proj(l)))
                cols_load(sp, f"wo{l}", lambda j: col_slab(a[f"{'abc'[KINDS[l]]}_w_o"][l // 3], 256 * j), *range(4))
                cols_load(sp, f"ff{l}b", lambda j: layer_ff(l, "ff2")[j](0), 0, 1)
                ff_load(sp, f"ff{l}b", FF_STEPS, *layer_ff(l, "ff2"),
                        lambda: l < LAYERS - 1 and cols_load(sp, f"ff{l + 1}a", lambda j: layer_ff(l + 1, "ff1")[j](0), 0, 1))
            for t in range(NT):
                sp.wait_ge(S("x_half"), 2 * NT * (3 * LAYERS - 1) + 2 * t + 2)
                sp.dma_start(out[t * P:(t + 1) * P, :], x[:, t, :]).then_inc(S("stored"), 16)
            sp.wait_ge(S("stored"), 32)

        @block.gpsimd
        def _(pool):
            done = steps(pool, "pool_order")
            pool.dma_start(wsmall[:, :, 0:36], a["w_router"].rearrange("(k p) n -> p k n", p=P)).then_inc(S("narrow_loaded"), 16)
            pool.dma_start(wsmall[:, :, 36:44], a["w_in"][:, 2560:2568].rearrange("(k p) n -> p k n", p=P)).then_inc(S("narrow_loaded"), 16)
            pool.dma_start(first[:], a["first"]).then_inc(S("first_loaded"), 16)
            pool.wait_ge(S("half"), 1)
            pre_pool(pool, 0)
            s5_tables_pool(pool, done)
            pre_pool(pool, 1)
            row_load(pool, 0)
            row_load(pool, 1)
            final_pool(pool)
            pre_pool(pool, 2)
            for l in range(LAYERS):
                if KINDS[l] == 1:
                    gmlp_loads(pool)
                post_pool(pool, 3 * l, 0.5)
                pre_pool(pool, 3 + 3 * l)
                row_load(pool, 3 * l + 2)
                if KINDS[l] == 1:
                    gmlp_pool(pool)
                else:
                    bias_pool(pool, l)
                post_pool(pool, 3 * l + 1, 1.0)
                pre_pool(pool, 4 + 3 * l)
                row_load(pool, 3 * l + 3)
                post_pool(pool, 3 * l + 2, 0.5)
                if l < LAYERS - 1:
                    pre_pool(pool, 5 + 3 * l)
                    row_load(pool, 3 * l + 4)

        @block.scalar
        def _(act):
            act.dma_start(cols[:], a["cols"]).then_inc(S("cols_loaded"), 16)
            act.dma_start(mats[:].rearrange("p m n -> p (m n)"), a["mats"]).then_inc(S("mats_loaded"), 16)
            act.dma_start(x[:], a["x"].rearrange("(t p) n -> p t n", p=P)).then_inc(S("x_loaded"), 16)
            for part in (2, 5):
                gate = slice(part * D, (part + 1) * D)
                act.dma_start(mod[:, gate], a["b_ada"][:, gate].to_broadcast([P, D])).then_inc(S("bias_loaded"), 16)
            s5_param_act(act)
            pre_act(act, 0)
            act.wait_ge(S("pre_sums"), 2 * NT)
            act.dma_start(junk, a["s5_b"]).then_inc(S("s5_b_loaded"), 16)
            head_act(act, "w_in")
            pre_hi_act(act, 0, 0, n_f=0)
            w_in_act(act)
            s5_act(act)
            gdn_act(act)
            split_act(act, 1, 1)
            wo_act(act, "w_out", "moe")
            pre_act(act, 1)
            pre_hi_act(act, 1, 2, n_f=2)
            head_act(act, "moe", 1)
            router_act(act)
            act.activation(warm, warm, ACT.Silu)
            ff_act(act, "moe", N_EXPERTS, 0, "ff0a", gate_bank)
            final_act(act)
            for l in range(LAYERS):
                pre_act(act, 2 + 3 * l)
                pre_hi_act(act, 2 + 3 * l, act_index(l, 0), pre_cols(l, 0))
                ff_act(act, f"ff{l}a", FF_STEPS, ff_hb(l, 0), f"mix{l}")
                post_act(act, 3 * l, 0.5)
                pre_act(act, 3 + 3 * l)
                pre_hi_act(act, 3 + 3 * l, act_index(l, 1), pre_cols(l, 1))
                if KINDS[l] == 1:
                    gmlp_act(act, l)
                else:
                    qkv_act(act, l)
                    att_act(act, l)
                split_act(act, act_index(l, 2), f_index(l))
                wo_act(act, f"wo{l}", f"ff{l}b")
                post_act(act, 3 * l + 1, 1.0)
                pre_act(act, 4 + 3 * l)
                pre_hi_act(act, 4 + 3 * l, act_index(l, 3), pre_cols(l, 2))
                head_act(act, f"ff{l}b", 1)
                ff_act(act, f"ff{l}b", FF_STEPS, ff_hb(l, 1), f"ff{l + 1}a" if l < LAYERS - 1 else None)
                post_act(act, 3 * l + 2, 0.5)

        @block.vector
        def _(dve):
            done = steps(dve, "dve_order")
            dve.wait_ge(S("cols_loaded"), 16)
            dve.wait_ge(S("mats_loaded"), 16)
            s5_param_dve(dve, done)
            for j in range(ADA_FIRST):
                ada_dve(dve, done, j)
            pre_diag_dve(dve, 0)
            mod_dve(dve, done, 0, "norm1")
            head_dve(dve, "w_in", 0)
            pre_dve(dve, 0, 0, lambda k: modc[:, 1, k:k + 1], lambda k: modc[:, 0, k:k + 1])
            head_dve(dve, "w_in", 1)
            w_in_dve(dve, done)
            s5_dve(dve, done)
            gdn_dve(dve, done)
            split_dve(dve, 1)
            wo_dve(dve, "w_out", "moe")
            residual_dve(dve, done, 1, PLAN.base["w_out"][1] + 2, 2, False)
            pre_diag_dve(dve, 1)
            pre_dve(dve, 1, 2, lambda k: modc[:, 3, k:k + 1], lambda k: modc[:, 2, k:k + 1])
            dve.wait_ge(S("first_loaded"), 16)
            head_dve(dve, "moe", 1)
            router_dve(dve, done)
            ff_dve(dve, "moe", N_EXPERTS, 0, "ff0a", gate_bank)
            residual_dve(dve, done, GD, PLAN.base["moe"][GD] + N_EXPERTS, 5, True)
            final_dve(dve)
            for l in range(LAYERS):
                pre_diag_dve(dve, 2 + 3 * l)
                pre_dve(dve, 2 + 3 * l, act_index(l, 0), pre_cols(l, 0))
                ff_dve(dve, f"ff{l}a", FF_STEPS, ff_hb(l, 0), f"mix{l}")
                post_dve(dve, 3 * l, 3 * l + 1)
                pre_diag_dve(dve, 3 + 3 * l)
                pre_dve(dve, 3 + 3 * l, act_index(l, 1), pre_cols(l, 1))
                if KINDS[l] == 1:
                    gmlp_dve(dve, l, done)
                else:
                    cols_dve(dve, l)
                    att_dve(dve, l, done)
                split_dve(dve, act_index(l, 2))
                wo_dve(dve, f"wo{l}", f"ff{l}b")
                post_dve(dve, 3 * l + 1, 3 * l + 2)
                pre_diag_dve(dve, 4 + 3 * l)
                pre_dve(dve, 4 + 3 * l, act_index(l, 3), pre_cols(l, 2))
                head_dve(dve, f"ff{l}b", 1)
                ff_dve(dve, f"ff{l}b", FF_STEPS, ff_hb(l, 1), f"ff{l + 1}a" if l < LAYERS - 1 else None)
                post_dve(dve, 3 * l + 2, 3 * l + 3)

        @block.tensor
        def _(pe):
            pe.wait_ge(S("mats_loaded"), 16)
            pe.wait_ge(S("c_act"), 1)
            for j in range(ADA_FIRST):
                ada_pe(pe, j)
            pre_pe(pe, 0)
            w_in_pe(pe)
            s5_pe(pe)
            gdn_pe(pe)
            wo_pe(pe, "w_out", 1)
            pre_pe(pe, 1)
            router_pe(pe)
            ff_pe(pe, "moe", N_EXPERTS, 0, 2, gate=gate_row)
            for l in range(LAYERS):
                pre_pe(pe, 2 + 3 * l)
                ff_pe(pe, f"ff{l}a", FF_STEPS, ff_hb(l, 0), act_index(l, 0), 3 * l)
                pre_pe(pe, 3 + 3 * l)
                nt = 4 if KINDS[l] == 1 else 8
                cols_pe(pe, f"mix{l}", 0, nt, "t", proj_base(l), 4 * act_index(l, 1))
                cols_pe(pe, f"mix{l}", nt, nt + 4, "n", proj_base(l))
                if KINDS[l] == 1:
                    gmlp_pe(pe)
                else:
                    att_pe(pe, l)
                wo_pe(pe, f"wo{l}", act_index(l, 2), post=True)
                pre_pe(pe, 4 + 3 * l)
                ff_pe(pe, f"ff{l}b", FF_STEPS, ff_hb(l, 1), act_index(l, 3), 3 * l + 2)


def kernel(**inputs):
    import concourse.bacc as bacc
    from concourse.bass_utils import run_bass_kernel_spmd

    v = {k: np.asarray(a) for k, a in inputs.items()}

    def chunks(row):
        return row.reshape(-1, P).T

    mats, alibi, first = constants()

    def states(m):
        return m.reshape(S5_TILES, P).T

    def inputs_of_state(m):
        z = np.zeros((CS5, 4, 2, 16, 2, 64), m.dtype)
        b = m.reshape(CS5, 4, 2, 64, 16)
        for g in range(2):
            z[:, :, g, :, g, :] = b[:, :, g].transpose(0, 1, 3, 2)
        return z.reshape(CS5, P, P).transpose(1, 0, 2).reshape(P, -1)

    def outputs_of_state(m):
        z = np.zeros((2, 64, S5_TILES, 2, 16), m.dtype)
        b = m.reshape(S5_TILES, 2, 16, 64)
        for g in range(2):
            z[g, :, :, g, :] = b[:, g].transpose(2, 0, 1)
        return z.reshape(P, -1)

    def over_all(row):
        return np.broadcast_to(row.reshape(1, -1), (P, row.size))

    pre = v["norm_g_2"][:, [0, 2, 4], :].reshape(-1, P).T
    lam = v["c_lambda_2"][0]
    parts = {
        "lam_re": states(v["lam_re"][0]), "lam_im": states(v["lam_im"][0]),
        "log_step": states(np.repeat(v["log_step"][0][:, None], 64, 1)),
        "s5_d": chunks(v["s5_d"][0]), "b_glu": chunks(v["b_glu"][0]),
        "conv_w": v["conv_w"][0].reshape(CONV, 12, P).transpose(2, 1, 0).reshape(P, -1),
        "norm1": chunks(v["norm1_g"][0]), "norm2": chunks(v["norm2_g"][0]), "pre": pre,
        "gdn_g": chunks(v["gdn_norm_g"][0]), "subln": chunks(v["c_subln_g_2"][0]), "c": chunks(v["c"][0]),
        "dt_bias": over_all(np.repeat(v["dt_bias"][0], NT)), "a_log": over_all(np.repeat(v["a_log"][0], NT)),
        "b_ada": v["b_ada"].reshape(6, KD, P)[[0, 1, 3, 4]].transpose(2, 0, 1).reshape(P, -1),
        "lam_c": np.concatenate([lam.T, np.zeros((P - lam.shape[1], 4), lam.dtype)], 0),
        "c_re": outputs_of_state(v["s5_c_re"][0]), "c_im": outputs_of_state(v["s5_c_im"][0]),
    }
    cols = np.zeros((P, NCOLS), np.float32)
    for name, part in parts.items():
        cols[:, COLS[name][0]:COLS[name][1]] = part
    rel = v["a_rel_bias_2"][:, :, np.clip(255 - np.arange(512), -128, 128) + 128]
    rows = np.concatenate([v["normf_g"][None], v["norm_g_2"][:, [1, 3, 5], :].reshape(-1, D)], 0)
    arrays = {
        "x": v["x"][0], "w_ada": v["w_ada"][0], "b_ada": v["b_ada"], "w_in": v["w_in"][0], "w_glu": v["w_glu"][0],
        "w_out": v["w_out"][0], "w_router": np.concatenate([v["w_router_grp"][0], v["w_router_exp"][0]], 1),
        "w_gate": v["w_gate"][0], "w_up": v["w_up"][0], "w_down": v["w_down"][0],
        "ff1_w_in": v["ff1_w_in_2"], "ff1_w_out": v["ff1_w_out_2"], "ff2_w_in": v["ff2_w_in_2"], "ff2_w_out": v["ff2_w_out_2"],
        "a_w_qkv": v["a_w_qkv_2"], "a_w_o": v["a_w_o_2"], "b_w_in": v["b_w_in_2"], "b_w_o": v["b_w_o_2"],
        "c_w_qkv": v["c_w_qkv_2"], "c_w_o": v["c_w_o_2"], "b_w_s": v["b_w_s_2"][0], "b_ln_g": v["b_ln_g_2"], "b_ln_b": v["b_ln_b_2"],
        "b_b_s": v["b_b_s_2"].reshape(1, -1), "cols": cols, "rows": rows, "rel_rows": rel.reshape(-1, 512), "mats": mats,
        "alibi": alibi, "first": first,
        "s5_b": np.concatenate([inputs_of_state(v["s5_b_re"][0]), inputs_of_state(v["s5_b_im"][0])], 1),
    }
    nc = bacc.Bacc("TRN2", target_bir_lowering=False, num_devices=1)
    args, feeds = {}, {}
    for name, arr in arrays.items():
        arr = np.ascontiguousarray(arr)
        feeds[f"in_{name}"] = arr
        args[name] = nc.dram_tensor(f"in_{name}", arr.shape, mybir.dt.from_np(arr.dtype), kind="ExternalInput").ap()
    result = nc.dram_tensor("result", (T, D), F32, kind="ExternalOutput").ap()
    build(nc, args, result)
    r = run_bass_kernel_spmd(nc, [feeds], core_ids=[0])
    return r.results[0]["result"].reshape(1, T, D)
```

```python
import math
from contextlib import ExitStack

import numpy as np

import concourse.bass as bass
from concourse import mybir

F32 = mybir.dt.float32
F32R = mybir.dt.float32r
ALU = mybir.AluOpType
ACT = mybir.ActivationFunctionType
AX = mybir.AxisListType.X

P = 128
D = 1024
T = 256
KD = D // P
NT = T // P
EPS = 1e-6
N_EXPERTS = 32
N_GROUPS = 4
PER_GROUP = 8
D_FF = 2816
HID = 256
FF_STEPS = D_FF // HID
LAYERS = 4
KINDS = [i % 3 for i in range(LAYERS)]
D_S5 = 512
CS5 = D_S5 // P
HEADS = 4
DK = 128
TH = HEADS * NT
CONV = 4
S5_TILES = 16
LEVELS = 7
LAMBDA_INIT = 0.8 - 0.6 * math.exp(-0.3 * 2)
GA, GU, GD = 0, 1, 2

COLS = {}


def _cols(spec):
    at = 0
    for name, n in spec:
        COLS[name] = (at, at + n)
        at += n
    return at


NCOLS = _cols([("lam_re", 16), ("lam_im", 16), ("log_step", 16), ("s5_d", CS5), ("b_glu", CS5),
               ("conv_w", 12 * CONV), ("norm1", KD), ("norm2", KD), ("gdn_g", 1),
               ("subln", 1), ("c", KD), ("dt_bias", TH), ("a_log", TH), ("lam_c", 4), ("b_ada", 4 * KD), ("ln_g", KD), ("ln_b", KD),
               ("c_re", S5_TILES * 32), ("c_im", S5_TILES * 32)])

MATS = {name: i for i, name in enumerate(["ident", "upto", "ones", "flip"] + [f"level{k}" for k in range(LEVELS)])}


def constants():
    i, j = np.arange(P)[:, None], np.arange(P)[None, :]
    mats = [i == j, i <= j, np.ones((P, P), bool), i + j == P - 1]
    for k in range(LEVELS):
        s = 1 << k
        mats.append((i // (2 * s) == j // (2 * s)) & (i // s % 2 == 1) & (j // s % 2 == 0))
    mats = np.stack(mats, 1).astype(np.float32).reshape(P, -1)
    slopes = (2.0 ** (-8.0 * (np.arange(8, dtype=np.float32) + 1.0) / 8)).astype(np.float32)
    q = np.arange(P)
    k1 = np.arange(T)
    dist = np.abs(q[:, None] + P - k1).astype(np.float32)
    barred = k1 >= ((q[:, None] + P) // 64 + 1) * 64
    alibi = np.where(barred, np.float32(-1e30), -slopes[:, None, None] * dist)
    alibi = np.repeat(alibi, 2, 0).transpose(1, 0, 2)
    first = np.tile(np.array([8, 7, 6, 5, 4, 3, 2, 1], np.float32), (P, 1))
    return mats, np.ascontiguousarray(alibi.astype(np.float32)), first


class Plan:

    def __init__(self):
        self.base = {}
        self.order = {}
        self.at = [0, 0, 0]

    def add(self, name, *counts):
        self.base[name] = tuple(self.at)
        self.at = [a + n for a, n in zip(self.at, counts)]

    def add_order(self, name, slots):
        self.order[name] = tuple(slots)
        self.add(name, *(self.order[name].count(s) for s in range(3)))

    def slab_at(self, name, j):
        slots = self.order.get(name, (0, 1))
        return slots[j], self.base[name][slots[j]] + slots[:j].count(slots[j])


PLAN = Plan()
PLAN.add_order("w_in", (0, 1) * 5)
PLAN.add("w_glu", 0, 0, 1)
PLAN.add_order("w_out", (0, 1) * 2)
PLAN.add("moe", N_EXPERTS, N_EXPERTS, N_EXPERTS)
for _l in range(LAYERS):
    PLAN.add(f"ff{_l}a", FF_STEPS, FF_STEPS, FF_STEPS)
    PLAN.add_order(f"mix{_l}", (0, 1, 2, 0) + (1, 0) * (2 if KINDS[_l] == 1 else 4))
    PLAN.add_order(f"wo{_l}", (1, 0, 1, 2))
    PLAN.add(f"ff{_l}b", FF_STEPS, FF_STEPS, FF_STEPS)


def build(nc, a, out):
    ctx = ExitStack()
    sems = {}

    def S(name):
        if name not in sems:
            sems[name] = ctx.enter_context(nc.semaphore(name))
        return sems[name]

    def sb(name, shape, dt=F32):
        return ctx.enter_context(nc.sbuf_tensor(name, shape, dt))

    with ctx:
        raw = [sb(f"raw{s}", [P, 2048]) for s in range(3)]
        whi = [sb(f"whi{s}", [P, 2048], F32R) for s in range(3)]
        wlo = [sb(f"wlo{s}", [P, 2048], F32R) for s in range(3)]
        x = sb("x", [P, NT, D])
        act_f = sb("act_f", [P, KD, T])
        act_hi = sb("act_hi", [P, KD, T], F32R)
        act_lo = sb("act_lo", [P, KD, T], F32R)
        h_hi = sb("h_hi", [P, 2, T], F32R)
        h_lo = sb("h_lo", [P, 2, T], F32R)
        tail_h_hi = sb("tail_h_hi", [P, 2, T], F32R)
        tail_h_lo = sb("tail_h_lo", [P, 2, T], F32R)
        scratch = sb("scratch", [P, 4096])
        junk = scratch[:, 0:1024]
        rows = scratch[:, 1024:3072].rearrange("p (s n) -> p s n", s=2)
        sil = scratch[:, 3072:3584]
        h_raw = scratch[:, 3584:4096]
        mats = sb("mats", [P, len(MATS), P])
        cols = sb("cols", [P, NCOLS])
        modc = sb("modc", [P, 4, KD])
        first = sb("first", [P, PER_GROUP])
        small = sb("small", [P, 512])
        half = sb("half", [P, 8])
        diag = sb("diag", [P, NT, P])
        arena = sb("arena", [P, 16384])
        psum = ctx.enter_context(nc.psum_tensor("psum", [P, 8, 512], F32))
        acc = psum[:, 0:4, :]
        gu = psum[:, 4:8, :]

        def mat(name):
            return mats[:, MATS[name], :]

        def col(name, k=0, n=1):
            at = COLS[name][0] + k
            return cols[:, at:at + n]

        def area(block, n, blocks=1):
            return arena[:, 1024 * block:1024 * block + n]

        ident = mat("ident")

        raw_loaded = [S(f"raw_loaded{s}") for s in range(3)]
        hi_ready = [S(f"hi_ready{s}") for s in range(3)]
        lo_ready = [S(f"lo_ready{s}") for s in range(3)]
        slab_used = [S(f"slab_used{s}") for s in range(3)]

        block = ctx.enter_context(nc.Block())

        def col_slab(w, c0):
            return w[:, c0:c0 + 256].rearrange("(k p) n -> p k n", p=P)

        def load(sp, s, n, src):
            if not (isinstance(n, int) and n == 0):
                sp.wait_ge(lo_ready[s], n)
            k = src.shape[1]
            sp.dma_start(raw[s][:, :k * src.shape[2]].rearrange("p (k n) -> p k n", k=k), src).then_inc(raw_loaded[s], 16)

        def split_hi(act, s, n):
            act.wait_ge(raw_loaded[s], n * 16 + 16)
            if not (isinstance(n, int) and n == 0):
                act.wait_ge(slab_used[s], n)
            act.activation(whi[s][:], raw[s][:], ACT.Copy).then_inc(hi_ready[s], 1)

        def split_lo(dve, s, n):
            dve.wait_ge(hi_ready[s], n + 1)
            dve.tensor_tensor(wlo[s][:], raw[s][:], whi[s][:].bitcast(F32), ALU.subtract).then_inc(lo_ready[s], 1)

        def slab_views(s, k):
            return (whi[s][:].rearrange("p (k n) -> p k n", k=k), wlo[s][:].rearrange("p (k n) -> p k n", k=k))

        def three(pe, out_ap, lhs, rhs, first, last):
            pe.matmul(out_ap, lhs[0], rhs[0], start=first, stop=False)
            pe.matmul(out_ap, lhs[0], rhs[1], start=False, stop=False)
            return pe.matmul(out_ap, lhs[1], rhs[0], start=False, stop=last)

        def proj_t(pe, s, bank, act_k=KD, m0=0, ms=2, k_cols=256, act0=None):
            hi, lo = slab_views(s, 2048 // k_cols)
            for m in range(ms):
                for k in range(act_k):
                    if act0 is not None and m == 0 and k % 2 == 0:
                        pe.wait_ge(S("act_lo"), act0 + 2 + k // 2 + 1)
                    c = (m0 + m) * P
                    last = three(pe, psum[:, bank, m * T:(m + 1) * T], (hi[:, k, c:c + P], lo[:, k, c:c + P]),
                                 (act_hi[:, k, :], act_lo[:, k, :]), k == 0, k == act_k - 1)
            return last

        def quarter_of(t, k):
            return 0 if t or k % 2 else k // 2 + 1

        def piece_of(t, k):
            return sum((p[0], p[1]) <= (t, k) for p in PIECES) if (t, k) in [(p[0], p[1]) for p in PIECES] else 0

        def proj_n(pe, s, out_of, first_done=None, act0=None, part_of=quarter_of, tiles=(0, 1)):
            hi, lo = slab_views(s, KD)
            for t in tiles:
                for k in range(KD):
                    if act0 is not None and part_of(t, k):
                        pe.wait_ge(S("act_lo"), act0 + part_of(t, k))
                    last = three(pe, out_of(t), (act_hi[:, k, t * P:(t + 1) * P], act_lo[:, k, t * P:(t + 1) * P]),
                                 (hi[:, k, :], lo[:, k, :]), k == 0, k == KD - 1)
                if first_done and t == 0:
                    last.then_inc(first_done, 1)
            return last

        ss_pre, ss_post = small[:, 0:2 * NT], small[:, 16:16 + 2 * NT]
        r_pre, r_post = small[:, 8:8 + NT], small[:, 24:24 + NT]
        HALF = D // 2

        TILES = tuple(range(NT))

        def pre_act(act, n, tiles=TILES, turn=False):
            for t in tiles:
                for h in range(2):
                    if n == 0:
                        act.wait_ge(S("x_loaded"), 16)
                    elif n <= 2:
                        act.wait_ge(S("x_ready"), NT * (n - 1) + t + 1)
                    else:
                        act.wait_ge(S("x_half"), 2 * NT * (n - 3) + 2 * t + h + 1)
                    if n:
                        act.wait_ge(S("pre_rstd"), NT * (n - 1) + t + 1)
                    if turn:
                        act.wait_ge(S("post_sums"), 2 * NT * (n - 3) + 2 * t + h + 1)
                    elif t:
                        act.wait_ge(S("pre_sums"), 2 * NT * n + h + 1)
                    elif n == 1:
                        act.wait_ge(S("pre_sums"), 2 * NT)
                    elif n == 2:
                        act.wait_ge(S("final_sums"), NT)
                    elif n > 2:
                        act.wait_ge(S("post_sums"), 2 * NT * (n - 2))
                    act.activation(junk[:, h * HALF:(h + 1) * HALF], x[:, t, h * HALF:(h + 1) * HALF], ACT.Square,
                                   scale=D ** -0.5, accum_out=ss_pre[:, 2 * t + h:2 * t + h + 1]).then_inc(S("pre_sums"), 1)

        pool_steps = [0]

        def power(pool, out_ap, ins, sem):
            ins.then_inc(S("pool_step"), 1)
            pool_steps[0] += 1
            pool.wait_ge(S("pool_step"), pool_steps[0])
            pool.tensor_tensor(out_ap, out_ap, half[:, 0:out_ap.shape[1]], ALU.pow).then_inc(sem, 1)

        def rstd(pool, out_ap, in_ap, scale, eps, sem):
            power(pool, out_ap, pool.tensor_scalar(out_ap, in_ap, scale, eps, ALU.mult, ALU.add), sem)

        def rstd_of_halves(pool, out_ap, means, eps, sem):
            power(pool, out_ap, pool.tensor_scalar(out_ap, means[:, 0:1], means[:, 1:2], eps, ALU.add, ALU.add), sem)

        def pre_pool(pool, n, tiles=TILES):
            for t in tiles:
                pool.wait_ge(S("pre_sums"), 2 * NT * n + 2 * t + 2)
                if n:
                    pool.wait_ge(S("normed"), 2 * NT * (n - 1) + 2 * t + 2)
                rstd_of_halves(pool, r_pre[:, t:t + 1], ss_pre[:, 2 * t:2 * t + 2], EPS, S("pre_rstd"))

        PIECES = ((0, 0, 4, 4), (0, 4, 4, 5), (1, 0, 2, 6), (1, 2, 2, 7), (1, 4, 2, 0), (1, 6, 2, 1))
        N_PIECES = len(PIECES)

        gain_row = act_f[:, 0:4, :].rearrange("p k t -> p (k t)")

        def gain_load(pool, n, sem, count):
            pool.wait_ge(S(sem), count)
            pool.dma_start(gain_row, a["gains"][n - 2:n - 1, :].to_broadcast([P, D])).then_inc(S("gain_loaded"), 16)

        def act_before(n_act):
            first = [0, N_PIECES, N_PIECES + 4]
            if n_act < 3:
                return first[n_act]
            l, i = divmod(n_act - 3, 4)
            return 2 * N_PIECES + 4 + l * (3 * N_PIECES + 4) + (0, N_PIECES, 2 * N_PIECES, 2 * N_PIECES + 4)[i]

        def keep_clock(pe, bank, count):
            for _ in range(count):
                pe.matmul(psum[:, bank, 0:P], ident, ident, start=True, stop=True)

        def pre_pe(pe, n, tiles=TILES):
            if n >= 2 and 0 in tiles:
                keep_clock(pe, 7, 22 if n == 2 else 12)
            for t, k0, nk, bank in PIECES:
                if t not in tiles:
                    continue
                pe.wait_ge(S("normed"), 2 * NT * n + 2 * t + k0 // 4 + 1)
                for c in range(nk):
                    k = k0 + c
                    last = pe.transpose(psum[:, bank, c * P:(c + 1) * P], normed_rows(n, t)[:, k * P:(k + 1) * P], ident)
                last.then_inc(S("transposed"), 1)

        def act_piece(ap, piece):
            t, k0, nk, _ = piece
            return ap[:, k0:k0 + nk, t * P:(t + 1) * P]

        def pre_rows_dve(dve, n, tiles=TILES):
            for t in tiles:
                dve.wait_ge(S("pre_rstd"), NT * n + t + 1)
                for h in range(2):
                    hs = slice(h * HALF, (h + 1) * HALF)
                    if n < 2:
                        ins = dve.tensor_scalar(normed_rows(n, t)[:, hs], x[:, t, hs], r_pre[:, t:t + 1], None, ALU.mult)
                    else:
                        dve.wait_ge(S("gain_loaded"), 16 * (n - 1))
                        ins = dve.scalar_tensor_tensor(normed_rows(n, t)[:, hs], x[:, t, hs], r_pre[:, t:t + 1], gain_row[:, hs],
                                                       ALU.mult, ALU.mult)
                    ins.then_inc(S("normed"), 1)

        def pre_dve(dve, n, n_act, tiles=TILES):
            for q, piece in enumerate(PIECES):
                if piece[0] not in tiles:
                    continue
                dve.wait_ge(S("act_hi"), act_before(n_act) + q + 1)
                _, _, nk, bank = piece
                whole = act_piece(act_f, piece) if n < 2 else th_view(psum[:, bank, 0:nk * P])
                dve.tensor_tensor(act_piece(act_lo, piece), whole, act_piece(act_hi, piece).bitcast(F32), ALU.subtract)\
                   .then_inc(S("act_lo"), 1)

        def pre_hi_act(act, n, n_act, tiles=TILES):
            for q, piece in enumerate(PIECES):
                if piece[0] not in tiles:
                    continue
                act.wait_ge(S("transposed"), N_PIECES * n + q + 1)
                _, _, nk, bank = piece
                act.activation(act_piece(act_hi, piece), th_view(psum[:, bank, 0:nk * P]), ACT.Copy).then_inc(S("act_hi"), 1)

        def pre_mod_act(act, n, n_act, n_f, scales, shifts):
            def modulated(q):
                act.wait_ge(S("transposed"), N_PIECES * n + q + 1)
                t, k0, nk, bank = PIECES[q]
                for c in range(nk):
                    k = k0 + c
                    last = act.activation(act_f[:, k, t * P:(t + 1) * P], psum[:, bank, c * P:(c + 1) * P], ACT.Identity,
                                          bias=shifts(k), scale=scales(k))
                last.then_inc(S("act_f"), nk // 2)

            f_count = 8 * n_f
            modulated(0)
            for q, piece in enumerate(PIECES):
                if q + 1 < N_PIECES:
                    modulated(q + 1)
                f_count += piece[2] // 2
                act.wait_ge(S("act_f"), f_count)
                act.activation(act_piece(act_hi, piece), act_piece(act_f, piece), ACT.Copy).then_inc(S("act_hi"), 1)

        def split_dve(dve, n_act):
            for q in range(4):
                dve.wait_ge(S("act_hi"), act_before(n_act) + q + 1)
                dve.tensor_tensor(act_lo[:, 2 * q:2 * q + 2, :], act_f[:, 2 * q:2 * q + 2, :],
                                  act_hi[:, 2 * q:2 * q + 2, :].bitcast(F32), ALU.subtract).then_inc(S("act_lo"), 1)

        def split_act(act, n_act, n_f):
            for q in range(4):
                act.wait_ge(S("act_f"), 8 * n_f + 2 * q + 2)
                act.activation(act_hi[:, 2 * q:2 * q + 2, :], act_f[:, 2 * q:2 * q + 2, :], ACT.Copy)\
                   .then_inc(S("act_hi"), 1)

        def xn(t):
            return arena[:, 14336 + t * D:14336 + (t + 1) * D]

        def normed_rows(n, t):
            return xn(t) if n else scratch[:, (1 + t) * D:(2 + t) * D]

        def steps(eng, name):
            count = [0]

            def done(ins):
                ins.then_inc(S(name), 1)
                count[0] += 1
                eng.wait_ge(S(name), count[0])
            return done

        def bc(ap, n):
            return ap.unsqueeze(2).to_broadcast([P, ap.shape[1], n])

        def th_view(ap):
            return ap.rearrange("p (e n) -> p e n", n=P)

        def rep(ap, m):
            return ap.unsqueeze(1).to_broadcast([P, m, ap.shape[1]])

        def y_before(n):
            return 5 + 8 * (n // 3) + (0, 3, 5)[n % 3]

        def y_wait(eng, n, t, h):
            l, part = divmod(n, 3)
            if part == 1:
                if t:
                    s, i = PLAN.slab_at(f"wo{l}", 2 * h + 1)
                    eng.wait_ge(slab_used[s], i + 1)
                else:
                    eng.wait_ge(S("y_ready"), y_before(n) + h + 1)
            elif t and h:
                eng.wait_ge(slab_used[GD], PLAN.base[f"ff{l}{'ab'[part // 2]}"][GD] + FF_STEPS)
            else:
                eng.wait_ge(S("y_ready"), y_before(n) + 2 * t + h + 1)

        def post_act(act, n, f, tiles=TILES, turn=False):
            for t in tiles:
                for h in range(2):
                    y_wait(act, n, t, h)
                    if n:
                        act.wait_ge(S("post_rstd"), NT * (n - 1) + t + 1)
                    if t and turn:
                        act.wait_ge(S("pre_sums"), 2 * NT * (n + 3) + h + 1)
                    elif t:
                        act.wait_ge(S("post_sums"), 2 * NT * n + h + 1)
                    else:
                        act.wait_ge(S("pre_sums"), 2 * NT * (n + 3))
                    act.activation(junk[:, h * HALF:(h + 1) * HALF], acc[:, 2 * t + h, :], ACT.Square, scale=D ** -0.5 / f,
                                   accum_out=ss_post[:, 2 * t + h:2 * t + h + 1]).then_inc(S("post_sums"), 1)

        def post_pool(pool, n, f, tiles=TILES):
            for t in tiles:
                pool.wait_ge(S("post_sums"), 2 * NT * n + 2 * t + 2)
                if n:
                    pool.wait_ge(S("x_half"), 2 * NT * (n - 1) + 2 * t + 2)
                rstd_of_halves(pool, r_post[:, t:t + 1], ss_post[:, 2 * t:2 * t + 2], EPS / (f * f), S("post_rstd"))

        def post_gain(dve, n, row, t, h):
            if n:
                dve.wait_ge(S("x_half"), 2 * NT * n)
            dve.wait_ge(S(f"row_loaded{row % 2}"), 16 * (row // 2 + 1))
            dve.wait_ge(S("post_sums"), 2 * NT * n + 2 * t + h + 1)
            hs = slice(h * HALF, (h + 1) * HALF)
            dve.tensor_tensor(xn(t)[:, hs], acc[:, 2 * t + h, :], rows[:, row % 2, hs], ALU.mult).then_inc(S("y_gained"), 1)

        def post_x(dve, n, t):
            dve.wait_ge(S("y_gained"), 2 * NT * n + 2 * t + 2)
            dve.wait_ge(S("post_rstd"), NT * n + t + 1)
            for h in range(2):
                hs = slice(h * HALF, (h + 1) * HALF)
                dve.scalar_tensor_tensor(x[:, t, hs], xn(t)[:, hs], r_post[:, t:t + 1], x[:, t, hs], ALU.mult, ALU.add)\
                   .then_inc(S("x_half"), 1)

        def post_dve(dve, n, row):
            for t in range(NT):
                for h in range(2):
                    post_gain(dve, n, row, t, h)
                post_x(dve, n, t)

        def turn_act(act, n, f, n_act):
            post_act(act, n, f, (0,), True)
            pre_act(act, n + 3, (0,), True)
            post_act(act, n, f, (1,), True)
            pre_hi_act(act, n + 3, n_act, (0,))
            pre_act(act, n + 3, (1,), True)
            pre_hi_act(act, n + 3, n_act, (1,))
            head_act(act, f"mix{n // 3}", 2)

        def turn_pool(pool, n, f):
            for t in range(NT):
                post_pool(pool, n, f, (t,))
                pre_pool(pool, n + 3, (t,))

        def turn_dve(dve, n, row, n_act):
            post_gain(dve, n, row, 0, 0)
            post_gain(dve, n, row, 0, 1)
            post_x(dve, n, 0)
            pre_rows_dve(dve, n + 3, (0,))
            post_gain(dve, n, row, 1, 0)
            pre_dve(dve, n + 3, n_act, (0,))
            post_gain(dve, n, row, 1, 1)
            post_x(dve, n, 1)
            pre_rows_dve(dve, n + 3, (1,))
            pre_dve(dve, n + 3, n_act, (1,))
            head_dve(dve, f"mix{n // 3}", 2)

        gate_bank = psum[:, 6, 0:T]
        lg = arena[:, 0:72].rearrange("p (t n) -> p t n", t=NT)
        comb = arena[:, 128:192].rearrange("p (t n) -> p t n", t=NT)
        sel4 = arena[:, 256:320].rearrange("p (t e g) -> p t e g", t=NT, e=PER_GROUP)
        tail_hi, tail_lo = (ap[:].rearrange("p k t -> p (k t)") for ap in (act_hi, act_lo))

        def ff_load(sp, name, n, g_src, u_src, d_src, nxt):
            b = PLAN.base[name]
            with sp.Fori(1, n) as i:
                load(sp, GA, i + b[GA], g_src(i))
                load(sp, GU, i + b[GU], u_src(i))
                load(sp, GD, i + (b[GD] - 1), d_src(i - 1))
            nxt()
            load(sp, GD, b[GD] + n - 1, d_src(n - 1))

        def step_banks(i, gates):
            return (6, 7) if gates is None and isinstance(i, int) and i == 0 else (4, 5)

        def silu_step(act, b, hb, i, gates=None):
            act.wait_ge(slab_used[GU], i + (b[GU] + 1))
            act.wait_ge(S("h_raw"), i + hb)
            act.activation(sil, psum[:, step_banks(i, gates)[0], :], ACT.Silu).then_inc(S("sil"), 1)

        def h_hi_step(act, b, hb, i):
            act.wait_ge(S("h_raw"), i + (hb + 1))
            act.wait_ge(slab_used[GD], i + b[GD])
            act.activation(h_hi[:].rearrange("p m t -> p (m t)"), h_raw, ACT.Copy).then_inc(S("h_hi"), 1)

        def ff_act(act, name, n, hb, nxt, gates=None):
            b = PLAN.base[name]

            def step(i):
                split_hi(act, GA, i + b[GA])
                silu_step(act, b, hb, i - 1, gates)
                split_hi(act, GU, i + b[GU])
                h_hi_step(act, b, hb, i - 1)
                split_hi(act, GD, i + (b[GD] - 1))
            step(1)
            with act.Fori(2, n) as i:
                step(i)
            head_act(act, nxt, 0)
            silu_step(act, b, hb, n - 1, gates)
            act.wait_ge(raw_loaded[GD], 16 * (b[GD] + n))
            act.activation(tail_hi, raw[GD][:], ACT.Copy).then_inc(hi_ready[GD], 1)
            act.wait_ge(S("h_raw"), hb + n)
            act.activation(tail_h_hi[:].rearrange("p m t -> p (m t)"), h_raw, ACT.Copy).then_inc(S("h_hi"), 1)
            head_act(act, nxt, 1)

        def gate_diag(dve, w):
            dve.tensor_tensor(diag[:], rep(ident, NT), w.to_broadcast([P, NT, P]), ALU.mult).then_inc(S("gate_diag"), 1)

        def h_step(dve, b, hb, i, gates):
            dve.wait_ge(S("sil"), i + (hb + 1))
            dve.wait_ge(S("h_lo"), i + hb)
            if gates is None:
                dve.tensor_tensor(h_raw, sil, psum[:, step_banks(i, gates)[1], :], ALU.mult).then_inc(S("h_raw"), 1)
            else:
                dve.tensor_tensor(h_raw, sil, psum[:, step_banks(i, gates)[1], :], ALU.mult).then_inc(S("h_ungated"), 1)
                dve.wait_ge(S("h_ungated"), i + 1)
                v = h_raw.rearrange("p (m t) -> p m t", m=2)
                dve.wait_ge(S("gate_row"), i + 1)
                dve.tensor_tensor(v, v, rep(gates, 2), ALU.mult).then_inc(S("h_raw"), 1)
                if not (isinstance(i, int) and i == N_EXPERTS - 1):
                    gate_diag(dve, comb[:, :, bass.ds(i + 1, 1)])

        def h_lo_step(dve, b, hb, i):
            dve.wait_ge(S("h_hi"), i + (hb + 1))
            dve.tensor_tensor(h_lo[:].rearrange("p m t -> p (m t)"), h_raw,
                              h_hi[:].rearrange("p m t -> p (m t)").bitcast(F32), ALU.subtract).then_inc(S("h_lo"), 1)

        def ff_dve(dve, name, n, hb, nxt, gates=None):
            b = PLAN.base[name]

            def step(i):
                split_lo(dve, GA, i + b[GA])
                h_step(dve, b, hb, i - 1, gates)
                split_lo(dve, GU, i + b[GU])
                h_lo_step(dve, b, hb, i - 1)
                split_lo(dve, GD, i + (b[GD] - 1))
            step(1)
            with dve.Fori(2, n) as i:
                step(i)
            head_dve(dve, nxt, 0)
            h_step(dve, b, hb, n - 1, gates)
            dve.wait_ge(hi_ready[GD], b[GD] + n)
            dve.tensor_tensor(tail_lo, raw[GD][:], tail_hi.bitcast(F32), ALU.subtract).then_inc(lo_ready[GD], 1)
            dve.wait_ge(S("h_hi"), hb + n)
            dve.tensor_tensor(tail_h_lo[:].rearrange("p m t -> p (m t)"), h_raw,
                              tail_h_hi[:].rearrange("p m t -> p (m t)").bitcast(F32), ALU.subtract).then_inc(S("h_lo"), 1)
            head_dve(dve, nxt, 1)

        def ff_up(pe, b, hb, i, gate, act0=None):
            pe.wait_ge(lo_ready[GA], i + (b[GA] + 1))
            g, u = step_banks(i, gate)
            if not isinstance(i, int) or i >= (1 if gate else 2):
                pe.wait_ge(S("h_raw"), i + hb)
            proj_t(pe, GA, g, act0=act0).then_inc(slab_used[GA], 1)
            pe.wait_ge(lo_ready[GU], i + (b[GU] + 1))
            proj_t(pe, GU, u).then_inc(slab_used[GU], 1)
            if gate:
                gate(pe, i)

        def ff_down(pe, b, hb, i, first, last):
            pe.wait_ge(S("h_lo"), i + (hb + 1))
            pe.wait_ge(lo_ready[GD], i + (b[GD] + 1))
            hi, lo = slab_views(GD, 2)
            hh, hl = h_hi, h_lo
            if last:
                hh, hl = tail_h_hi, tail_h_lo
                hi, lo = (w.rearrange("p (k n) -> p k n", k=2) for w in (tail_hi, tail_lo))
            for t in range(NT):
                ts = slice(t * P, (t + 1) * P)
                for n in range(2):
                    ns = slice(n * 512, (n + 1) * 512)
                    for j in range(2):
                        ins = three(pe, acc[:, 2 * t + n, :], (hh[:, j, ts], hl[:, j, ts]),
                                    (hi[:, j, ns], lo[:, j, ns]), first and j == 0, last and j == 1)
                    if last and not (t and n):
                        ins.then_inc(S("y_ready"), 1)
            ins.then_inc(slab_used[GD], 1)

        def ff_pe(pe, name, n, hb, n_act, gate=None):
            b = PLAN.base[name]
            ff_up(pe, b, hb, 0, gate, act_before(n_act))
            ff_up(pe, b, hb, 1, gate)
            ff_down(pe, b, hb, 0, True, False)
            with pe.Fori(2, n) as i:
                ff_up(pe, b, hb, i, gate)
                ff_down(pe, b, hb, i - 1, False, False)
            ff_down(pe, b, hb, n - 1, False, True)

        def slab_at(name, j):
            return PLAN.slab_at(name, j)

        def head_act(act, name, *which):
            for j in which or range(2):
                if name:
                    split_hi(act, *slab_at(name, j))

        def head_dve(dve, name, *which):
            for j in which or range(2):
                if name:
                    split_lo(dve, *slab_at(name, j))

        def next_hi(act, name, j, n):
            if j + 2 < n:
                split_hi(act, *slab_at(name, j + 2))

        def next_lo(dve, name, j, n):
            if j + 2 < n:
                split_lo(dve, *slab_at(name, j + 2))

        def cols_load(sp, name, src, *which):
            for j in which:
                load(sp, *slab_at(name, j), src(j))

        def cols_used(eng, name, j):
            s, n = slab_at(name, j)
            eng.wait_ge(slab_used[s], n + 1)

        def cols_pe(pe, name, n0, n1, evac0, act0):
            def one(i, s, act0=None):
                pe.wait_ge(lo_ready[s], i + (PLAN.base[name][s] + 1))
                pe.wait_ge(S("proj_evac"), i * 2 + (evac0 + s - 1))
                proj_t(pe, s, 4 + s, act0=act0).then_inc(slab_used[s], 1)
            one(n0 // 2, 0, act0)
            one(n0 // 2, 1)
            with pe.Fori(n0 // 2 + 1, n1 // 2) as i:
                one(i, 0)
                one(i, 1)

        def mix_cols_pe(pe, l, n0, n1, kind):
            name, evac0 = f"mix{l}", proj_base(l)

            def one(i, m, s, n):
                pe.wait_ge(lo_ready[s], n + 1)
                pe.wait_ge(S("proj_evac"), i * 2 + (evac0 + m - 1))
                if kind == "t":
                    last = proj_t(pe, s, 4 + m)
                else:
                    last = proj_n(pe, s, lambda t: psum[:, 4 + m, t * T:(t + 1) * T])
                last.then_inc(slab_used[s], 1)
            if n0 == 2:
                for m in range(2):
                    one(1, m, *slab_at(name, 2 + m))
            else:
                with pe.Fori(n0 // 2, n1 // 2) as i:
                    one(i, 0, 1, i + (slab_at(name, 4)[1] - 2))
                    one(i, 1, 0, i + (slab_at(name, 5)[1] - 2))

        def mix_next(j):
            return j + 3 if j < 2 else j + 2 if j > 2 else None

        def mix_next_hi(act, name, j, n):
            if mix_next(j) and mix_next(j) < n:
                split_hi(act, *slab_at(name, mix_next(j)))

        def mix_next_lo(dve, name, j, n):
            if mix_next(j) and mix_next(j) < n:
                split_lo(dve, *slab_at(name, mix_next(j)))

        def first_cols_pe(pe, name, evac0, n, n_act):
            for t in range(NT):
                pre_pe(pe, n, (t,))
                for s in range(2):
                    if t == 0:
                        pe.wait_ge(lo_ready[s], PLAN.base[name][s] + 1)
                        pe.wait_ge(S("proj_evac"), evac0)
                    last = proj_n(pe, s, lambda t: psum[:, 4 + s, t * T:(t + 1) * T], None, None if s else act_before(n_act), piece_of, (t,))
                    if t:
                        last.then_inc(slab_used[s], 1)

        def wo_pe(pe, name, n_act):
            for j in range(4):
                s, n = slab_at(name, j)
                pe.wait_ge(lo_ready[s], n + 1)
                proj_n(pe, s, lambda t: acc[:, 2 * t + j // 2, (j % 2) * T:(j % 2 + 1) * T], S("y_ready") if j % 2 else None,
                       None if j else act_before(n_act))\
                    .then_inc(slab_used[s], 1)

        def wo_act(act, name, nxt):
            act.activation(warm, warm, ACT.Silu)
            if name == "w_out":
                for j in range(4):
                    next_hi(act, name, j, 4)
                head_act(act, nxt, 0)
            else:
                head_act(act, name, 2)
                head_act(act, nxt)

        def wo_dve(dve, name, nxt):
            if name == "w_out":
                for j in range(4):
                    next_lo(dve, name, j, 4)
                head_dve(dve, nxt, 0)
            else:
                head_dve(dve, name, 2)
                head_dve(dve, nxt, 0)

        at = [64]

        def tiny(n):
            at[0] += n
            return small[:, at[0] - n:at[0]]

        eps_col, one_col, warm = tiny(1), tiny(1), tiny(1)
        c_act = tiny(KD)
        step_s, lr_s, rad_s, th_s, k_s, red_s, sin_s, cos_s, den_s, ca_s, cb_s, tmp_s = (tiny(16) for _ in range(12))
        turn_w = small[:, at[0]:at[0] + 32]
        g_s, beta_s, sp_s, e_s, gc_s, egc_s, bg_s, ea_s = (tiny(TH) for _ in range(8))
        tail_s = tiny(HEADS)
        f_sum, f_rstd = tiny(NT), tiny(NT)
        wsmall = sb("wsmall", [P, KD, 44])
        w_router, w_ab = wsmall[:, :, 0:36], wsmall[:, :, 36:44]

        N_ADA, ADA_FIRST = 6 * D // 256, 2 * D // 256
        mod = arena[:, 0:6 * D]
        ada_tiles = [raw[0][:], raw[1][:], raw[2][:], act_f[:].rearrange("p k t -> p (k t)"), scratch[:, 2048:4096],
                     arena[:, 0:2048], arena[:, 3072:5120]]
        ADA_RING = (2, 0, 1)

        def ada_place(j):
            if j < ADA_FIRST:
                return (j, 1) if j < 7 else (2, 2)
            turn, i = divmod(j - ADA_FIRST, 3)
            return ADA_RING[i], turn + (3 if i == 0 else 2)

        def ada_load(sp, j):
            b, _ = ada_place(j)
            if j == 7:
                sp.wait_ge(S("ada_used"), 3)
            elif j >= ADA_FIRST + 3:
                sp.wait_ge(S("ada_used"), j - 2)
            elif j >= ADA_FIRST:
                sp.wait_ge(lo_ready[b], PLAN.base["w_out" if b < GD else "moe"][b])
            sp.dma_start(ada_tiles[b].rearrange("p (k n) -> p k n", k=KD), col_slab(a["w_ada"], 256 * j)).then_inc(S(f"ada_loaded{b}"), 16)

        def ada_bank(j):
            return psum[:, 4 + j % 2 if j < ADA_FIRST else 6, 0:256]

        def ada_pe(pe, j):
            b, uses = ada_place(j)
            pe.wait_ge(S(f"ada_loaded{b}"), 16 * uses)
            if 2 <= j < ADA_FIRST:
                pe.wait_ge(S("proj_evac"), j - 1)
            elif j > ADA_FIRST:
                pe.wait_ge(S("ada_evac"), j - ADA_FIRST)
            slab = ada_tiles[b].rearrange("p (k n) -> p k n", k=KD)
            for k in range(KD):
                last = pe.matmul(ada_bank(j), c_act[:, k:k + 1].to_broadcast([P, P]), slab[:, k, :], start=k == 0, stop=k == KD - 1)
            last.then_inc(S("ada_used"), 1)

        def ada_dve(dve, done, j):
            dve.wait_ge(S("ada_used"), j + 1)
            sem = S("proj_evac" if j < ADA_FIRST else "ada_evac")
            part, c = divmod(j, D // 256)
            if part in (2, 5):
                dve.wait_ge(S("bias_loaded"), 32)
                row = mod[:, j * 256:(j + 1) * 256]
                dve.tensor_tensor(row, row, ada_bank(j), ALU.add).then_inc(sem, 1)
            else:
                dve.tensor_tensor(diag[:], ada_bank(j).rearrange("p (k n) -> p k n", k=2), rep(ident, 2), ALU.mult).then_inc(sem, 1)
                dve.wait_ge(sem, j + 1 if j < ADA_FIRST else j - ADA_FIRST + 1)
                done(dve.reduce_sum(modc[:, (0, 1, None, 2, 3)[part], 2 * c:2 * c + 2], diag[:], AX))

        def mod_dve(dve, done, shift, norm):
            for q in (shift, shift + 1):
                done(dve.tensor_tensor(modc[:, q, :], modc[:, q, :], col("b_ada", q * KD, KD), ALU.add))
            dve.scalar_tensor_tensor(modc[:, shift + 1, :], modc[:, shift + 1, :], 1.0, col(norm, 0, KD), ALU.add, ALU.mult)\
               .then_inc(S("mod_cols"), 1)

        e_re = arena[:, 6 * 1024:10 * 1024].rearrange("p (j t) -> p j t", j=S5_TILES)
        e_im = arena[:, 10 * 1024:14 * 1024].rearrange("p (j t) -> p j t", j=S5_TILES)
        cx_re = col("c_re", 0, 512).rearrange("p (j h) -> p j h", j=S5_TILES)
        cx_nim = col("c_im", 0, 512).rearrange("p (j h) -> p j h", j=S5_TILES)
        TWO_PI = 2 * math.pi
        C1 = 6.28125

        def s5_param_act(act):
            act.wait_ge(S("cols_loaded"), 16)
            act.activation(c_act, col("c", 0, KD), ACT.Silu).then_inc(S("c_act"), 1)
            act.activation(step_s, col("log_step", 0, 16), ACT.Exp).then_inc(S("s5_step"), 1)
            act.wait_ge(S("s5_lr"), 1)
            act.activation(rad_s, lr_s, ACT.Exp).then_inc(S("s5_rad"), 1)
            act.wait_ge(S("s5_angle"), 1)
            act.activation(sin_s, red_s, ACT.Sin).then_inc(S("s5_turn"), 1)
            act.activation(cos_s, k_s, ACT.Sin).then_inc(S("s5_turn"), 1)

        def s5_param_dve(dve, done):
            dve.memset(eps_col, EPS)
            dve.memset(one_col, 1.0)
            dve.memset(warm, 0.0)
            dve.memset(half[:], -0.5).then_inc(S("half"), 1)
            dve.wait_ge(S("s5_step"), 1)
            dve.tensor_tensor(lr_s, col("lam_re", 0, 16), step_s, ALU.mult).then_inc(S("s5_lr"), 1)
            done(dve.tensor_tensor(th_s, col("lam_im", 0, 16), step_s, ALU.mult))
            done(dve.tensor_scalar(k_s, th_s, 1 / TWO_PI, 12582912.0, ALU.mult, ALU.add))
            done(dve.tensor_scalar(k_s, k_s, 12582912.0, None, ALU.subtract))
            done(dve.scalar_tensor_tensor(red_s, k_s, -C1, th_s, ALU.mult, ALU.add))
            done(dve.scalar_tensor_tensor(red_s, k_s, -(TWO_PI - C1), red_s, ALU.mult, ALU.add))
            done(dve.tensor_scalar(red_s, red_s, 3.1415925, -3.1415925, ALU.min, ALU.max))
            done(dve.tensor_scalar(k_s, red_s, -1.0, None, ALU.mult))
            done(dve.tensor_tensor(k_s, k_s, red_s, ALU.max))
            dve.tensor_scalar(k_s, k_s, -1.0, math.pi / 2, ALU.mult, ALU.add).then_inc(S("s5_angle"), 1)
            dve.wait_ge(S("s5_turn"), 2)
            dve.wait_ge(S("s5_rad"), 1)
            lre, lim = col("lam_re", 0, 16), col("lam_im", 0, 16)
            done(dve.tensor_tensor(ca_s, rad_s, cos_s, ALU.mult))
            done(dve.tensor_scalar(ca_s, ca_s, 1.0, None, ALU.subtract))
            done(dve.tensor_tensor(cb_s, rad_s, sin_s, ALU.mult))
            done(dve.tensor_tensor(den_s, lre, lre, ALU.mult))
            done(dve.tensor_tensor(tmp_s, lim, lim, ALU.mult))
            done(dve.tensor_tensor(den_s, den_s, tmp_s, ALU.add))
            done(dve.reciprocal(den_s, den_s))
            done(dve.tensor_tensor(tmp_s, ca_s, lre, ALU.mult))
            done(dve.tensor_tensor(k_s, cb_s, lim, ALU.mult))
            done(dve.tensor_tensor(k_s, k_s, tmp_s, ALU.add))
            done(dve.tensor_tensor(tmp_s, cb_s, lre, ALU.mult))
            done(dve.tensor_tensor(cb_s, ca_s, lim, ALU.mult))
            done(dve.tensor_tensor(cb_s, tmp_s, cb_s, ALU.subtract))
            done(dve.tensor_tensor(cb_s, cb_s, den_s, ALU.mult))
            dve.tensor_tensor(ca_s, k_s, den_s, ALU.mult).then_inc(S("s5_coef"), 1)

        def s5_tables_pool(pool, done):
            pool.wait_ge(S("s5_turn"), 2)
            wr, wi = turn_w[:, 0:16], turn_w[:, 16:32]
            w2, w3 = lr_s, th_s
            pool.memset(e_re[:, :, 0:1], 1.0)
            pool.memset(e_im[:, :, 0:1], 0.0)
            pool.tensor_copy(wr, cos_s)
            done(pool.tensor_copy(wi, sin_s))
            for d in (1, 2, 4, 8, 16, 32, 64, 128):
                if d == 32:
                    pre_pool(pool, 0)
                for at0 in range(0, d, 64):
                    n = min(d, 64)
                    m1 = arena[:, 14336:14336 + 16 * n].rearrange("p (j t) -> p j t", j=16)
                    m2 = arena[:, 15360:15360 + 16 * n].rearrange("p (j t) -> p j t", j=16)
                    src, dst = slice(at0, at0 + n), slice(d + at0, d + at0 + n)
                    pool.tensor_tensor(m1, e_re[:, :, src], bc(wr, n), ALU.mult)
                    done(pool.tensor_tensor(m2, e_im[:, :, src], bc(wi, n), ALU.mult))
                    done(pool.tensor_tensor(e_re[:, :, dst], m1, m2, ALU.subtract))
                    pool.tensor_tensor(m1, e_re[:, :, src], bc(wi, n), ALU.mult)
                    done(pool.tensor_tensor(m2, e_im[:, :, src], bc(wr, n), ALU.mult))
                    done(pool.tensor_tensor(e_im[:, :, dst], m1, m2, ALU.add))
                pool.tensor_tensor(w2, wr, wr, ALU.mult)
                done(pool.tensor_tensor(w3, wi, wi, ALU.mult))
                done(pool.tensor_tensor(w2, w2, w3, ALU.subtract))
                done(pool.tensor_tensor(w3, wr, wi, ALU.mult))
                pool.tensor_tensor(wi, w3, w3, ALU.add)
                done(pool.tensor_copy(wr, w2))
            pool.wait_ge(S("s5_coef"), 1)
            m1 = arena[:, 14336:14336 + 512].rearrange("p (j t) -> p j t", j=16)
            m2 = arena[:, 14848:14848 + 512].rearrange("p (j t) -> p j t", j=16)
            pool.tensor_tensor(m1, cx_re, bc(cb_s, 32), ALU.mult)
            done(pool.tensor_tensor(m2, cx_nim, bc(cb_s, 32), ALU.mult))
            done(pool.tensor_tensor(cx_re, cx_re, bc(ca_s, 32), ALU.mult))
            done(pool.tensor_tensor(cx_re, cx_re, m2, ALU.subtract))
            done(pool.tensor_tensor(cx_nim, cx_nim, bc(ca_s, 32), ALU.mult))
            done(pool.tensor_tensor(cx_nim, cx_nim, m1, ALU.add))
            pool.tensor_scalar(cx_nim, cx_nim, -1.0, None, ALU.mult).then_inc(S("s5_tables"), 1)

        u = area(0, 1024).rearrange("p (c t) -> p c t", c=CS5)
        zs = area(1, 1024).rearrange("p (c t) -> p c t", c=HEADS)
        q_t = area(3, 1024).rearrange("p (c t) -> p c t", c=HEADS)
        k_t = area(4, 1024).rearrange("p (c t) -> p c t", c=HEADS)
        v_t = scratch[:, 1024:2048].rearrange("p (c t) -> p c t", c=HEADS)
        qkv = [q_t, k_t, v_t]
        PADT = T + CONV - 1
        pads = [scratch[:, 2048 + s * 2 * PADT:2048 + (s + 1) * 2 * PADT].rearrange("p (m t) -> p m t", m=2) for s in range(2)]
        ab_bank = psum[:, 7, 0:16].rearrange("p (t e) -> p t e", t=NT)

        def w_in_pe(pe):
            cols_pe(pe, "w_in", 0, 10, ADA_FIRST, 0)
            pe.wait_ge(S("narrow_loaded"), 32)
            for t in range(NT):
                for k in range(KD):
                    last = pe.matmul(ab_bank[:, t, :], act_f[:, k, t * P:(t + 1) * P], w_ab[:, k, :], start=k == 0, stop=k == KD - 1)
            last.then_inc(S("gates_raw"), 1)

        def w_in_act(act):
            for j in range(10):
                s = j % 2
                cols_used(act, "w_in", j)
                bank = psum[:, 4 + s, :].rearrange("p (m t) -> p m t", m=2)
                if j < 2:
                    act.activation(u[:, 2 * j:2 * j + 2, :], bank, ACT.Copy).then_inc(S("proj_evac"), 1)
                elif j < 8:
                    act.wait_ge(S("pads_zero"), 1)
                    if j >= 4:
                        act.wait_ge(S("convolved"), j - 3)
                    act.activation(pads[s][:, :, CONV - 1:], bank, ACT.Copy).then_inc(S("proj_evac"), 1)
                else:
                    act.activation(zs[:, 2 * (j - 8):2 * (j - 8) + 2, :], bank, ACT.Silu).then_inc(S("proj_evac"), 1)
                next_hi(act, "w_in", j, 10)
            split_hi(act, GD, PLAN.base["w_glu"][GD])

        def w_in_dve(dve, done):
            for s in range(2):
                last = dve.memset(pads[s][:, :, 0:CONV - 1], 0.0)
            last.then_inc(S("pads_zero"), 1)
            for j in range(10):
                if 2 <= j < 8:
                    jj = j - 2
                    dve.wait_ge(S("proj_evac"), ADA_FIRST + j + 1)
                    dst = qkv[jj // 2][:, 2 * (jj % 2):2 * (jj % 2) + 2, :]
                    for i in range(CONV):
                        for m in range(2):
                            w = col("conv_w", (2 * jj + m) * CONV + i)
                            src = pads[j % 2][:, m, i:i + T]
                            if i == 0:
                                last = dve.tensor_scalar(dst[:, m, :], src, w, None, ALU.mult)
                            else:
                                last = dve.scalar_tensor_tensor(dst[:, m, :], src, w, dst[:, m, :], ALU.mult, ALU.add)
                        if i < CONV - 1:
                            done(last)
                    last.then_inc(S("convolved"), 1)
                next_lo(dve, "w_in", j, 10)
            split_lo(dve, GD, PLAN.base["w_glu"][GD])

        parts = [[b[:, i * 512:(i + 1) * 512].rearrange("p (m t) -> p m t", m=2) for i in range(4)]
                 for b in (arena[:, 14336:16384], scratch[:, 2048:4096])]

        def s5_pe(pe):
            b_re, b_im = (junk[:, i * 512:(i + 1) * 512].rearrange("p (c s) -> p c s", c=CS5) for i in range(2))
            pe.wait_ge(S("s5_b_loaded"), 16)

            def bu(g):
                if g >= 2:
                    pe.wait_ge(S("s5_turned"), g - 1)
                for m in range(2):
                    j = 2 * g + m
                    r, c = 32 * (j % 4), j // 4
                    bank = psum[:, 2 * (g % 2) + m, :]
                    pe.matmul(bank[:, 0:T], b_re[r:r + 32, c, :], u[r:r + 32, c, :], start=True, stop=True)
                    last = pe.matmul(bank[:, T:2 * T], b_im[r:r + 32, c, :], u[r:r + 32, c, :], start=True, stop=True)
                last.then_inc(S("s5_bu"), 1)

            pe.wait_ge(S("proj_evac"), ADA_FIRST + 10)
            pe.wait_ge(S("s5_tables"), 1)
            bu(0)
            for g in range(8):
                if g < 7:
                    bu(g + 1)
                ada_pe(pe, ADA_FIRST + g)
                pe.wait_ge(S("s5_states"), g + 1)
                q1, q4, q2, q3 = parts[g % 2]
                for m in range(2):
                    j = 2 * g + m
                    r, c = 32 * (j % 4), j // 4
                    y = psum[r:r + 32, 4 + c % 2, (c // 2) * T:(c // 2 + 1) * T]
                    pe.matmul(y, cx_re[:, j, :], q1[:, m, :], start=True, stop=False)
                    pe.matmul(y, cx_re[:, j, :], q2[:, m, :], start=False, stop=False)
                    pe.matmul(y, cx_nim[:, j, :], q3[:, m, :], start=False, stop=False)
                    last = pe.matmul(y, cx_nim[:, j, :], q4[:, m, :], start=False, stop=True)
                last.then_inc(S("s5_y"), 1)
            ada_pe(pe, ADA_FIRST + 8)
            pe.wait_ge(S("glu_lo"), 2)
            pe.wait_ge(lo_ready[GD], PLAN.base["w_glu"][GD] + 1)
            for m in range(2):
                last = proj_t(pe, GD, m, act_k=CS5, m0=2 * m, k_cols=512)
            last.then_inc(slab_used[GD], 1)
            ada_pe(pe, ADA_FIRST + 9)

        def s5_dve(dve, done):
            for g in range(8):
                p1, p2, p3, p4 = parts[g % 2]
                dve.wait_ge(S("s5_bu"), g + 1)
                if g >= 2:
                    dve.wait_ge(S("s5_y"), g - 1)
                b = psum[:, 2 * (g % 2):2 * (g % 2) + 2, :]
                er, ei = e_re[:, 2 * g:2 * g + 2, :], e_im[:, 2 * g:2 * g + 2, :]
                dve.tensor_tensor(p1, b[:, :, 0:T], er, ALU.mult)
                dve.tensor_tensor(p2, b[:, :, T:2 * T], ei, ALU.mult)
                dve.tensor_tensor(p3, b[:, :, T:2 * T], er, ALU.mult)
                ins = dve.tensor_tensor(p4, b[:, :, 0:T], ei, ALU.mult)
                ins.then_inc(S("s5_turned"), 1)
                dve.wait_ge(S("s5_turned"), g + 1)
                dve.tensor_tensor(p1, p1, p2, ALU.add)
                done(dve.tensor_tensor(p3, p3, p4, ALU.subtract))
                for m in range(2):
                    r = rad_s[:, 2 * g + m:2 * g + m + 1].to_broadcast([P, T])
                    dve.tensor_tensor_scan(p2[:, m, :], r, p1[:, m, :], 0.0, ALU.mult, ALU.add)
                    last = dve.tensor_tensor_scan(p4[:, m, :], r, p3[:, m, :], 0.0, ALU.mult, ALU.add)
                done(last)
                dve.tensor_tensor(p1, p2, er, ALU.mult)
                dve.scalar_tensor_tensor(p3, p4, -1.0, ei, ALU.mult, ALU.mult)
                dve.tensor_tensor(p4, p4, er, ALU.mult)
                dve.tensor_tensor(p2, p2, ei, ALU.mult).then_inc(S("s5_states"), 1)
                ada_dve(dve, done, ADA_FIRST + g)
            dve.wait_ge(S("s5_y"), 8)
            for c in range(CS5):
                y = psum[:, 4 + c % 2, (c // 2) * T:(c // 2 + 1) * T]
                dve.scalar_tensor_tensor(act_f[:, c, :], u[:, c, :], col("s5_d", c), y, ALU.mult, ALU.add).then_inc(S("s5_yd"), 1)
            ada_dve(dve, done, ADA_FIRST + 8)
            for q in range(2):
                dve.wait_ge(S("glu_hi"), q + 1)
                dve.tensor_tensor(act_lo[:, 2 * q:2 * q + 2, :], act_f[:, 2 * q:2 * q + 2, :],
                                  act_hi[:, 2 * q:2 * q + 2, :].bitcast(F32), ALU.subtract).then_inc(S("glu_lo"), 1)
            sg = arena[:, 14336:15360].rearrange("p (m t) -> p m t", m=CS5)
            for m in range(CS5):
                dve.wait_ge(S("glu_gate"), m + 1)
                dve.tensor_tensor(act_f[:, m, :], act_f[:, m, :], sg[:, m, :], ALU.mult).then_inc(S("act_f"), 1)
            ada_dve(dve, done, ADA_FIRST + 9)

        def s5_act(act):
            for q in range(2):
                act.wait_ge(S("s5_yd"), 2 * q + 2)
                act.activation(act_f[:, 2 * q:2 * q + 2, :], act_f[:, 2 * q:2 * q + 2, :], ACT.Gelu_apprx_tanh).then_inc(S("glu_f"), 1)
                act.wait_ge(S("glu_f"), q + 1)
                act.activation(act_hi[:, 2 * q:2 * q + 2, :], act_f[:, 2 * q:2 * q + 2, :], ACT.Copy).then_inc(S("glu_hi"), 1)
            sg = arena[:, 14336:15360].rearrange("p (m t) -> p m t", m=CS5)
            act.wait_ge(slab_used[GD], PLAN.base["w_glu"][GD] + 1)
            for m in range(CS5):
                act.activation(sg[:, m, :], psum[:, m // 2, (m % 2) * T:(m % 2 + 1) * T], ACT.Sigmoid, bias=col("b_glu", m))\
                   .then_inc(S("glu_gate"), 1)
        def column_sums(pe, out_ap, sq_ap, sem):
            n = sq_ap.shape[1] // P
            for e in range(n):
                last = pe.matmul(out_ap[:, e:e + 1], sq_ap[:, e * P:(e + 1) * P], mat("ones")[:, 0:1], start=True, stop=True)
            last.then_inc(sem, 1)

        def diagonals(dve, out_ap, cols_ap, sem):
            n = cols_ap.shape[1] // 2
            for i in range(2):
                dve.tensor_tensor(th_view(out_ap[:, i * n * P:(i + 1) * n * P]), rep(ident, n), bc(cols_ap[:, i * n:(i + 1) * n], P),
                                  ALU.mult).then_inc(sem, 1)

        def rows_of(pe, bank, diag_ap, diag_sem, before, sem):
            n = diag_ap.shape[1] // 512
            for i in range(n):
                if i % (n // 2) == 0:
                    pe.wait_ge(diag_sem, before + 1 + i // (n // 2))
                last = pe.matmul(psum[:, bank + i, :], mat("ones"), diag_ap[:, i * 512:(i + 1) * 512], start=True, stop=True)
            last.then_inc(sem, 1)

        def blk(b):
            return area(b, 1024)

        def tok_view(ap):
            return ap.rearrange("p (c t) -> p c t", t=T)

        sq, qk_diag = arena[:, 6 * 1024:8 * 1024], arena[:, 8 * 1024:10 * 1024]
        qk_r, o_r = tiny(16), tiny(8)
        g_b, beta_b, kb_t, eg = blk(10), blk(11), blk(12), blk(13)
        diff = blk(6)
        n_t, qk_t = blk(7), blk(8)
        vb = blk(9)
        qd, kt = arena[:, 14336:14848], arena[:, 14848:15360]
        kbg = arena[:, 15360:15872]
        m_inv, mt_inv = blk(10), blk(11)
        p_sb = blk(0)
        scr_a, scr_b = scratch[:, 2048:3072], scratch[:, 3072:4096]
        nkc, vn0, s1, vn1 = scr_a[:, 0:512], scr_a[:, 512:1024], scr_b[:, 0:512], scr_b[:, 512:1024]
        o_f, o_sq, o_diag = blk(12), blk(13), blk(6)

        def banks(b, n=2):
            return psum[:, b:b + n, :].rearrange("p b n -> p (b n)")

        def half_blocks(ap, lv, odd):
            v = ap.rearrange("p (b two n) -> p b two n", two=2, n=1 << lv)
            return v[:, :, odd, :]

        def gdn_pe(pe):
            upto = mat("upto")
            pe.wait_ge(S("qk_sq"), 2)
            pe.wait_ge(S("glu_gate"), CS5)
            column_sums(pe, psum[:, 0, 0:16], sq, S("head_sums"))
            ada_pe(pe, ADA_FIRST + 10)
            pe.wait_ge(S("g_rows"), 2)
            pe.matmul(psum[:, 7, 32:32 + TH], upto, g_s, start=True, stop=True).then_inc(S("g_cum"), 1)
            for e in range(TH):
                last = pe.matmul(banks(4)[:, e * P:(e + 1) * P], th_view(g_b)[:, e, :], upto, start=True, stop=True)
            last.then_inc(S("g_cum_rows"), 1)
            ada_pe(pe, ADA_FIRST + 11)
            rows_of(pe, 0, qk_diag, S("head_diag"), 0, S("head_rows"))
            pe.wait_ge(S("qk_normed"), 2)
            for e in range(TH):
                last = pe.matmul(banks(0)[:, e * P:(e + 1) * P], th_view(beta_b)[:, e, :], ident, start=True, stop=True)
            last.then_inc(S("beta_rows"), 1)
            ada_pe(pe, ADA_FIRST + 12)
            pe.wait_ge(S("kb"), 1)
            pe.wait_ge(S("diff"), 1)
            kn, qn, kb = (tok_view(b) for b in (blk(4), blk(3), kb_t))
            for bank, rhs in ((2, kb), (4, qn)):
                for e in range(TH):
                    ts = slice((e % 2) * P, (e % 2 + 1) * P)
                    last = pe.matmul(banks(bank)[:, e * P:(e + 1) * P], kn[:, e // 2, ts], rhs[:, e // 2, ts], start=True, stop=True)
                last.then_inc(S("kk_qk"), 1)
            ada_pe(pe, ADA_FIRST + 13)
            for e in range(TH):
                last = pe.transpose(banks(0)[:, e * P:(e + 1) * P], blk(4)[:, e * P:(e + 1) * P], ident)
            last.then_inc(S("k_nat"), 1)
            ada_pe(pe, ADA_FIRST + 14)
            pe.wait_ge(S("n_qk"), 2)
            for e in range(TH):
                last = pe.transpose(banks(2)[:, e * P:(e + 1) * P], scratch[:, 1024 + e * P:1024 + (e + 1) * P], ident)
            last.then_inc(S("v_nat"), 1)
            ada_pe(pe, ADA_FIRST + 15)
            pe.wait_ge(S("nat_read"), 1)
            m3, mt3, n3, p3 = (th_view(b) for b in (m_inv, mt_inv, n_t, p_sb))
            for lv in range(LEVELS):
                for hf in range(2):
                    es = range(4 * hf, 4 * hf + 4)
                    if lv:
                        pe.wait_ge(S("inv_done"), 2 * (lv - 1) + hf + 1)
                    for e in es:
                        p_at = psum[:, hf, (e % 4) * P:(e % 4 + 1) * P]
                        if lv:
                            last = pe.matmul(half_blocks(p_at, lv, 0), n3[:, e, :], half_blocks(m3[:, e, :], lv, 0), start=True, stop=True)
                        else:
                            last = pe.transpose(p_at, n3[:, e, :], ident)
                    last.then_inc(S("inv_p"), 1)
                for hf in range(2):
                    es = range(4 * hf, 4 * hf + 4)
                    pe.wait_ge(S("inv_masked"), 2 * lv + hf + 1)
                    for e in es if lv else ():
                        pe.matmul(half_blocks(psum[:, 2 + hf, (e % 4) * P:(e % 4 + 1) * P], lv, 0), mt3[:, e, :],
                                  half_blocks(p3[:, e, :], lv, 0), start=True, stop=True)
                    for e in es:
                        q_at = psum[:, 4 + hf, (e % 4) * P:(e % 4 + 1) * P]
                        if lv:
                            last = pe.matmul(half_blocks(q_at, lv, 1), p3[:, e, :], half_blocks(mt3[:, e, :], lv, 1), start=True, stop=True)
                        else:
                            last = pe.transpose(q_at, p3[:, e, :], ident)
                    last.then_inc(S("inv_q"), 1)
            pe.wait_ge(S("inv_done"), 2 * LEVELS)
            kbg3, kt3, vn03, s13, vn13, nkc3, qd3 = (th_view(b) for b in (kbg, kt, vn0, s1, vn1, nkc, qd))
            vb3, qk3 = th_view(vb), th_view(qk_t)

            def hp(h):
                return slice(h * P, (h + 1) * P)
            for h in range(HEADS):
                last = pe.matmul(psum[:, 0, hp(h)], kbg3[:, h, :], mt3[:, 2 * h + 1, :], start=True, stop=True)
            last.then_inc(S("kc"), 1)
            for h in range(HEADS):
                last = pe.matmul(psum[:, 1, hp(h)], mt3[:, 2 * h, :], vb3[:, 2 * h, :], start=True, stop=True)
            last.then_inc(S("v_new"), 1)
            pe.wait_ge(S("vn_read"), 1)
            for h in range(HEADS):
                last = pe.matmul(psum[:, 6, hp(h)], kt3[:, h, :], vn03[:, h, :], start=True, stop=True)
            last.then_inc(S("state"), 1)
            pe.wait_ge(S("state_read"), 1)
            pe.wait_ge(S("kc_read"), 1)
            for h in range(HEADS):
                pe.matmul(psum[:, 7, hp(h)], mt3[:, 2 * h + 1, :], vb3[:, 2 * h + 1, :], start=True, stop=False)
                last = pe.matmul(psum[:, 7, hp(h)], nkc3[:, h, :], s13[:, h, :], start=False, stop=True)
            last.then_inc(S("v_new"), 1)
            pe.wait_ge(S("vn_read"), 2)
            for h in range(HEADS):
                o0, o1 = banks(2)[:, 2 * h * P:(2 * h + 1) * P], banks(2)[:, (2 * h + 1) * P:(2 * h + 2) * P]
                pe.matmul(o0, vn03[:, h, :], qk3[:, 2 * h, :], start=True, stop=True)
                pe.matmul(o1, s13[:, h, :], qd3[:, h, :], start=True, stop=False)
                last = pe.matmul(o1, vn13[:, h, :], qk3[:, 2 * h + 1, :], start=False, stop=True)
            last.then_inc(S("gdn_o"), 1)
            pe.wait_ge(S("gdn_sq"), 1)
            column_sums(pe, psum[:, 4, 0:TH], o_sq, S("head_sums"))
            rows_of(pe, 0, o_diag, S("head_diag"), 2, S("head_rows"))
            keep_clock(pe, 7, 12)

        def gdn_act(act):
            for i in range(3):
                act.wait_ge(S("convolved"), 2 * i + 2)
                act.activation(qkv[i], qkv[i], ACT.Silu).then_inc(S("qkv"), 1)
            for i in range(2):
                act.wait_ge(S("qkv"), i + 1)
                act.activation(sq[:, i * 1024:(i + 1) * 1024], blk(3 + i), ACT.Square).then_inc(S("qk_sq"), 1)
            act.wait_ge(S("gate_in"), 1)
            act.activation(e_s, e_s, ACT.Exp, scale=-1.0).then_inc(S("gate_exp"), 1)
            act.activation(bg_s, bg_s, ACT.Exp, scale=-1.0).then_inc(S("gate_exp"), 1)
            act.activation(ea_s, col("a_log", 0, TH), ACT.Exp).then_inc(S("gate_exp"), 1)
            act.wait_ge(S("gate_exp"), 1)
            act.activation(e_s, e_s, ACT.Ln, bias=one_col).then_inc(S("gate_ln"), 1)
            act.wait_ge(S("head_sums"), 1)
            act.activation(qk_r, psum[:, 0, 0:16], ACT.Sqrt, bias=eps_col).then_inc(S("head_root"), 1)
            act.wait_ge(S("g_cum_rows"), 1)
            act.activation(eg, banks(4), ACT.Exp).then_inc(S("eg"), 1)
            act.wait_ge(S("gc"), 1)
            act.activation(egc_s, gc_s, ACT.Exp).then_inc(S("egc"), 1)
            act.wait_ge(S("tail"), 1)
            act.activation(tail_s, tail_s, ACT.Exp).then_inc(S("tail_exp"), 1)
            act.wait_ge(S("diff"), 1)
            act.activation(diff, diff, ACT.Exp).then_inc(S("decay_exp"), 1)
            head_act(act, "w_out")
            act.wait_ge(S("kc"), 1)
            act.activation(nkc, psum[:, 0, :], ACT.Copy, scale=-1.0).then_inc(S("kc_read"), 1)
            act.wait_ge(S("v_new"), 1)
            act.activation(vn0, psum[:, 1, :], ACT.Copy).then_inc(S("vn_read"), 1)
            act.wait_ge(S("state"), 1)
            act.activation(s1, psum[:, 6, :], ACT.Copy).then_inc(S("state_read"), 1)
            act.wait_ge(S("v_new"), 2)
            act.activation(vn1, psum[:, 7, :], ACT.Copy).then_inc(S("vn_read"), 1)
            act.wait_ge(S("gdn_o"), 1)
            act.activation(o_sq, banks(2), ACT.Square).then_inc(S("gdn_sq"), 1)
            act.activation(o_f, banks(2), ACT.Copy).then_inc(S("gdn_of"), 1)
            act.wait_ge(S("head_sums"), 2)
            act.activation(o_r, psum[:, 4, 0:TH], ACT.Sqrt, bias=eps_col, scale=1.0 / DK).then_inc(S("head_root"), 1)

        def gdn_dve(dve, done):
            dve.wait_ge(S("gates_raw"), 1)
            a_v = psum[:, 7, 0:16].rearrange("p (t e) -> p e t", t=NT)
            heads_v = [ap.rearrange("p (h t) -> p h t", h=HEADS) for ap in (g_s, bg_s)]
            done(dve.tensor_tensor(heads_v[0], a_v[:, 0:4, :], col("dt_bias", 0, TH).rearrange("p (h t) -> p h t", h=HEADS), ALU.add))
            done(dve.tensor_copy(heads_v[1], a_v[:, 4:8, :]))
            done(dve.tensor_scalar(e_s, g_s, -1.0, None, ALU.mult))
            done(dve.tensor_scalar(sp_s, g_s, 0.0, None, ALU.max))
            dve.tensor_tensor(e_s, e_s, g_s, ALU.max).then_inc(S("gate_in"), 1)
            dve.wait_ge(S("gate_exp"), 3)
            done(dve.tensor_scalar(bg_s, bg_s, 1.0, None, ALU.add))
            done(dve.reciprocal(beta_s, bg_s))
            dve.wait_ge(S("gate_ln"), 1)
            done(dve.tensor_tensor(sp_s, sp_s, e_s, ALU.add))
            done(dve.scalar_tensor_tensor(g_s, sp_s, -1.0, ea_s, ALU.mult, ALU.mult))
            dve.tensor_copy(th_view(g_b), bc(g_s, P)).then_inc(S("g_rows"), 1)
            dve.tensor_copy(th_view(beta_b), bc(beta_s, P)).then_inc(S("g_rows"), 1)
            ada_dve(dve, done, ADA_FIRST + 10)
            dve.wait_ge(S("g_cum"), 1)
            dve.tensor_copy(gc_s, psum[:, 7, 32:32 + TH]).then_inc(S("gc"), 1)
            ada_dve(dve, done, ADA_FIRST + 11)
            dve.wait_ge(S("head_root"), 1)
            done(dve.reciprocal(qk_r, qk_r))
            diagonals(dve, qk_diag, qk_r, S("head_diag"))
            dve.wait_ge(S("head_rows"), 1)
            dve.scalar_tensor_tensor(blk(3), blk(3), DK ** -0.5, banks(0), ALU.mult, ALU.mult).then_inc(S("qk_normed"), 1)
            dve.tensor_tensor(blk(4), blk(4), banks(2), ALU.mult).then_inc(S("qk_normed"), 1)
            dve.wait_ge(S("beta_rows"), 1)
            dve.wait_ge(S("qk_normed"), 2)
            dve.tensor_tensor(kb_t, blk(4), banks(0), ALU.mult).then_inc(S("kb"), 1)
            ada_dve(dve, done, ADA_FIRST + 12)
            dve.wait_ge(S("eg"), 1)
            dve.wait_ge(S("gc"), 1)
            cum = th_view(banks(4))
            done(dve.tensor_tensor(th_view(diff), cum, bc(gc_s, P), ALU.subtract))
            last_g = banks(4).rearrange("p (h t n) -> p h t n", h=HEADS, t=NT)[:, :, 0, P - 1]
            dve.tensor_tensor(tail_s, last_g, gc_s.rearrange("p (h t) -> p h t", h=HEADS)[:, :, 0], ALU.subtract).then_inc(S("tail"), 1)
            dve.tensor_scalar(diff, diff, 0.0, None, ALU.min).then_inc(S("diff"), 1)
            dve.tensor_tensor(qd.rearrange("p (h n) -> p h n", h=HEADS), tok_view(blk(3))[:, :, P:T], tok_view(eg)[:, :, P:T], ALU.mult)
            ada_dve(dve, done, ADA_FIRST + 13)
            dve.wait_ge(S("decay_exp"), 1)
            done(dve.tensor_tensor(th_view(diff), th_view(diff), rep(mat("upto"), TH), ALU.mult))
            dve.wait_ge(S("kk_qk"), 1)
            dve.tensor_tensor(n_t, banks(2), diff, ALU.mult).then_inc(S("n_qk"), 1)
            dve.wait_ge(S("kk_qk"), 2)
            dve.tensor_tensor(qk_t, banks(4), diff, ALU.mult).then_inc(S("n_qk"), 1)
            ada_dve(dve, done, ADA_FIRST + 14)
            dve.wait_ge(S("egc"), 1)
            done(dve.tensor_tensor(bg_s, beta_s, egc_s, ALU.mult))
            dve.wait_ge(S("k_nat"), 1)
            dve.wait_ge(S("tail_exp"), 1)
            k_nat = banks(0).rearrange("p (h t n) -> p h t n", h=HEADS, t=NT)
            bg1 = bg_s.rearrange("p (h t) -> p h t", h=HEADS)[:, :, 1]
            dve.tensor_tensor(kbg.rearrange("p (h n) -> p h n", h=HEADS), k_nat[:, :, 1, :], bc(bg1, P), ALU.mult)
            dve.tensor_tensor(kt.rearrange("p (h n) -> p h n", h=HEADS), k_nat[:, :, 0, :], bc(tail_s, P), ALU.mult)
            dve.wait_ge(S("v_nat"), 1)
            dve.tensor_tensor(th_view(vb), th_view(banks(2)), bc(beta_s, P), ALU.mult).then_inc(S("nat_read"), 1)
            ada_dve(dve, done, ADA_FIRST + 15)
            halves = [[ap[:, hf * 512:(hf + 1) * 512] for ap in (m_inv, mt_inv, p_sb)] for hf in range(2)]
            for lv in range(LEVELS):
                for hf in range(2):
                    dve.wait_ge(S("inv_p"), 2 * lv + hf + 1)
                    dve.tensor_tensor(th_view(halves[hf][2]), th_view(psum[:, hf, :]), rep(mat(f"level{lv}"), 4), ALU.mult)\
                       .then_inc(S("inv_masked"), 1)
                for hf in range(2):
                    if lv:
                        dve.wait_ge(S("inv_q"), 2 * lv + hf + 1)
                        m, mt = half_blocks(halves[hf][0], lv, 0), half_blocks(halves[hf][1], lv, 1)
                        dve.tensor_tensor(m, m, half_blocks(psum[:, 2 + hf, :], lv, 0), ALU.subtract)
                        dve.tensor_tensor(mt, mt, half_blocks(psum[:, 4 + hf, :], lv, 1), ALU.subtract).then_inc(S("inv_done"), 1)
                    else:
                        dve.wait_ge(S("inv_masked"), hf + 1)
                        dve.tensor_tensor(th_view(halves[hf][0]), rep(ident, 4), th_view(halves[hf][2]), ALU.subtract)
                        dve.wait_ge(S("inv_q"), hf + 1)
                        dve.tensor_tensor(th_view(halves[hf][1]), rep(ident, 4), th_view(psum[:, 4 + hf, :]), ALU.subtract)\
                           .then_inc(S("inv_done"), 1)
            head_dve(dve, "w_out")
            mod_dve(dve, done, 2, "norm2")
            dve.wait_ge(S("head_root"), 2)
            done(dve.reciprocal(o_r, o_r))
            diagonals(dve, o_diag, o_r, S("head_diag"))
            dve.wait_ge(S("gdn_of"), 1)
            dve.wait_ge(S("head_rows"), 2)
            done(dve.tensor_tensor(o_f, o_f, banks(0), ALU.mult))
            for h in range(HEADS):
                dve.scalar_tensor_tensor(act_f[:, CS5 + h, :], tok_view(o_f)[:, h, :], col("gdn_g"), zs[:, h, :], ALU.mult, ALU.mult)\
                   .then_inc(S("act_f"), 1)


        def router_pe(pe):
            pe.wait_ge(S("act_f"), 8 * 3)
            for t in range(NT):
                for k in range(KD):
                    last = pe.matmul(psum[:, 3, t * 36:(t + 1) * 36], act_f[:, k, t * P:(t + 1) * P], w_router[:, k, :],
                                     start=k == 0, stop=k == KD - 1)
            last.then_inc(S("router_raw"), 1)

        def gate_row(pe, i):
            pe.wait_ge(S("gate_diag"), i + 1)
            for t in range(NT):
                last = pe.matmul(gate_bank[:, t * P:(t + 1) * P], mat("ones"), diag[:, t, :], start=True, stop=True)
            last.then_inc(S("gate_row"), 1)

        def router_act(act):
            act.wait_ge(S("group_diff"), 1)
            act.activation(gexp, gexp, ACT.Exp).then_inc(S("group_exp"), 1)
            act.wait_ge(S("pair_diff"), 1)
            act.activation(pair_e, pair_e, ACT.Exp).then_inc(S("pair_exp"), 1)

        gexp = tiny(NT * N_GROUPS)
        geq = tiny(NT * N_GROUPS)
        gmax, gden, wmax, m1, m2, pair_e, w1, w2 = (tiny(NT) for _ in range(8))
        sel, eq8, oh1, oh2 = (tiny(NT * PER_GROUP) for _ in range(4))

        def router_dve(dve, done):
            def by(ap, n):
                return ap.rearrange("p (t n) -> p t n", n=n)

            def best(src, n, mx, onehot, order):
                done(dve.reduce_max(mx, by(src, n), AX))
                done(dve.tensor_tensor(by(eq8[:, 0:NT * n], n), by(src, n), bc(mx, n), ALU.is_equal))
                done(dve.tensor_tensor(by(eq8[:, 0:NT * n], n), by(eq8[:, 0:NT * n], n), rep(order, NT), ALU.mult))
                done(dve.reduce_max(wmax, by(eq8[:, 0:NT * n], n), AX))
                done(dve.tensor_tensor(by(onehot, n), by(eq8[:, 0:NT * n], n), bc(wmax, n), ALU.is_equal))

            dve.wait_ge(S("router_raw"), 1)
            done(dve.tensor_copy(lg, psum[:, 3, 0:72].rearrange("p (t n) -> p t n", t=NT)))
            done(dve.tensor_copy(by(gexp, 4), lg[:, :, 0:4]))
            best(gexp, N_GROUPS, gmax, geq, first[:, 4:8])
            dve.tensor_tensor(by(gexp, 4), by(gexp, 4), bc(gmax, 4), ALU.subtract).then_inc(S("group_diff"), 1)
            for t in range(NT):
                ex = lg[:, t, 4:36].rearrange("p (g e) -> p e g", g=N_GROUPS)
                done(dve.tensor_tensor(sel4[:, t, :, :], ex, rep(by(geq, 4)[:, t, :], PER_GROUP), ALU.mult))
            done(dve.reduce_sum(by(sel, 8), sel4, AX))
            best(sel, PER_GROUP, m1, oh1, first[:])
            done(dve.scalar_tensor_tensor(sel, oh1, -3.0e38, sel, ALU.mult, ALU.add))
            best(sel, PER_GROUP, m2, oh2, first[:])
            dve.tensor_tensor(pair_e, m2, m1, ALU.subtract).then_inc(S("pair_diff"), 1)
            dve.wait_ge(S("group_exp"), 1)
            done(dve.reduce_sum(gden, by(gexp, 4), AX))
            done(dve.reciprocal(gden, gden))
            dve.wait_ge(S("pair_exp"), 1)
            done(dve.tensor_scalar(w1, pair_e, 1.0, None, ALU.add))
            done(dve.reciprocal(w1, w1))
            done(dve.tensor_tensor(w1, w1, gden, ALU.mult))
            done(dve.tensor_tensor(w2, w1, pair_e, ALU.mult))
            done(dve.tensor_tensor(by(oh1, 8), by(oh1, 8), bc(w1, 8), ALU.mult))
            done(dve.tensor_tensor(by(oh2, 8), by(oh2, 8), bc(w2, 8), ALU.mult))
            done(dve.tensor_tensor(oh1, oh1, oh2, ALU.add))
            for t in range(NT):
                dst = comb[:, t, :].rearrange("p (g e) -> p g e", g=N_GROUPS)
                last = dve.tensor_tensor(dst, bc(by(geq, 4)[:, t, :], PER_GROUP), rep(by(oh1, 8)[:, t, :], N_GROUPS), ALU.mult)
            done(last)
            gate_diag(dve, comb[:, :, 0:1])

        def residual_dve(dve, done, s, used, part, final):
            gate = mod[:, part * D:(part + 1) * D].rearrange("p (b n) -> p b n", b=2)
            for t in range(NT):
                if t:
                    dve.wait_ge(slab_used[s], used)
                else:
                    dve.wait_ge(S("y_ready"), 4 if final else 2)
                done(dve.tensor_tensor(xn(t).rearrange("p (b n) -> p b n", b=2), acc[:, 2 * t:2 * t + 2, :], gate, ALU.mult))
                dve.tensor_tensor(x[:, t, :], x[:, t, :], xn(t), ALU.add).then_inc(S("moe_x" if final else "x_ready"), 1)

        def final_act(act):
            for t in range(NT):
                act.wait_ge(S("moe_x"), t + 1)
                if t:
                    act.wait_ge(S("final_sums"), t)
                act.activation(junk, x[:, t, :], ACT.Square, accum_out=f_sum[:, t:t + 1]).then_inc(S("final_sums"), 1)

        def final_pool(pool):
            for t in range(NT):
                pool.wait_ge(S("final_sums"), t + 1)
                rstd(pool, f_rstd[:, t:t + 1], f_sum[:, t:t + 1], 1.0 / D, EPS, S("final_rstd"))

        def final_dve(dve):
            dve.wait_ge(S("row_loaded0"), 16)
            for t in range(NT):
                dve.wait_ge(S("final_rstd"), t + 1)
                dve.scalar_tensor_tensor(x[:, t, :], x[:, t, :], f_rstd[:, t:t + 1], rows[:, 0, :], ALU.mult, ALU.mult)\
                   .then_inc(S("x_ready"), 1)
        ATT = [l for l in range(LAYERS) if KINDS[l] != 1]
        SC = T + P
        q_a = arena[:, 0:2048].rearrange("p (c t) -> p c t", t=T)
        k_a = arena[:, 2048:4096].rearrange("p (c t) -> p c t", t=T)
        v_a = arena[:, 4096:6144].rearrange("p (t n) -> p t n", t=NT)
        bias_a = [arena[:, 6144 + i * 4 * T:6144 + (i + 1) * 4 * T].rearrange("p (h n) -> p h n", h=4) for i in range(2)]
        prob_a = [arena[:, 9216 + i * 2 * SC:9216 + (i + 1) * 2 * SC].rearrange("p (h n) -> p h n", h=2) for i in range(2)]
        pt_a = arena[:, 12288:12288 + 2 * SC]
        mx_a = [tiny(4) for _ in range(2)]
        sum_a = [tiny(4) for _ in range(2)]
        TURNS = 8
        lam_p, lam_e, nlam, subg = tiny(2), tiny(2), tiny(1), tiny(1)
        o2, sub_diag = arena[:, 14336:16384], arena[:, 0:2048]
        sub_r = tiny(16)

        def same_before(l):
            return KINDS[:l].count(KINDS[l])

        def n_proj(l):
            return 8 if KINDS[l] == 1 else 12

        def order(l, j):
            return (j - 4) % n_proj(l)

        def proj_base(l):
            return ADA_FIRST + 10 + sum(n_proj(i) for i in range(l))

        def act_index(l, which):
            return 3 + 4 * l + which

        def f_index(l):
            return 3 + l

        def qkv_act(act, l, j0, j1):
            name = f"mix{l}"
            for j in range(j0, j1):
                if KINDS[l] == 2 and j == 5:
                    act.wait_ge(S("lam_sum"), 1)
                    act.activation(lam_e, psum[:, 7, 0:2], ACT.Exp).then_inc(S("lam_exp"), 1)
                cols_used(act, name, j)
                bank = psum[:, 4 + j % 2, :].rearrange("p (m t) -> p m t", m=2)
                if j < 4:
                    act.activation(v_a[:, :, j * 256:(j + 1) * 256], bank, ACT.Copy).then_inc(S("proj_evac"), 1)
                elif j < 8:
                    act.activation(q_a[:, 2 * j - 8:2 * j - 6, :], bank, ACT.Copy, scale=0.125).then_inc(S("proj_evac"), 1)
                else:
                    act.activation(k_a[:, 2 * j - 16:2 * j - 14, :], bank, ACT.Copy).then_inc(S("proj_evac"), 1)
                mix_next_hi(act, name, j, 12)

        def cols_dve(dve, l, done):
            name = f"mix{l}"
            if KINDS[l] == 2:
                lam = col("lam_c", 0, 4).rearrange("p (a b) -> p a b", b=2)
                dve.tensor_tensor(lam_p, lam[:, :, 0], lam[:, :, 1], ALU.mult).then_inc(S("lam_prod"), 1)
                done(dve.tensor_scalar(subg, col("subln"), 1.0 - LAMBDA_INIT, None, ALU.mult))
            for j in range(n_proj(l)):
                mix_next_lo(dve, name, j, n_proj(l))
                if KINDS[l] == 2 and j == 7:
                    dve.wait_ge(S("lam_exp"), 1)
                    done(dve.tensor_tensor(nlam, lam_e[:, 1:2], lam_e[:, 0:1], ALU.subtract))
                    done(dve.tensor_scalar(nlam, nlam, LAMBDA_INIT, None, ALU.subtract))

        def bias_pool(pool, l):
            n = ATT.index(l)
            pool.wait_ge(S("pre_rstd"), NT * (4 + 3 * l))
            for b in range(4):
                bt = 4 * n + b
                s = bt % 2
                if bt >= 2:
                    pool.wait_ge(S("scores"), 2 * (bt - 1))
                if KINDS[l] == 2:
                    pool.dma_start(bias_a[s], a["alibi"][:, 4 * b:4 * b + 4, :]).then_inc(S(f"bias_in{s}"), 16)
                else:
                    tab = a["rel_rows"]
                    base = tab.offset + ((l // 3) * 16 + 4 * b) * 512
                    pool.dma_start(bias_a[s], bass.AP(tensor=tab.tensor, offset=base, ap=[[1, P], [512, 4], [1, T]]))\
                        .then_inc(S(f"bias_in{s}"), 16)
                    pool.wait_ge(S(f"bias_in{s}"), 16 * (bt // 2 + 1))
                    pool.memset(bias_a[s][64:P, :, 192:256], -1e30).then_inc(S("bias_ready"), 1)
            if KINDS[l] == 0:
                pool.wait_ge(S("bias_ready"), 4 * same_before(l) + 4)

        def lam_pe(pe):
            pe.wait_ge(S("lam_prod"), 1)
            pe.matmul(psum[:, 7, 0:2], mat("ones"), lam_p, start=True, stop=True).then_inc(S("lam_sum"), 1)

        def att_pe(pe, l):
            n = ATT.index(l)
            turn = mat("ident") if KINDS[l] == 2 else mat("flip")

            def scores(g):
                gt = TURNS * n + g
                if g % 2 == 0:
                    b = 4 * n + g // 2
                    if KINDS[l] == 0:
                        pe.wait_ge(S("bias_ready"), 4 * same_before(l) + g // 2 + 1)
                    else:
                        pe.wait_ge(S(f"bias_in{b % 2}"), 16 * (b // 2 + 1))
                if gt >= 2:
                    pe.wait_ge(S("exp"), 4 * (gt - 1))
                for hh in range(2):
                    h = 2 * g + hh
                    rs, c, bank = slice((h % 2) * 64, (h % 2 + 1) * 64), h // 2, 2 * (g % 2) + hh
                    bias = bias_a[(4 * n + g // 2) % 2][:, 2 * (g % 2) + hh, :]
                    pe.matmul(psum[:, bank, 0:T], turn, bias, start=True, stop=False)
                    pe.matmul(psum[:, bank, 0:T], q_a[rs, c, P:T], k_a[rs, c, :], start=False, stop=True)
                    pe.matmul(psum[:, bank, T:SC], turn, bias[:, P:T], start=True, stop=False)
                    last = pe.matmul(psum[:, bank, T:SC], q_a[rs, c, 0:P], k_a[rs, c, 0:P], start=False, stop=True)
                last.then_inc(S("scores"), 1)

            def turned(g):
                gt = TURNS * n + g
                pe.wait_ge(S("prob"), 2 * gt + 2)
                pe.wait_ge(S("pt"), gt)
                for hh in range(2):
                    for i, at0 in enumerate((T, 0, P)):
                        e = 3 * hh + i
                        last = pe.transpose(psum[:, 4 + e // 4, (e % 4) * P:(e % 4 + 1) * P], prob_a[gt % 2][:, hh, at0:at0 + P], ident)
                last.then_inc(S("pt_raw"), 1)

            def out_of(g):
                pe.wait_ge(S("pt"), TURNS * n + g + 1)
                if g >= 2:
                    if KINDS[l] == 0:
                        pe.wait_ge(S("act_f"), 8 * f_index(l) + g - 1)
                    else:
                        pe.wait_ge(S("att_read"), TURNS * same_before(l) + g - 1)
                for hh in range(2):
                    p0, p1 = pt_a[:, hh * SC:hh * SC + T], pt_a[:, hh * SC + T:(hh + 1) * SC]
                    if KINDS[l] == 0:
                        h = 2 * g + hh
                        dst, vs = psum[hh * 64:(hh + 1) * 64, 6 + g % 2, 0:T], slice(h * 64, (h + 1) * 64)
                    else:
                        dst, vs = psum[:, 6 + g % 2, 0:T], slice(g * P, (g + 1) * P)
                    alone = KINDS[l] == 0
                    pe.matmul(dst, v_a[:, 0, vs], p0, start=alone or hh == 0, stop=False)
                    last = pe.matmul(dst[:, P:T], v_a[:, 1, vs], p1, start=False, stop=alone or hh == 1)
                last.then_inc(S("att_o"), 1)

            pe.wait_ge(S("proj_evac"), proj_base(l) + 9)
            scores(0)
            scores(1)
            mix_cols_pe(pe, l, 10, 12, "t")
            for g in range(TURNS):
                if g == 0:
                    pe.wait_ge(S("proj_evac"), proj_base(l) + 12)
                if g + 2 < TURNS:
                    scores(g + 2)
                if g:
                    out_of(g - 1)
                turned(g)
            out_of(TURNS - 1)
            if KINDS[l] == 2:
                pe.wait_ge(S("att_read"), TURNS * (same_before(l) + 1))
                pe.wait_ge(S("exp"), 4 * TURNS * (n + 1))
                column_sums(pe, psum[:, 0, 0:16], o2, S("head_sums"))
                rows_of(pe, 0, sub_diag, S("head_diag"), 4 + 2 * same_before(l), S("head_rows"))
                keep_clock(pe, 7, 12)

        def att_act(act, l):
            n = ATT.index(l)

            def exps(g):
                gt = TURNS * n + g
                act.wait_ge(S("nmax"), gt + 1)
                if gt >= 2:
                    act.wait_ge(S("pt_raw"), gt - 1)
                for i, ks in enumerate((slice(0, T), slice(T, SC))):
                    for hh in range(2):
                        e = 2 * i + hh
                        act.activation(prob_a[gt % 2][:, hh, ks], psum[:, 2 * (g % 2) + hh, ks], ACT.Exp, bias=mx_a[gt % 2][:, e:e + 1],
                                       accum_out=sum_a[gt % 2][:, e:e + 1]).then_inc(S("exp"), 1)

            def read_out(g):
                act.wait_ge(S("att_o"), TURNS * n + g + 1)
                o = psum[:, 6 + g % 2, 0:T]
                if KINDS[l] == 0:
                    act.activation(act_f[:, g, :], o, ACT.Copy).then_inc(S("act_f"), 1)
                else:
                    act.activation(act_f[:, g, :], o, ACT.Copy)
                    act.activation(o2[:, g * T:(g + 1) * T], o, ACT.Square).then_inc(S("att_read"), 1)

            qkv_act(act, l, 0, 11)
            exps(0)
            exps(1)
            qkv_act(act, l, 11, 12)
            for g in range(TURNS):
                if g in (0, 2, 4):
                    head_act(act, f"wo{l}", (0, 1, 3)[g // 2])
                act.wait_ge(S("pt_raw"), TURNS * n + g + 1)
                act.wait_ge(S("att_o"), TURNS * n + g)
                act.activation(pt_a, banks(4, 2)[:, 0:2 * SC], ACT.Copy).then_inc(S("pt"), 1)
                if g + 2 < TURNS:
                    exps(g + 2)
                if g:
                    read_out(g - 1)
            read_out(TURNS - 1)
            if KINDS[l] == 2:
                act.wait_ge(S("head_sums"), same_before(l) + 3)
                act.activation(sub_r, psum[:, 0, 0:16], ACT.Sqrt, bias=eps_col, scale=1.0 / P).then_inc(S("head_root"), 1)

        def att_dve(dve, l, done):
            n = ATT.index(l)
            def maxes(g):
                gt = TURNS * n + g
                mx, b0 = mx_a[gt % 2], 2 * (g % 2)
                dve.wait_ge(S("scores"), gt + 1)
                dve.reduce_max(mx[:, 0:2], psum[:, b0:b0 + 2, 0:T], AX)
                done(dve.reduce_max(mx[:, 2:4], psum[:, b0:b0 + 2, T:SC], AX))
                dve.tensor_scalar(mx, mx, -1.0, None, ALU.mult).then_inc(S("nmax"), 1)

            def normalise(g):
                gt = TURNS * n + g
                inv, pr = sum_a[gt % 2], prob_a[gt % 2]
                dve.wait_ge(S("exp"), 4 * gt + 4)
                done(dve.reciprocal(inv, inv))
                if KINDS[l] == 2:
                    odd = inv.rearrange("p (e m) -> p e m", m=2)[:, :, 1]
                    done(dve.tensor_scalar(odd, odd, nlam, None, ALU.mult))
                dve.tensor_tensor(pr[:, :, 0:T], pr[:, :, 0:T], bc(inv[:, 0:2], T), ALU.mult).then_inc(S("prob"), 1)
                dve.tensor_tensor(pr[:, :, T:SC], pr[:, :, T:SC], bc(inv[:, 2:4], P), ALU.mult).then_inc(S("prob"), 1)

            maxes(0)
            maxes(1)
            for g in range(TURNS):
                normalise(g)
                if g in (1, 3, 5):
                    head_dve(dve, f"wo{l}", (0, 1, 3)[g // 2])
                if g + 2 < TURNS:
                    maxes(g + 2)
            if KINDS[l] == 2:
                dve.wait_ge(S("head_root"), same_before(l) + 3)
                done(dve.reciprocal(sub_r, sub_r))
                diagonals(dve, sub_diag, sub_r, S("head_diag"))
                dve.wait_ge(S("head_rows"), same_before(l) + 3)
                for h in range(8):
                    dve.scalar_tensor_tensor(act_f[:, h, :], act_f[:, h, :], subg, psum[:, h // 2, (h % 2) * T:(h % 2 + 1) * T], ALU.mult, ALU.mult)\
                       .then_inc(S("act_f"), 1)

        GROUPS = 8
        u_b, v_b = tok_view(arena[:, 0:2048]), arena[:, 2048:4096].rearrange("p (t n) -> p t n", t=NT)
        ws_t, ws_in = th_view(blk(4)), th_view(blk(5))
        w_sum, bs_b, vc_sq = blk(6), blk(8), blk(9)
        v_part = tiny(NT * 4)
        v_mean, v_var, v_rstd = tiny(NT), tiny(NT), tiny(NT)

        def gmlp_loads(pool):
            pool.dma_start(ws_in, a["b_w_s"].rearrange("g t s -> t g s")).then_inc(S("ws_in"), 16)
            pool.dma_start(bs_b, a["b_b_s"].to_broadcast([P, D])).then_inc(S("b_rows"), 16)

        def gmlp_turn_pe(pe):
            pe.wait_ge(S("ws_in"), 16)
            for g in range(GROUPS):
                last = pe.transpose(banks(2)[:, g * P:(g + 1) * P], ws_in[:, g, :], ident)
            last.then_inc(S("ws_turned"), 1)

        def gmlp_sums_pe(pe):
            pe.wait_ge(S("ws_t"), 1)
            for i in range(2):
                last = pe.matmul(psum[:, i, :], mat("ones"), blk(4)[:, i * 512:(i + 1) * 512], start=True, stop=True)
            last.then_inc(S("w_sums"), 1)

        def gmlp_pe(pe):
            pe.wait_ge(S("w_part"), GROUPS)
            for t in range(NT):
                pe.wait_ge(S("v_normed"), t + 1)
                for g in range(GROUPS):
                    last = pe.matmul(psum[:, 2 * t + g // 4, (g % 4) * P:(g % 4 + 1) * P], v_b[:, t, g * P:(g + 1) * P], ws_t[:, g, :],
                                     start=True, stop=True)
                    if g % 4 == 3:
                        last.then_inc(S("spatial"), 1)

        def gmlp_act(act, l):
            name = f"mix{l}"
            for j in range(8):
                cols_used(act, name, j)
                bank = psum[:, 4 + j % 2, :].rearrange("p (m t) -> p m t", m=2)
                if j < 4:
                    act.activation(v_b[:, 0, j * 256:(j + 1) * 256], bank[:, 0, :], ACT.Gelu, accum_out=v_part[:, j:j + 1])
                    act.activation(v_b[:, 1, j * 256:(j + 1) * 256], bank[:, 1, :], ACT.Gelu, accum_out=v_part[:, 4 + j:5 + j])\
                       .then_inc(S("proj_evac"), 1)
                else:
                    act.activation(u_b[:, 2 * j - 8:2 * j - 6, :], bank, ACT.Gelu).then_inc(S("proj_evac"), 1)
                mix_next_hi(act, name, j, 8)
                if j == 3:
                    for t in range(NT):
                        act.wait_ge(S("v_mean"), 1)
                        if t:
                            act.wait_ge(S("v_sq"), t)
                        act.activation(vc_sq, v_b[:, t, :], ACT.Square, bias=v_mean[:, t:t + 1], accum_out=v_var[:, t:t + 1])\
                           .then_inc(S("v_sq"), 1)
                if j in (5, 6):
                    head_act(act, f"wo{l}", (3, 0)[j - 5])

        def gmlp_pool(pool):
            pool.wait_ge(S("v_sq"), NT)
            rstd(pool, v_rstd, v_var, 1.0 / D, EPS, S("v_rstd"))

        def gmlp_dve(dve, l, done):
            name = f"mix{l}"
            for j in range(n_proj(l)):
                if j == 4:
                    dve.wait_ge(S("v_rstd"), 1)
                    for t in range(NT):
                        dve.tensor_scalar(v_b[:, t, :], v_b[:, t, :], v_mean[:, t:t + 1], v_rstd[:, t:t + 1], ALU.add, ALU.mult)\
                           .then_inc(S("v_normed"), 1)
                mix_next_lo(dve, name, j, n_proj(l))
                if j == 0:
                    dve.wait_ge(S("ws_turned"), 1)
                    dve.tensor_tensor(ws_t, th_view(banks(2)), rep(mat("upto"), GROUPS), ALU.mult).then_inc(S("ws_t"), 1)
                if j == 3:
                    dve.wait_ge(S("w_sums"), 1)
                    dve.wait_ge(S("b_rows"), 16)
                    for g in range(GROUPS):
                        gs = slice(g * P, (g + 1) * P)
                        dve.scalar_tensor_tensor(w_sum[:, gs], banks(0)[:, gs], col("ln_b", g), bs_b[:, gs], ALU.mult, ALU.add)\
                           .then_inc(S("w_part"), 1)
                    dve.wait_ge(S("proj_evac"), proj_base(l) + 4)
                    done(dve.reduce_sum(v_mean, v_part.rearrange("p (t i) -> p t i", t=NT), AX))
                    dve.tensor_scalar(v_mean, v_mean, -1.0 / D, None, ALU.mult).then_inc(S("v_mean"), 1)
            head_dve(dve, f"wo{l}", 3)
            dve.wait_ge(S("w_part"), GROUPS)
            dve.wait_ge(S("spatial"), 2 * NT)
            for g in range(GROUPS):
                sv = psum[:, 0:4, (g % 4) * P:(g % 4 + 1) * P].rearrange("p (t b) n -> p t b n", t=NT)[:, :, g // 4, :]
                y = act_f[:, g, :].rearrange("p (t n) -> p t n", t=NT)
                last = dve.scalar_tensor_tensor(y, sv, col("ln_g", g), rep(w_sum[:, g * P:(g + 1) * P], NT), ALU.mult, ALU.add)
            done(last)
            for i in range(4):
                if i == 3:
                    head_dve(dve, f"wo{l}", 0)
                dve.wait_ge(S("proj_evac"), proj_base(l) + 5 + i)
                pair = slice(2 * i, 2 * i + 2)
                dve.tensor_tensor(act_f[:, pair, :], act_f[:, pair, :], u_b[:, pair, :], ALU.mult).then_inc(S("act_f"), 2)

        def ff_hb(l, which):
            return N_EXPERTS + (2 * l + which) * FF_STEPS

        def row_load(pool, r):
            if r == 2:
                pool.wait_ge(S("x_ready"), 2 * NT)
            elif r > 2:
                pool.wait_ge(S("x_half"), 2 * NT * (r - 2))
            pool.dma_start(rows[:, r % 2, :], a["rows"][r:r + 1, :].to_broadcast([P, D])).then_inc(S(f"row_loaded{r % 2}"), 16)

        @block.sync
        def _(sp):
            for j in range(ADA_FIRST):
                if j == 1:
                    sp.dma_start(mats[:].rearrange("p m n -> p (m n)"), a["mats"]).then_inc(S("mats_loaded"), 16)
                elif j == ADA_FIRST - 1:
                    sp.dma_start(x[:], a["x"].rearrange("(t p) n -> p t n", p=P)).then_inc(S("x_loaded"), 16)
                ada_load(sp, j)
            sp.wait_ge(S("ada_used"), 2)
            cols_load(sp, "w_in", lambda j: col_slab(a["w_in"], 256 * j), *range(10))
            sp.wait_ge(S("ada_used"), ADA_FIRST)
            load(sp, GD, PLAN.base["w_glu"][GD], a["w_glu"].rearrange("(k p) n -> p k n", p=P))
            w_out = lambda j: col_slab(a["w_out"], 256 * j)
            for j in range(ADA_FIRST, N_ADA):
                ada_load(sp, j)
            sp.wait_ge(S("ada_used"), N_ADA)
            cols_load(sp, "w_out", w_out, *range(4))

            def expert(name):
                def src(i):
                    w = a[name][bass.ds(i, 1), :, :] if not isinstance(i, int) else a[name][i:i + 1, :, :]
                    return w.rearrange("o (k p) n -> p (o k) n", p=P)
                return src

            def ff_src(w, l, c0):
                def src(i):
                    return w[l, :, bass.ds(i * HID + c0, HID)].rearrange("(k p) n -> p k n", p=P) if not isinstance(i, int) \
                        else w[l, :, i * HID + c0:(i + 1) * HID + c0].rearrange("(k p) n -> p k n", p=P)
                return src

            def ff_row(w, l):
                def src(i):
                    r = w[l, bass.ds(i * HID, HID), :] if not isinstance(i, int) else w[l, i * HID:(i + 1) * HID, :]
                    return r.rearrange("(j p) n -> p j n", p=P)
                return src

            def layer_ff(l, half_ff):
                wi, wo = a[f"{half_ff}_w_in"], a[f"{half_ff}_w_out"]
                return ff_src(wi, l, 0), ff_src(wi, l, D_FF), ff_row(wo, l)

            def mixer_src(l):
                w = a["b_w_in" if KINDS[l] == 1 else f"{'abc'[KINDS[l]]}_w_qkv"]
                return lambda j: col_slab(w[l // 3], 256 * order(l, j))

            experts = expert("w_gate"), expert("w_up"), expert("w_down")
            cols_load(sp, "moe", lambda j: experts[j](0), 0, 1)
            ff_load(sp, "moe", N_EXPERTS, *experts, lambda: cols_load(sp, "ff0a", lambda j: layer_ff(0, "ff1")[j](0), 0, 1))
            for l in range(LAYERS):
                ff_load(sp, f"ff{l}a", FF_STEPS, *layer_ff(l, "ff1"), lambda: cols_load(sp, f"mix{l}", mixer_src(l), 0, 1))
                cols_load(sp, f"mix{l}", mixer_src(l), *range(2, n_proj(l)))
                cols_load(sp, f"wo{l}", lambda j: col_slab(a[f"{'abc'[KINDS[l]]}_w_o"][l // 3], 256 * j), 3, 0, 1, 2)
                cols_load(sp, f"ff{l}b", lambda j: layer_ff(l, "ff2")[j](0), 0, 1)
                ff_load(sp, f"ff{l}b", FF_STEPS, *layer_ff(l, "ff2"),
                        lambda: l < LAYERS - 1 and cols_load(sp, f"ff{l + 1}a", lambda j: layer_ff(l + 1, "ff1")[j](0), 0, 1))
            for t in range(NT):
                sp.wait_ge(S("x_half"), 2 * NT * (3 * LAYERS - 1) + 2 * t + 2)
                sp.dma_start(out[t * P:(t + 1) * P, :], x[:, t, :]).then_inc(S("stored"), 16)
            sp.wait_ge(S("stored"), 32)

        @block.gpsimd
        def _(pool):
            done = steps(pool, "pool_order")
            pool.dma_start(wsmall[:, :, 0:36], a["w_router"].rearrange("(k p) n -> p k n", p=P)).then_inc(S("narrow_loaded"), 16)
            pool.dma_start(wsmall[:, :, 36:44], a["w_in"][:, 2560:2568].rearrange("(k p) n -> p k n", p=P)).then_inc(S("narrow_loaded"), 16)
            pool.dma_start(first[:], a["first"]).then_inc(S("first_loaded"), 16)
            pool.wait_ge(S("half"), 1)
            s5_tables_pool(pool, done)
            pre_pool(pool, 1)
            row_load(pool, 0)
            row_load(pool, 1)
            pool.wait_ge(S("router_raw"), 1)
            gain_load(pool, 2, "act_lo", act_before(3))
            final_pool(pool)
            pre_pool(pool, 2)
            for l in range(LAYERS):
                if KINDS[l] == 1:
                    gmlp_loads(pool)
                gain_load(pool, 3 + 3 * l, "normed", 2 * NT * (3 + 3 * l))
                turn_pool(pool, 3 * l, 0.5)
                row_load(pool, 3 * l + 2)
                if KINDS[l] == 1:
                    gmlp_pool(pool)
                else:
                    bias_pool(pool, l)
                gain_load(pool, 4 + 3 * l, "act_lo", act_before(act_index(l, 3)))
                post_pool(pool, 3 * l + 1, 1.0)
                pre_pool(pool, 4 + 3 * l)
                row_load(pool, 3 * l + 3)
                if l < LAYERS - 1:
                    gain_load(pool, 5 + 3 * l, "normed", 2 * NT * (5 + 3 * l))
                post_pool(pool, 3 * l + 2, 0.5)
                if l < LAYERS - 1:
                    pre_pool(pool, 5 + 3 * l)
                    row_load(pool, 3 * l + 4)

        @block.scalar
        def _(act):
            act.dma_start(cols[:], a["cols"]).then_inc(S("cols_loaded"), 16)
            s5_param_act(act)
            pre_act(act, 0)
            for part in (2, 5):
                gate = slice(part * D, (part + 1) * D)
                act.dma_start(mod[:, gate], a["b_ada"][:, gate].to_broadcast([P, D])).then_inc(S("bias_loaded"), 16)
            act.wait_ge(S("pre_sums"), 2 * NT)
            act.dma_start(junk, a["s5_b"]).then_inc(S("s5_b_loaded"), 16)
            head_act(act, "w_in", 0)
            act.wait_ge(S("mod_cols"), 1)
            pre_mod_act(act, 0, 0, 0, lambda k: modc[:, 1, k:k + 1], lambda k: modc[:, 0, k:k + 1])
            head_act(act, "w_in", 1)
            w_in_act(act)
            s5_act(act)
            gdn_act(act)
            split_act(act, 1, 1)
            wo_act(act, "w_out", "moe")
            pre_act(act, 1)
            act.wait_ge(S("mod_cols"), 2)
            pre_mod_act(act, 1, 2, 2, lambda k: modc[:, 3, k:k + 1], lambda k: modc[:, 2, k:k + 1])
            head_act(act, "moe", 1)
            router_act(act)
            act.activation(warm, warm, ACT.Silu)
            ff_act(act, "moe", N_EXPERTS, 0, "ff0a", gate_bank)
            final_act(act)
            for l in range(LAYERS):
                pre_act(act, 2 + 3 * l)
                pre_hi_act(act, 2 + 3 * l, act_index(l, 0))
                ff_act(act, f"ff{l}a", FF_STEPS, ff_hb(l, 0), f"mix{l}")
                turn_act(act, 3 * l, 0.5, act_index(l, 1))
                if KINDS[l] == 1:
                    gmlp_act(act, l)
                else:
                    att_act(act, l)
                split_act(act, act_index(l, 2), f_index(l))
                if KINDS[l] == 1:
                    head_act(act, f"wo{l}", 1)
                wo_act(act, f"wo{l}", f"ff{l}b")
                post_act(act, 3 * l + 1, 1.0)
                pre_act(act, 4 + 3 * l)
                pre_hi_act(act, 4 + 3 * l, act_index(l, 3))
                ff_act(act, f"ff{l}b", FF_STEPS, ff_hb(l, 1), f"ff{l + 1}a" if l < LAYERS - 1 else None)
                post_act(act, 3 * l + 2, 0.5)

        @block.vector
        def _(dve):
            done = steps(dve, "dve_order")
            dve.wait_ge(S("cols_loaded"), 16)
            s5_param_dve(dve, done)
            dve.wait_ge(S("mats_loaded"), 16)
            for j in range(ADA_FIRST):
                ada_dve(dve, done, j)
            pre_rows_dve(dve, 0)
            mod_dve(dve, done, 0, "norm1")
            head_dve(dve, "w_in", 0)
            pre_dve(dve, 0, 0)
            head_dve(dve, "w_in", 1)
            w_in_dve(dve, done)
            s5_dve(dve, done)
            gdn_dve(dve, done)
            split_dve(dve, 1)
            wo_dve(dve, "w_out", "moe")
            residual_dve(dve, done, 1, PLAN.base["w_out"][1] + 2, 2, False)
            pre_rows_dve(dve, 1)
            pre_dve(dve, 1, 2)
            dve.wait_ge(S("first_loaded"), 16)
            head_dve(dve, "moe", 1)
            router_dve(dve, done)
            ff_dve(dve, "moe", N_EXPERTS, 0, "ff0a", gate_bank)
            residual_dve(dve, done, GD, PLAN.base["moe"][GD] + N_EXPERTS, 5, True)
            final_dve(dve)
            for l in range(LAYERS):
                pre_rows_dve(dve, 2 + 3 * l)
                pre_dve(dve, 2 + 3 * l, act_index(l, 0))
                ff_dve(dve, f"ff{l}a", FF_STEPS, ff_hb(l, 0), f"mix{l}")
                turn_dve(dve, 3 * l, 3 * l + 1, act_index(l, 1))
                if KINDS[l] == 1:
                    gmlp_dve(dve, l, done)
                else:
                    cols_dve(dve, l, done)
                    att_dve(dve, l, done)
                split_dve(dve, act_index(l, 2))
                if KINDS[l] == 1:
                    head_dve(dve, f"wo{l}", 1)
                wo_dve(dve, f"wo{l}", f"ff{l}b")
                post_dve(dve, 3 * l + 1, 3 * l + 2)
                pre_rows_dve(dve, 4 + 3 * l)
                pre_dve(dve, 4 + 3 * l, act_index(l, 3))
                head_dve(dve, f"ff{l}b", 1)
                ff_dve(dve, f"ff{l}b", FF_STEPS, ff_hb(l, 1), f"ff{l + 1}a" if l < LAYERS - 1 else None)
                post_dve(dve, 3 * l + 2, 3 * l + 3)

        @block.tensor
        def _(pe):
            pe.wait_ge(S("c_act"), 1)
            for j in range(ADA_FIRST):
                ada_pe(pe, j)
            pe.wait_ge(S("mats_loaded"), 16)
            pre_pe(pe, 0)
            w_in_pe(pe)
            s5_pe(pe)
            gdn_pe(pe)
            wo_pe(pe, "w_out", 1)
            pre_pe(pe, 1)
            router_pe(pe)
            ff_pe(pe, "moe", N_EXPERTS, 0, 2, gate_row)
            for l in range(LAYERS):
                pre_pe(pe, 2 + 3 * l)
                ff_pe(pe, f"ff{l}a", FF_STEPS, ff_hb(l, 0), act_index(l, 0))
                first_cols_pe(pe, f"mix{l}", proj_base(l), 3 + 3 * l, act_index(l, 1))
                if KINDS[l] == 1:
                    gmlp_turn_pe(pe)
                mix_cols_pe(pe, l, 2, 4, "n")
                if KINDS[l] == 1:
                    gmlp_sums_pe(pe)
                    mix_cols_pe(pe, l, 4, 6, "t")
                    gmlp_pe(pe)
                    mix_cols_pe(pe, l, 6, 8, "t")
                else:
                    if KINDS[l] == 2:
                        lam_pe(pe)
                    mix_cols_pe(pe, l, 4, 10, "t")
                    att_pe(pe, l)
                wo_pe(pe, f"wo{l}", act_index(l, 2))
                pre_pe(pe, 4 + 3 * l)
                ff_pe(pe, f"ff{l}b", FF_STEPS, ff_hb(l, 1), act_index(l, 3))


def kernel(**inputs):
    import concourse.bacc as bacc
    from concourse.bass_utils import run_bass_kernel_spmd

    v = {k: np.asarray(a) for k, a in inputs.items()}

    def chunks(row):
        return row.reshape(-1, P).T

    mats, alibi, first = constants()

    def states(m):
        return m.reshape(S5_TILES, P).T

    def inputs_of_state(m):
        z = np.zeros((CS5, 4, 2, 16, 2, 64), m.dtype)
        b = m.reshape(CS5, 4, 2, 64, 16)
        for g in range(2):
            z[:, :, g, :, g, :] = b[:, :, g].transpose(0, 1, 3, 2)
        return z.reshape(CS5, P, P).transpose(1, 0, 2).reshape(P, -1)

    def outputs_of_state(m):
        z = np.zeros((2, 64, S5_TILES, 2, 16), m.dtype)
        b = m.reshape(S5_TILES, 2, 16, 64)
        for g in range(2):
            z[g, :, :, g, :] = b[:, g].transpose(2, 0, 1)
        return z.reshape(P, -1)

    def over_all(row):
        return np.broadcast_to(row.reshape(1, -1), (P, row.size))

    lam = v["c_lambda_2"][0]
    parts = {
        "lam_re": states(v["lam_re"][0]), "lam_im": states(v["lam_im"][0]),
        "log_step": states(np.repeat(v["log_step"][0][:, None], 64, 1)),
        "s5_d": chunks(v["s5_d"][0]), "b_glu": chunks(v["b_glu"][0]),
        "conv_w": v["conv_w"][0].reshape(CONV, 12, P).transpose(2, 1, 0).reshape(P, -1),
        "norm1": chunks(v["norm1_g"][0]), "norm2": chunks(v["norm2_g"][0]),
        "gdn_g": chunks(v["gdn_norm_g"][0]), "subln": chunks(v["c_subln_g_2"][0]), "c": chunks(v["c"][0]),
        "dt_bias": over_all(np.repeat(v["dt_bias"][0], NT)), "a_log": over_all(np.repeat(v["a_log"][0], NT)),
        "b_ada": v["b_ada"].reshape(6, KD, P)[[0, 1, 3, 4]].transpose(2, 0, 1).reshape(P, -1),
        "ln_g": chunks(v["b_ln_g_2"][0]), "ln_b": chunks(v["b_ln_b_2"][0]),
        "lam_c": np.concatenate([lam.T, np.zeros((P - lam.shape[1], 4), lam.dtype)], 0),
        "c_re": outputs_of_state(v["s5_c_re"][0]), "c_im": outputs_of_state(v["s5_c_im"][0]),
    }
    cols = np.zeros((P, NCOLS), np.float32)
    for name, part in parts.items():
        cols[:, COLS[name][0]:COLS[name][1]] = part
    rel = v["a_rel_bias_2"][:, :, np.clip(255 - np.arange(512), -128, 128) + 128]
    gains = v["norm_g_2"][:, [0, 2, 4], :].reshape(-1, D)
    rows = np.concatenate([v["normf_g"][None], v["norm_g_2"][:, [1, 3, 5], :].reshape(-1, D)], 0)
    arrays = {
        "x": v["x"][0], "w_ada": v["w_ada"][0], "b_ada": v["b_ada"], "w_in": v["w_in"][0], "w_glu": v["w_glu"][0],
        "w_out": v["w_out"][0], "w_router": np.concatenate([v["w_router_grp"][0], v["w_router_exp"][0]], 1),
        "w_gate": v["w_gate"][0], "w_up": v["w_up"][0], "w_down": v["w_down"][0],
        "ff1_w_in": v["ff1_w_in_2"], "ff1_w_out": v["ff1_w_out_2"], "ff2_w_in": v["ff2_w_in_2"], "ff2_w_out": v["ff2_w_out_2"],
        "a_w_qkv": v["a_w_qkv_2"], "a_w_o": v["a_w_o_2"], "b_w_in": v["b_w_in_2"], "b_w_o": v["b_w_o_2"],
        "c_w_qkv": v["c_w_qkv_2"], "c_w_o": v["c_w_o_2"], "b_w_s": v["b_w_s_2"][0],
        "b_b_s": v["b_b_s_2"].reshape(1, -1), "cols": cols, "rows": rows, "gains": gains, "rel_rows": rel.reshape(-1, 512), "mats": mats,
        "alibi": alibi, "first": first,
        "s5_b": np.concatenate([inputs_of_state(v["s5_b_re"][0]), inputs_of_state(v["s5_b_im"][0])], 1),
    }
    nc = bacc.Bacc("TRN2", target_bir_lowering=False, num_devices=1)
    args, feeds = {}, {}
    for name, arr in arrays.items():
        arr = np.ascontiguousarray(arr)
        feeds[f"in_{name}"] = arr
        args[name] = nc.dram_tensor(f"in_{name}", arr.shape, mybir.dt.from_np(arr.dtype), kind="ExternalInput").ap()
    result = nc.dram_tensor("result", (T, D), F32, kind="ExternalOutput").ap()
    build(nc, args, result)
    r = run_bass_kernel_spmd(nc, [feeds], core_ids=[0])
    return r.results[0]["result"].reshape(1, T, D)
```
